# Optimizing a Trainium2 kernel written in Bass

```python
import jax, jax.numpy as jnp
from jax import lax
import numpy as np

D_MODEL = 1024
BATCH = 1
SEQ = 2048
DEPTH = 1
DEC_BATCH = 8
DEC_SEQ = 8
PAST_LEN = 16384
PAGE_SIZE = 128

CONV_WIDTH = D_MODEL // 2
CONV_KERNEL = 31
HEAD_DIM = 64
RWKV_WIDTH = D_MODEL
RWKV_HEADS = RWKV_WIDTH // HEAD_DIM
DECAY_RANK = 64
ICLR_RANK = 64
GATE_RANK = 128
GLU_COLS = 2 * CONV_WIDTH
RW_START = GLU_COLS
RW_COLS = 3 * RWKV_WIDTH + DECAY_RANK + ICLR_RANK + GATE_RANK
GATE_START = RW_START + RW_COLS
IN_COLS = GATE_START + 2 * D_MODEL
N_GROUPS = 4
EXPERTS_PER_GROUP = 8
N_EXPERTS = N_GROUPS * EXPERTS_PER_GROUP
TOP_K_IN_GROUP = 2
D_EXPERT = 256
MOE_BLOCK = 128
NORM_EPS = 1e-6
LN_EPS = 1e-5
GN_EPS = 64e-5

kernel_name = "hybrid_conformer_rwkv7_hiermoe_step"

def rmsnorm(x, g):
    xf = x.astype(jnp.float32)
    return xf * lax.rsqrt(jnp.mean(xf * xf, axis=-1, keepdims=True) + NORM_EPS) * g.astype(jnp.float32)

def conformer_conv(glu_in, conv_buf, w_dw, b_dw, ln_g, ln_b, w_out, b_out):
    a, gt = jnp.split(glu_in, 2, axis=-1)
    glu = a * jax.nn.sigmoid(gt)
    full = jnp.concatenate([conv_buf.astype(jnp.float32), glu], axis=1)
    y = lax.conv_general_dilated(full, w_dw.astype(jnp.float32)[:, None, :], window_strides=(1,),
                                 padding='VALID', dimension_numbers=('NWC', 'WIO', 'NWC'),
                                 feature_group_count=CONV_WIDTH) + b_dw
    m = jnp.mean(y, axis=-1, keepdims=True)
    var = jnp.mean(jnp.square(y - m), axis=-1, keepdims=True)
    y = (y - m) * lax.rsqrt(var + LN_EPS) * ln_g + ln_b
    y = jax.nn.silu(y)
    return y @ w_out + b_out, full[:, -(CONV_KERNEL - 1):]

def wkv_scan(S0, r, decay, kk, b, v, k):
    def step(S, xs):
        r_t, w_t, kk_t, b_t, v_t, k_t = xs
        sa = jnp.einsum('bhvk,bhk->bhv', S, kk_t)
        S = S * w_t[:, :, None, :] - sa[..., None] * b_t[:, :, None, :] + v_t[..., None] * k_t[:, :, None, :]
        return S, jnp.einsum('bhvk,bhk->bhv', S, r_t)
    xs = tuple(jnp.moveaxis(a, 1, 0) for a in (r, decay, kk, b, v, k))
    S, ys = lax.scan(step, S0, xs)
    return jnp.moveaxis(ys, 0, 1), S

def rwkv7_mix(p_rw, prev_rw, S0, mu, w0, w2, a0, a2, g2, k_k, k_a, r_k, gn_g, gn_b, w_out):
    B, T, _ = p_rw.shape
    p_prev = jnp.concatenate([prev_rw[:, None, :], p_rw[:, :-1]], axis=1)
    xm = p_rw + mu * (p_prev - p_rw)
    o1, o2, o3 = RWKV_WIDTH, 2 * RWKV_WIDTH, 3 * RWKV_WIDTH
    o4, o5 = o3 + DECAY_RANK, o3 + DECAY_RANK + ICLR_RANK
    r, k, v = xm[..., :o1], xm[..., o1:o2], xm[..., o2:o3]
    wd, ad, gd = xm[..., o3:o4], xm[..., o4:o5], xm[..., o5:]
    w = -jax.nn.softplus(-(w0 + jnp.tanh(wd) @ w2)) - 0.5
    decay = jnp.exp(-jnp.exp(w))
    a = jax.nn.sigmoid(a0 + ad @ a2)
    g = jax.nn.sigmoid(gd) @ g2
    hs = lambda t: t.reshape(B, T, RWKV_HEADS, HEAD_DIM)
    kk = hs(k * k_k)
    kk = kk / jnp.maximum(jnp.linalg.norm(kk, axis=-1, keepdims=True), 1e-12)
    k = k * (1.0 + (a - 1.0) * k_a)
    r_h, k_h, v_h, a_h = hs(r), hs(k), hs(v), hs(a)
    y, S = wkv_scan(S0.astype(jnp.float32), r_h, hs(decay), kk, kk * a_h, v_h, k_h)
    m = jnp.mean(y, axis=-1, keepdims=True)
    var = jnp.mean(jnp.square(y - m), axis=-1, keepdims=True)
    y = ((y - m) * lax.rsqrt(var + GN_EPS)).reshape(B, T, RWKV_WIDTH) * gn_g + gn_b
    bonus = jnp.sum(r_h * k_h * r_k, axis=-1, keepdims=True) * v_h
    y = (y + bonus.reshape(B, T, RWKV_WIDTH)) * g
    return y @ w_out, S

def hier_moe(v, rg_w, rg_b, re_w, re_b, w_gate, w_up, w_down):
    T = v.shape[0]
    lg = v @ rg_w + rg_b
    pg = jax.nn.softmax(lg, axis=-1)
    gsel = jnp.argmax(lg, axis=-1)
    le = (v @ re_w + re_b).reshape(T, N_GROUPS, EXPERTS_PER_GROUP)
    le_sel = jnp.take_along_axis(le, gsel[:, None, None], axis=1)[:, 0]
    top_v, top_i = lax.top_k(le_sel, TOP_K_IN_GROUP)
    gate = jnp.take_along_axis(pg, gsel[:, None], axis=1) * jax.nn.softmax(top_v, axis=-1)
    eidx = gsel[:, None] * EXPERTS_PER_GROUP + top_i
    A = T * TOP_K_IN_GROUP
    NB = -(-A // MOE_BLOCK) + N_EXPERTS
    P = NB * MOE_BLOCK
    e_flat = eidx.reshape(A).astype(jnp.int32)
    tok_flat = jnp.repeat(jnp.arange(T, dtype=jnp.int32), TOP_K_IN_GROUP)
    order = jnp.argsort(e_flat)
    e_sorted, tok_sorted, gate_sorted = e_flat[order], tok_flat[order], gate.reshape(A)[order]
    counts = jnp.zeros((N_EXPERTS,), jnp.int32).at[e_flat].add(1)
    padded = ((counts + MOE_BLOCK - 1) // MOE_BLOCK) * MOE_BLOCK
    ends_padded = jnp.cumsum(padded)
    starts_padded = ends_padded - padded
    starts = jnp.cumsum(counts) - counts
    dest = starts_padded[e_sorted] + (jnp.arange(A, dtype=jnp.int32) - starts[e_sorted])
    row_tok = jnp.full((P,), T, jnp.int32).at[dest].set(tok_sorted)
    row_gate = jnp.zeros((P,), jnp.float32).at[dest].set(gate_sorted)
    block_expert = jnp.clip(jnp.searchsorted(ends_padded, jnp.arange(NB, dtype=jnp.int32) * MOE_BLOCK,
                                             side='right'), 0, N_EXPERTS - 1)
    v_pad = jnp.concatenate([v, jnp.zeros((1, v.shape[1]), v.dtype)], axis=0)
    xb = v_pad[row_tok].reshape(NB, MOE_BLOCK, v.shape[1])

    def expert_block(args):
        xblk, e = args
        h = jax.nn.silu(xblk @ w_gate[e].astype(jnp.float32)) * (xblk @ w_up[e].astype(jnp.float32))
        return h @ w_down[e].astype(jnp.float32)

    yb = lax.map(expert_block, (xb, block_expert)).reshape(P, v.shape[1])
    out = jnp.zeros((T + 1, v.shape[1]), jnp.float32).at[row_tok].add(yb * row_gate[:, None])
    return out[:T]

def layer(x, conv_buf, shift_row, S0, norm1_g, w_in, conv_dw_w, conv_dw_b, conv_ln_g, conv_ln_b,
          conv_out_w, conv_out_b, rwkv_mu, rwkv_w0, rwkv_w2, rwkv_a0, rwkv_a2, rwkv_g2, rwkv_k_k,
          rwkv_k_a, rwkv_r_k, rwkv_gn_g, rwkv_gn_b, rwkv_out_w, w_o, norm2_g, router_group_w,
          router_group_b, router_expert_w, router_expert_b, expert_w_gate, expert_w_up, expert_w_down):
    f32 = lambda t: t.astype(jnp.float32)
    x = f32(x)
    B, T, D = x.shape
    u = rmsnorm(x, norm1_g)
    w_in = f32(w_in)
    p = u @ w_in
    prev_rw = f32(shift_row) @ w_in[:, RW_START:GATE_START]
    yA, new_buf = conformer_conv(p[..., :GLU_COLS], conv_buf, conv_dw_w, f32(conv_dw_b), f32(conv_ln_g),
                                 f32(conv_ln_b), f32(conv_out_w), f32(conv_out_b))
    yB, S = rwkv7_mix(p[..., RW_START:GATE_START], prev_rw, S0, f32(rwkv_mu), f32(rwkv_w0), f32(rwkv_w2),
                      f32(rwkv_a0), f32(rwkv_a2), f32(rwkv_g2), f32(rwkv_k_k), f32(rwkv_k_a), f32(rwkv_r_k),
                      f32(rwkv_gn_g), f32(rwkv_gn_b), f32(rwkv_out_w))
    gates = jax.nn.sigmoid(p[..., GATE_START:])
    x = x + (gates[..., :D] * yA + gates[..., D:] * yB) @ f32(w_o)
    hmoe = rmsnorm(x, norm2_g).reshape(B * T, D)
    x = x + hier_moe(hmoe, f32(router_group_w), f32(router_group_b), f32(router_expert_w),
                     f32(router_expert_b), expert_w_gate, expert_w_up, expert_w_down).reshape(B, T, D)
    return x, new_buf, u[:, -1], S

def setup_inputs(seed: int = 0) -> dict:
    key = jax.random.key(seed)
    ks = jax.random.split(key, 40)
    nrm = lambda i, shape, s: jax.random.normal(ks[i], shape, jnp.float32) * s
    L = DEPTH
    return {
        "x_prompt": nrm(0, (BATCH, SEQ, D_MODEL), 1.0),
        "x_sample": nrm(1, (DEC_BATCH, DEC_SEQ, D_MODEL), 1.0),
        "state_conv": nrm(2, (L, DEC_BATCH, CONV_KERNEL - 1, CONV_WIDTH), 0.5),
        "state_shift": nrm(3, (L, DEC_BATCH, D_MODEL), 1.0),
        "state_wkv": nrm(4, (L, DEC_BATCH, RWKV_HEADS, HEAD_DIM, HEAD_DIM), 0.1),
        "norm1_g": 1.0 + nrm(5, (L, D_MODEL), 0.05),
        "w_in": nrm(6, (L, D_MODEL, IN_COLS), D_MODEL ** -0.5),
        "conv_dw_w": nrm(7, (L, CONV_KERNEL, CONV_WIDTH), CONV_KERNEL ** -0.5),
        "conv_dw_b": nrm(8, (L, CONV_WIDTH), 0.01),
        "conv_ln_g": 1.0 + nrm(9, (L, CONV_WIDTH), 0.05),
        "conv_ln_b": nrm(10, (L, CONV_WIDTH), 0.01),
        "conv_out_w": nrm(11, (L, CONV_WIDTH, D_MODEL), CONV_WIDTH ** -0.5),
        "conv_out_b": nrm(12, (L, D_MODEL), 0.01),
        "rwkv_mu": jax.random.uniform(ks[13], (L, RW_COLS), jnp.float32),
        "rwkv_w0": nrm(14, (L, RWKV_WIDTH), 0.5),
        "rwkv_w2": nrm(15, (L, DECAY_RANK, RWKV_WIDTH), 0.1),
        "rwkv_a0": nrm(16, (L, RWKV_WIDTH), 0.1),
        "rwkv_a2": nrm(17, (L, ICLR_RANK, RWKV_WIDTH), 0.1),
        "rwkv_g2": nrm(18, (L, GATE_RANK, RWKV_WIDTH), GATE_RANK ** -0.5),
        "rwkv_k_k": 0.85 + nrm(19, (L, RWKV_WIDTH), 0.05),
        "rwkv_k_a": 1.0 + nrm(20, (L, RWKV_WIDTH), 0.05),
        "rwkv_r_k": nrm(21, (L, RWKV_HEADS, HEAD_DIM), 0.1),
        "rwkv_gn_g": 1.0 + nrm(22, (L, RWKV_WIDTH), 0.05),
        "rwkv_gn_b": nrm(23, (L, RWKV_WIDTH), 0.01),
        "rwkv_out_w": nrm(24, (L, RWKV_WIDTH, D_MODEL), RWKV_WIDTH ** -0.5),
        "w_o": nrm(25, (L, D_MODEL, D_MODEL), D_MODEL ** -0.5),
        "norm2_g": 1.0 + nrm(26, (L, D_MODEL), 0.05),
        "router_group_w": nrm(27, (L, D_MODEL, N_GROUPS), D_MODEL ** -0.5),
        "router_group_b": nrm(28, (L, N_GROUPS), 0.01),
        "router_expert_w": nrm(29, (L, D_MODEL, N_EXPERTS), D_MODEL ** -0.5),
        "router_expert_b": nrm(30, (L, N_EXPERTS), 0.01),
        "expert_w_gate": nrm(31, (L, N_EXPERTS, D_MODEL, D_EXPERT), D_MODEL ** -0.5),
        "expert_w_up": nrm(32, (L, N_EXPERTS, D_MODEL, D_EXPERT), D_MODEL ** -0.5),
        "expert_w_down": nrm(33, (L, N_EXPERTS, D_EXPERT, D_MODEL), D_EXPERT ** -0.5),
        "final_norm_g": 1.0 + nrm(34, (D_MODEL,), 0.05),
    }

def reference(x_prompt, x_sample, state_conv, state_shift, state_wkv, norm1_g, w_in, conv_dw_w, conv_dw_b,
              conv_ln_g, conv_ln_b, conv_out_w, conv_out_b, rwkv_mu, rwkv_w0, rwkv_w2, rwkv_a0, rwkv_a2,
              rwkv_g2, rwkv_k_k, rwkv_k_a, rwkv_r_k, rwkv_gn_g, rwkv_gn_b, rwkv_out_w, w_o, norm2_g,
              router_group_w, router_group_b, router_expert_w, router_expert_b, expert_w_gate, expert_w_up,
              expert_w_down, final_norm_g):
    B = x_prompt.shape[0]
    hp, hs = x_prompt, x_sample
    conv_p, shift_p, wkv_p, conv_s, shift_s, wkv_s = [], [], [], [], [], []
    for l in range(DEPTH):
        w = (norm1_g[l], w_in[l], conv_dw_w[l], conv_dw_b[l], conv_ln_g[l], conv_ln_b[l], conv_out_w[l],
             conv_out_b[l], rwkv_mu[l], rwkv_w0[l], rwkv_w2[l], rwkv_a0[l], rwkv_a2[l], rwkv_g2[l],
             rwkv_k_k[l], rwkv_k_a[l], rwkv_r_k[l], rwkv_gn_g[l], rwkv_gn_b[l], rwkv_out_w[l], w_o[l],
             norm2_g[l], router_group_w[l], router_group_b[l], router_expert_w[l], router_expert_b[l],
             expert_w_gate[l], expert_w_up[l], expert_w_down[l])
        buf0 = jnp.zeros((B, CONV_KERNEL - 1, CONV_WIDTH), jnp.float32)
        shift0 = jnp.zeros((B, D_MODEL), jnp.float32)
        S0 = jnp.zeros((B, RWKV_HEADS, HEAD_DIM, HEAD_DIM), jnp.float32)
        hp, cb, sr, S = layer(hp, buf0, shift0, S0, *w)
        conv_p.append(cb); shift_p.append(sr); wkv_p.append(S)
        hs, cb, sr, S = layer(hs, state_conv[l], state_shift[l], state_wkv[l], *w)
        conv_s.append(cb); shift_s.append(sr); wkv_s.append(S)
    y_prompt = rmsnorm(hp, final_norm_g).astype(x_prompt.dtype)
    y_sample = rmsnorm(hs, final_norm_g).astype(x_sample.dtype)
    sdt = state_wkv.dtype
    return (y_prompt, y_sample,
            jnp.stack(conv_p).astype(state_conv.dtype), jnp.stack(shift_p).astype(state_shift.dtype),
            jnp.stack(wkv_p).astype(sdt),
            jnp.stack(conv_s).astype(state_conv.dtype), jnp.stack(shift_s).astype(state_shift.dtype),
            jnp.stack(wkv_s).astype(sdt))


_drawn_inputs = setup_inputs


def setup_inputs(seed=0):
    import zlib

    import numpy as np

    out = dict(_drawn_inputs(seed))
    spreads = {}
    factors = {'conv_ln_b': 5.594,
     'conv_out_b': 4.113,
     'rwkv_k_k': 24.129,
     'rwkv_gn_b': 5.51,
     'router_group_b': 35.707,
     'conv_dw_b': 3.694,
     'router_expert_b': 4.055}
    for name, (base, spread) in spreads.items():
        noise = np.random.default_rng([zlib.crc32(name.encode()), seed]).standard_normal(out[name].shape)
        drawn = base * np.exp(spread * noise) if base else spread * noise
        out[name] = __import__('jax').numpy.asarray(drawn.astype(out[name].dtype))
    for name, factor in factors.items():
        out[name] = (out[name] * factor).astype(out[name].dtype)
    return out
```

```python
from contextlib import ExitStack
from math import exp

import concourse.bass as bass
from concourse import mybir

P = 128
D = 1024
KC = D // P
NP = 2048
DB, DS = 8, 8
NS = DB * DS
T = NP + NS
TC = T + DB
CW = D // 2
CB = CW // P
CK = 31
HIST = CK - 1
HD = 64
NPAIR = D // P
C = 64
NCH = T // C
RWB = 26
Q, QW = 5, TC // 5
SEG, SW = 6, T // 6
NG, NE, EPG = 4, 32, 8
DE = 256
EB = 128
NBLK = (2 * T + NE * (EB - 1)) // EB
NT = (T + P - 1) // P

ALU = mybir.AluOpType
ACT = mybir.ActivationFunctionType
AX = mybir.AxisListType
F32 = mybir.dt.float32
I32 = mybir.dt.int32
U32 = mybir.dt.uint32
NORM_EPS, LN_EPS, GN_EPS = 1e-6, 1e-5, 64e-5
ds = bass.ds


class Tensors:

    def __init__(self, ins, outs):
        self.xT, self.norm1, self.w_in, self.state_conv, self.conv_w, self.conv_b = (ins[n] for n in ("xT", "norm1", "w_in", "state_conv", "conv_w", "conv_b"))
        self.mu, self.rwkv_par, self.lora, self.norm_par, self.w_branch, self.conv_out_b = (ins[n] for n in ("mu", "rwkv_par", "lora", "norm_par", "w_branch", "conv_out_b"))
        self.w_o, self.router_w, self.router_b, self.norm2, self.x, self.w_up = (ins[n] for n in ("w_o", "router_w", "router_b", "norm2", "x", "w_up"))
        self.w_down, self.ident, self.masks, self.doubling, self.eye, self.seq = (ins[n] for n in ("w_down", "ident", "masks", "doubling", "eye", "seq"))
        self.state_s, self.norm_f, self.earlier = (ins[n] for n in ("state_s", "norm_f", "earlier"))
        self.y_out, self.wkv_p, self.wkv_s, self.shift_p, self.shift_s, self.conv_p = (outs[n] for n in ("y_out", "wkv_p", "wkv_s", "shift_p", "shift_s", "conv_p"))
        self.conv_s = outs["conv_s"]


class Phase:

    def __init__(self, nc, name):
        self.nc, self.name, self.ctx, self.sems = nc, name, ExitStack(), []

    def __enter__(self):
        return self

    def __exit__(self, *a):
        for s in self.sems:
            self.nc.gpsimd.sem_clear(s)
        self.ctx.close()

    def sb(self, name, shape, dt=F32):
        return self.ctx.enter_context(self.nc.sbuf_tensor(f"{self.name}_{name}", shape, dt))

    def psum(self, name, shape, dt=F32):
        return self.ctx.enter_context(self.nc.psum_tensor(f"{self.name}_{name}", shape, dt))

    def sem(self, name):
        self.sems.append(self.ctx.enter_context(self.nc.semaphore(f"{self.name}_{name}")))
        return self.sems[-1]

    def pool_dma_sem(self, name):
        return self.nc.alloc_semaphore(f"{self.name}_{name}")

    def block(self):
        return self.nc.Block()


def norm_inputs(nc, g):
    with Phase(nc, "norm") as ph:
        ones = ph.sb("ones", [P, P])
        raw_shift = ph.sb("raw_shift", [P, KC, DB])
        sq = ph.sb("sq", [P, 2, KC, SW])
        ms = ph.sb("ms", [P, 2, SW])
        rms = ph.sb("rms", [P, 2, SW])
        rstd = ph.sb("rstd", [P, 2, SW])
        gain = ph.sb("gain", [P, KC])
        total = ph.psum("total", [P, 2, 512])
        x_loaded, gain_loaded, out_stored = ph.sem("x_loaded"), ph.sem("gain_loaded"), ph.sem("out_stored")
        ones_set, squared, summed, ms_ready, rms_ready, rstd_ready, scaled = (
            ph.sem(n) for n in ("ones_set", "squared", "summed", "ms_ready", "rms_ready", "rstd_ready", "scaled"))
        with ph.block() as block:
            @block.sync
            def _(sp):
                for kc in range(KC):
                    sp.dma_start(g.u[:, kc, :], g.xT[kc]).then_inc(x_loaded, 16)
                sp.dma_start(gain[:, :], g.norm1).then_inc(gain_loaded, 16)
                sp.wait_ge(scaled, SEG)
                with nc.allow_non_contiguous_dma(reason="one column per channel"):
                    sp.dma_start(g.shift_p, g.u[:, :, NP - 1:NP]).then_inc(out_stored, 16)
                    for kc in range(KC):
                        sp.dma_start(g.shift_s[:, kc], g.u[:, kc, NP + DS - 1:T:DS]).then_inc(out_stored, 16)
                sp.wait_ge(out_stored, 16 * (1 + KC))

            @block.scalar
            def _(act):
                act.wait_ge(x_loaded, 16 * KC)
                with act.Fori(0, SEG // 2) as i:
                    for u in range(2):
                        s = i * 2 + u
                        act.wait_ge(summed, s + 1)
                        act.activation(sq[:, u], g.u[:, :, ds(s * SW, SW)], ACT.Square).then_inc(squared, 1)
                        act.wait_ge(ms_ready, s + 1)
                        act.activation(rms[:, u], ms[:, u], ACT.Sqrt).then_inc(rms_ready, 1)

            @block.tensor
            def _(pe):
                pe.sem_inc(summed, 2)
                pe.wait_ge(ones_set, 1)
                with pe.Fori(0, SEG // 2) as i:
                    for u in range(2):
                        s = i * 2 + u
                        pe.wait_ge(squared, s + 1)
                        pe.wait_ge(ms_ready, s) if u else pe.wait_ge(ms_ready, i * 2)
                        for kc in range(KC):
                            mm = pe.matmul(total[:, u, 0:SW], ones[:, :], sq[:, u, kc], start=kc == 0, stop=kc == KC - 1)
                        mm.then_inc(summed, 1)

            @block.vector
            def _(dve):
                dve.memset(ones[:, :], 1.0).then_inc(ones_set, 1)
                dve.wait_ge(x_loaded, 16 * KC)
                dve.wait_ge(gain_loaded, 16)
                with dve.Fori(0, SEG // 2) as i:
                    for u in range(2):
                        s = i * 2 + u
                        dve.wait_ge(summed, s + 3)
                        dve.tensor_scalar(ms[:, u], total[:, u, 0:SW], 1.0 / D, NORM_EPS, ALU.mult, ALU.add).then_inc(ms_ready, 1)
                        dve.wait_ge(rms_ready, s + 1)
                        dve.reciprocal(rstd[:, u], rms[:, u]).then_inc(rstd_ready, 1)
                        dve.wait_ge(rstd_ready, s + 1)
                        for kc in range(KC):
                            cols = g.u[:, kc, ds(s * SW, SW)]
                            op = dve.scalar_tensor_tensor(cols, cols, gain[:, kc:kc + 1], rstd[:, u], ALU.mult, ALU.mult)
                        op.then_inc(scaled, 1)


def project_block(pe, bank, w, u, waits, bank_ready):
    for q in range(Q):
        waits(q)
        for kc in range(KC):
            mm = pe.matmul(bank[:, q, 0:QW], w[:, kc, :], u[:, kc, q * QW:(q + 1) * QW],
                           start=kc == 0, stop=kc == KC - 1)
        mm.then_inc(bank_ready, 1)


def project_glu(nc, g):
    with Phase(nc, "glu") as ph:
        w = ph.sb("w", [P, 2, KC, P])
        sig = ph.sb("sig", [P, TC])
        bank = ph.psum("bank", [P, Q, 512])
        w_loaded = [ph.sem("gate_w_loaded"), ph.sem("value_w_loaded")]
        gate_ready, value_ready, sig_ready, glu_ready, zeroed, hist_loaded, stored = (
            ph.sem(n) for n in ("gate_ready", "value_ready", "sig_ready", "glu_ready", "zeroed",
                                "hist_loaded", "stored"))
        last = Q - 1
        tail = NP - last * QW
        with ph.block() as block:
            @block.sync
            def _(sp):
                sp.dma_start(g.hist_s[:, :, :, :], g.state_conv).then_inc(hist_loaded, 16)
                with sp.Fori(0, CB) as cb:
                    for u in range(2):
                        sp.wait_ge((gate_ready, value_ready)[u], cb * Q + 1)
                        sp.dma_start(w[:, u], g.w_in[ds(cb + CB * (1 - u), 1)].rearrange("a p k c -> p (a k) c")).then_inc(w_loaded[u], 16)
                sp.wait_ge(glu_ready, Q * CB + Q)
                sp.wait_ge(hist_loaded, 16)
                sp.wait_ge(zeroed, 2)
                with nc.allow_non_contiguous_dma(reason="the last 30 rows of each sequence"):
                    sp.dma_start(g.conv_p, g.glu_p[:, :, NP:NP + HIST]).then_inc(stored, 16)
                    for cb in range(CB):
                        sp.dma_start(g.conv_s[:, cb], g.glu_s[:, cb, :, DS:DS + HIST]).then_inc(stored, 16)
                sp.wait_ge(stored, 16 * (1 + CB))

            @block.tensor
            def _(pe):
                pe.sem_inc(gate_ready, 1)
                pe.sem_inc(value_ready, 1)
                with pe.Fori(0, CB) as cb:
                    pe.wait_ge(w_loaded[0], cb * 16 + 16)
                    project_block(pe, bank, w[:, 0], g.u, lambda q: pe.wait_ge(glu_ready, cb * Q + (q + 1)), gate_ready)
                    pe.wait_ge(w_loaded[1], cb * 16 + 16)
                    project_block(pe, bank, w[:, 1], g.u, lambda q: pe.wait_ge(sig_ready, cb * Q + (q + 1)), value_ready)

            @block.scalar
            def _(act):
                with act.Fori(0, CB) as cb:
                    for q in range(Q):
                        act.wait_ge(gate_ready, cb * Q + (q + 2))
                        act.wait_ge(glu_ready, cb * Q + (q + 1))
                        act.activation(sig[:, q * QW:(q + 1) * QW], bank[:, q, 0:QW], ACT.Sigmoid).then_inc(sig_ready, 1)

            @block.vector
            def _(dve):
                dve.sem_inc(glu_ready, Q)
                dve.memset(g.glu_p[:, :, 0:HIST], 0.0).then_inc(zeroed, 1)
                dve.wait_ge(hist_loaded, 16)
                dve.tensor_copy(g.glu_s[:, :, :, 0:HIST], g.hist_s[:, :, :, :]).then_inc(zeroed, 1)
                with dve.Fori(0, CB) as cb:
                    for q in range(Q):
                        dve.wait_ge(value_ready, cb * Q + (q + 2))
                        dve.wait_ge(sig_ready, cb * Q + (q + 1))
                        n = tail if q == last else QW
                        s0 = q * QW
                        op = dve.tensor_tensor(g.glu_p[:, ds(cb, 1), HIST + s0:HIST + s0 + n].rearrange("p a n -> p (a n)"),
                                               bank[:, q, 0:n], sig[:, s0:s0 + n], ALU.mult)
                        if q == last:
                            op = dve.tensor_tensor(
                                g.glu_s[:, ds(cb, 1), :, HIST:HIST + DS].rearrange("p a b n -> p (a b) n"),
                                bank[:, q, n:n + NS].rearrange("p (b n) -> p b n", n=DS),
                                sig[:, NP:T].rearrange("p (b n) -> p b n", n=DS), ALU.mult)
                        op.then_inc(glu_ready, 1)


def project_rwkv(nc, g):
    with Phase(nc, "mix") as ph:
        w = ph.sb("w", [P, 2, KC, P])
        row = ph.sb("row", [P, 2, 1 + TC])
        diff = ph.sb("diff", [P, 2, T])
        xm = ph.sb("xm", [P, 2, T])
        mu = ph.sb("mu", [P, RWB])
        bank = ph.psum("bank", [P, Q, 512])
        w_loaded = [ph.sem("w_loaded0"), ph.sem("w_loaded1")]
        xm_stored, xm_free = ph.pool_dma_sem("xm_stored"), ph.sem("xm_free")
        bank_ready = [ph.sem("bank_ready0"), ph.sem("bank_ready1")]
        row_ready, zeroed, mu_loaded, shifted, xm_ready, diff_ready, seq_ready = (
            ph.sem(n) for n in ("row_ready", "zeroed", "mu_loaded", "shifted",
                                "xm_ready", "diff_ready", "seq_ready"))
        with ph.block() as block:
            @block.sync
            def _(sp):
                sp.dma_start(mu[:, :], g.mu).then_inc(mu_loaded, 16)
                with sp.Fori(0, RWB // 2) as i:
                    for u in range(2):
                        sp.wait_ge(bank_ready[u], i * Q + 1)
                        sp.dma_start(w[:, u], g.w_in[ds(i * 2 + (u + 2 * CB), 1)].rearrange("a p k c -> p (a k) c")).then_inc(w_loaded[u], 16)

            @block.tensor
            def _(pe):
                pe.sem_inc(bank_ready[0], 1)
                pe.sem_inc(bank_ready[1], 1)
                with pe.Fori(0, RWB // 2) as i:
                    for u in range(2):
                        pe.wait_ge(w_loaded[u], i * 16 + 16)
                        project_block(pe, bank, w[:, u], g.u,
                                      lambda q: pe.wait_ge(row_ready, i * (2 * Q) + (u * Q + q + 1)), bank_ready[u])

            @block.scalar
            def _(act):
                act.sem_inc(row_ready, Q)
                act.wait_ge(zeroed, 1)
                with act.Fori(0, RWB // 2) as i:
                    for u in range(2):
                        act.wait_ge(xm_ready, i * 2 + (u + 1))
                        for q in range(Q):
                            act.wait_ge(bank_ready[u], i * Q + (q + 2))
                            act.copy(row[:, u, 1 + q * QW:1 + (q + 1) * QW], bank[:, q, 0:QW]).then_inc(row_ready, 1)

            @block.vector
            def _(dve):
                dve.sem_inc(xm_ready, 2)
                dve.memset(row[:, :, 0:1], 0.0).then_inc(zeroed, 1)
                dve.wait_ge(mu_loaded, 16)
                dve.wait_ge(zeroed, 1)
                with dve.Fori(0, RWB // 2) as i:
                    for u in range(2):
                        n = i * 2 + u
                        dve.wait_ge(row_ready, n * Q + 2 * Q)
                        now = row[:, u, 1:1 + T]
                        dve.tensor_tensor(diff[:, u], row[:, u, 0:T], now, ALU.subtract).then_inc(diff_ready, 1)
                        dve.wait_ge(diff_ready, n + 1)
                        dve.tensor_tensor(diff[:, u, NP:T:DS], row[:, u, 1 + T:1 + TC], row[:, u, 1 + NP:1 + T:DS],
                                          ALU.subtract).then_inc(seq_ready, 1)
                        dve.wait_ge(seq_ready, n + 1)
                        dve.wait_ge(xm_free, n + 1)
                        dve.scalar_tensor_tensor(xm[:, u], diff[:, u], mu[:, ds(n, 1)], now, ALU.mult, ALU.add).then_inc(xm_ready, 1)

            @block.gpsimd
            def _(pool):
                pool.sem_inc(xm_free, 2)
                with pool.Fori(0, RWB // 2) as i:
                    for u in range(2):
                        pool.wait_ge(xm_ready, i * 2 + (u + 3))
                        pool.dma_start(g.xm[ds(i * 2 + u, 1)].rearrange("a p t -> p (a t)"), xm[:, u]).then_inc(xm_stored, 16)
                        pool.wait_ge(xm_stored, i * 32 + (u + 1) * 16)
                        pool.sem_inc(xm_free, 1)


def project_gates(nc, g):
    with Phase(nc, "gate") as ph:
        w = ph.sb("w", [P, 2, KC, P])
        row = ph.sb("row", [P, 2, T])
        taps = ph.sb("taps", [P, CB, CK])
        bias = ph.sb("bias", [P, CB])
        bank = ph.psum("bank", [P, Q, 512])
        w_loaded = [ph.sem("w_loaded0"), ph.sem("w_loaded1")]
        row_stored, row_free = ph.pool_dma_sem("row_stored"), ph.sem("row_free")
        bank_ready = [ph.sem("bank_ready0"), ph.sem("bank_ready1")]
        row_ready, taps_loaded, tapped = (
            ph.sem(n) for n in ("row_ready", "taps_loaded", "tapped"))
        NB = 2 * KC
        with ph.block() as block:
            @block.sync
            def _(sp):
                sp.dma_start(taps[:, :, :], g.conv_w).then_inc(taps_loaded, 16)
                sp.dma_start(bias[:, :], g.conv_b).then_inc(taps_loaded, 16)
                with sp.Fori(0, NB // 2) as i:
                    for u in range(2):
                        sp.wait_ge(bank_ready[u], i * Q + 1)
                        sp.dma_start(w[:, u], g.w_in[ds(i * 2 + (u + 2 * CB + RWB), 1)].rearrange("a p k c -> p (a k) c")).then_inc(w_loaded[u], 16)

            @block.tensor
            def _(pe):
                pe.sem_inc(bank_ready[0], 1)
                pe.sem_inc(bank_ready[1], 1)
                with pe.Fori(0, NB // 2) as i:
                    for u in range(2):
                        pe.wait_ge(w_loaded[u], i * 16 + 16)
                        project_block(pe, bank, w[:, u], g.u,
                                      lambda q: pe.wait_ge(row_ready, i * (2 * Q) + (u * Q + q + 1)), bank_ready[u])

            @block.scalar
            def _(act):
                act.sem_inc(row_ready, Q)
                with act.Fori(0, NB // 2) as i:
                    for u in range(2):
                        act.wait_ge(row_free, i * 2 + (u + 1))
                        for q in range(Q):
                            n = min(QW, T - q * QW)
                            act.wait_ge(bank_ready[u], i * Q + (q + 2))
                            act.activation(row[:, u, q * QW:q * QW + n], bank[:, q, 0:n], ACT.Sigmoid).then_inc(row_ready, 1)

            @block.vector
            def _(dve):
                dve.wait_ge(taps_loaded, 32)
                with dve.Fori(0, CB) as cb:
                    def full(j, sample):
                        if sample:
                            return g.glu_s[:, ds(cb, 1), :, ds(j, DS)].rearrange("p a b n -> p (a b) n")
                        return g.glu_p[:, ds(cb, 1), ds(j, NP)].rearrange("p a n -> p (a n)")

                    acc_p = g.conv[:, ds(cb, 1), 0:NP].rearrange("p a n -> p (a n)")
                    acc_s = g.conv[:, ds(cb, 1), NP:T].rearrange("p a (b n) -> p (a b) n", n=DS)
                    for acc, sample in ((acc_p, 0), (acc_s, 1)):
                        dve.tensor_scalar(acc, full(0, sample), taps[:, ds(cb, 1), 0], bias[:, ds(cb, 1)],
                                          ALU.mult, ALU.add).then_inc(tapped, 1)
                    with dve.Fori(0, HIST) as j:
                        for acc, sample in ((acc_p, 0), (acc_s, 1)):
                            dve.wait_ge(tapped, cb * (2 * CK) + j * 2 + (sample + 1))
                            dve.scalar_tensor_tensor(acc, full(j + 1, sample), taps[:, ds(cb, 1), ds(j + 1, 1)].rearrange("p a j -> p (a j)"),
                                                     acc, ALU.mult, ALU.add).then_inc(tapped, 1)

            @block.gpsimd
            def _(pool):
                pool.sem_inc(row_free, 2)
                with pool.Fori(0, NB // 2) as i:
                    for u in range(2):
                        pool.wait_ge(row_ready, i * (2 * Q) + (u + 2) * Q)
                        pool.dma_start(g.gates[ds(i * 2 + u, 1)].rearrange("a p t -> p (a t)"), row[:, u]).then_inc(row_stored, 16)
                        pool.wait_ge(row_stored, i * 32 + (u + 1) * 16)
                        pool.sem_inc(row_free, 1)


def prepare_recurrence(nc, g):
    with Phase(nc, "prep") as ph:
        lora_in = ph.sb("lora_in", [P, T])
        gate_in = ph.sb("gate_in", [P, T])
        keep = ph.sb("keep", [P, T])
        rows = {n: ph.sb(n, [P, T]) for n in
                ("r", "k", "v", "W", "L", "X1", "X2", "X3", "A", "N", "KK", "G", "RK", "B")}
        r, k, v, W, L, X1, X2, X3, A, N, KK, G, RK, B = rows.values()
        heads = ph.sb("heads", [P, P])
        lora_w = ph.sb("lora_w", [P, 3, P])
        par = ph.sb("par", [P, NPAIR, 6])
        pp = ph.sb("pp", [P, 6])
        lora_bank = ph.psum("lora_bank", [P, 3, 2, 512])
        head_bank = ph.psum("head_bank", [P, 2, 512])
        r_loaded, k_loaded, v_loaded, lora_loaded, par_loaded, in_loaded = (
            ph.pool_dma_sem(n) for n in ("r_loaded", "k_loaded", "v_loaded", "lora_loaded", "par_loaded", "in_loaded"))
        consts_set, in_ready, keep_set, pp_ready, g_stored, alpha_stored, rho_stored, beta_stored, kappa_stored, bonus_stored = (
            ph.sem(n) for n in ("consts_set", "in_ready", "keep_set", "pp_ready", "g_stored", "alpha_stored", "rho_stored",
                                "beta_stored", "kappa_stored", "bonus_stored"))
        sq_ready, lw_ready, sum_ready, before_ready, kk0_ready, rn_ready, kk_ready, t1_ready, kp_ready, b_ready, \
            lam_ready, lam_before_ready, lam_inv_ready, alpha_ready, rho_ready, rk_ready, kappa_ready, beta_ready, \
            ends_ready, ln_ready = credit = [ph.sem(n) for n in (
                "sq_ready", "lw_ready", "sum_ready", "before_ready", "kk0_ready", "rn_ready", "kk_ready", "t1_ready",
                "kp_ready", "b_ready", "lam_ready", "lam_before_ready", "lam_inv_ready", "alpha_ready", "rho_ready",
                "rk_ready", "kappa_ready", "beta_ready", "ends_ready", "ln_ready")]
        lora_done, lora_read, head_done, head_read = (
            ph.sem(n) for n in ("lora_done", "lora_read", "head_done", "head_read"))
        seg = [slice(s * SW, (s + 1) * SW) for s in range(SEG)]
        stores = ((g_stored, 16), (alpha_stored, 16), (rho_stored, 16), (beta_stored, 16), (kappa_stored, 16), (bonus_stored, 16))

        with ph.block() as block:
            @block.gpsimd
            def _(pool):
                pool.dma_start(par[:, :, :], g.rwkv_par).then_inc(par_loaded, 16)
                pool.dma_start(lora_in[:, :], g.xm[RWB - 2]).then_inc(in_loaded, 16)
                pool.dma_start(gate_in[:, :], g.xm[RWB - 1]).then_inc(in_loaded, 16)
                with pool.Fori(0, NPAIR) as p:
                    def this(s):
                        pool.wait_ge(s, p + 1)
                    pool.wait_ge(lora_done, p * SEG + 1)
                    pool.dma_start(lora_w[:, :, :], g.lora[ds(p, 1)].rearrange("a p k c -> p (a k) c")).then_inc(lora_loaded, 16)
                    this(rk_ready)
                    this(kappa_ready)
                    pool.dma_start(k[:, :], g.xm[ds(p + NPAIR, 1)].rearrange("a p t -> p (a t)")).then_inc(k_loaded, 16)
                    this(rho_ready)
                    this(rk_ready)
                    pool.dma_start(r[:, :], g.xm[ds(p, 1)].rearrange("a p t -> p (a t)")).then_inc(r_loaded, 16)
                    pool.wait_ge(head_read, p * (2 * SEG) + 2)
                    pool.dma_start(v[:, :], g.xm[ds(p + 2 * NPAIR, 1)].rearrange("a p t -> p (a t)")).then_inc(v_loaded, 16)

            @block.sync
            def _(sp):
                for s, n in stores:
                    sp.sem_inc(s, n)
                with sp.Fori(0, NPAIR) as p:
                    def chunked(i):
                        return g.zc[:, :, i, ds(p, 1), :].rearrange("c p a t -> p c (a t)")

                    def row(x):
                        return x[:, :].rearrange("p (c t) -> p c t", t=C)
                    sp.wait_ge(lora_read, p * SEG + (SEG + 2))
                    sp.dma_start(g.go[ds(p, 1)].rearrange("a p t -> p (a t)"), G[:, :]).then_inc(g_stored, 16)
                    for ready, i, x, stored in ((alpha_ready, 0, X1, alpha_stored), (rho_ready, 1, X2, rho_stored),
                                                (kappa_ready, 3, X3, kappa_stored), (beta_ready, 2, A, beta_stored)):
                        sp.wait_ge(ready, p + 2)
                        sp.dma_start(chunked(i), row(x)).then_inc(stored, 16)
                    sp.wait_ge(head_read, p * (2 * SEG) + (2 * SEG + 2))
                    sp.dma_start(g.bonus[ds(p, 1)].rearrange("a p t -> p (a t)"), B[:, :]).then_inc(bonus_stored, 16)
                for s, n in stores:
                    sp.wait_ge(s, n + 16 * NPAIR)

            @block.tensor
            def _(pe):
                pe.sem_inc(lora_done, 1)
                pe.sem_inc(head_done, 1)
                pe.wait_ge(consts_set, 3)
                pe.wait_ge(in_ready, 2)
                with pe.Fori(0, NPAIR) as p:
                    pe.wait_ge(lora_loaded, p * 16 + 16)
                    for s in range(SEG):
                        pe.wait_ge(lora_read, p * SEG + (s + 1))
                        for j, x in enumerate((lora_in, lora_in, gate_in)):
                            mm = pe.matmul(lora_bank[:, j, s % 2, 0:SW], lora_w[:, j, :], x[:, seg[s]], start=True, stop=True)
                        mm.then_inc(lora_done, 1)
                    for h, (ready, x) in enumerate(((sq_ready, RK), (rk_ready, RK))):
                        pe.wait_ge(ready, p + 2)
                        for s in range(SEG):
                            pe.wait_ge(head_read, p * (2 * SEG) + (h * SEG + s + 1))
                            pe.matmul(head_bank[:, s % 2, 0:SW], heads[:, :], x[:, seg[s]], start=True, stop=True).then_inc(head_done, 1)

            @block.scalar
            def _(act):
                for s in (sq_ready, lam_ready, lam_before_ready, lam_inv_ready, rn_ready, ln_ready):
                    act.sem_inc(s, 1)
                act.sem_inc(lora_read, 2)
                act.wait_ge(in_loaded, 32)
                act.activation(lora_in[0:C, :], lora_in[0:C, :], ACT.Tanh).then_inc(in_ready, 1)
                act.activation(gate_in[:, :], gate_in[:, :], ACT.Sigmoid).then_inc(in_ready, 1)
                act.wait_ge(par_loaded, 16)
                with act.Fori(0, NPAIR) as p:
                    def last(s):
                        act.wait_ge(s, p + 1)
                    act.wait_ge(k_loaded, p * 16 + 16)
                    act.wait_ge(head_done, p * (2 * SEG) + 1)
                    act.wait_ge(pp_ready, p + 1)
                    act.activation(RK[:, :], k[:, :], ACT.Square, scale=pp[:, 2:3]).then_inc(sq_ready, 1)
                    last(before_ready)
                    last(sum_ready)
                    act.wait_ge(beta_stored, p * 16 + 16)
                    act.wait_ge(g_stored, p * 16 + 16)
                    for s in range(SEG):
                        act.wait_ge(lora_done, p * SEG + (s + 2))
                        act.activation(W[:, seg[s]], lora_bank[:, 0, s % 2, 0:SW], ACT.Sigmoid, bias=pp[:, 0:1])
                        act.activation(A[:, seg[s]], lora_bank[:, 1, s % 2, 0:SW], ACT.Sigmoid, bias=pp[:, 1:2])
                        act.copy(G[:, seg[s]], lora_bank[:, 2, s % 2, 0:SW]).then_inc(lora_read, 1)
                    act.wait_ge(head_read, p * (2 * SEG) + (SEG + 2))
                    act.activation(N[:, :], N[:, :], ACT.Ln, scale=2.0 ** 30).then_inc(ln_ready, 1)
                    act.wait_ge(ln_ready, p + 2)
                    act.activation(N[:, :], N[:, :], ACT.Exp, scale=-0.5).then_inc(rn_ready, 1)
                    act.wait_ge(before_ready, p + 2)
                    act.activation(X1[:, :], X1[:, :], ACT.Exp).then_inc(lam_before_ready, 1)
                    act.wait_ge(rho_stored, p * 16 + 16)
                    act.activation(X2[:, :], L[:, :], ACT.Exp).then_inc(lam_ready, 1)
                    act.wait_ge(kappa_stored, p * 16 + 16)
                    act.activation(X3[:, :], L[:, :], ACT.Exp, scale=-1.0).then_inc(lam_inv_ready, 1)

            @block.vector
            def _(dve):
                for s in credit:
                    if s not in (sq_ready, lam_ready, lam_before_ready, lam_inv_ready, rn_ready, ln_ready):
                        dve.sem_inc(s, 1)
                dve.sem_inc(head_read, 2)
                dve.memset(heads[:, :], 0.0).then_inc(consts_set, 1)
                dve.wait_ge(consts_set, 1)
                for h in range(2):
                    o = dve.memset(heads[h * HD:(h + 1) * HD, h * HD:(h + 1) * HD], 1.0).then_inc(consts_set, 1)
                dve.memset(keep[:, :], 1.0).then_inc(keep_set, 1)
                dve.wait_ge(keep_set, 1)
                dve.memset(keep[:, 0:NP:C], 0.0)
                dve.memset(keep[:, NP:T:DS], 0.0).then_inc(keep_set, 1)
                dve.wait_ge(par_loaded, 16)
                dve.tensor_scalar(par[:, :, 4], par[:, :, 3], -1.0, 1.0, ALU.mult, ALU.add).then_inc(keep_set, 1)
                dve.wait_ge(keep_set, 3)
                with dve.Fori(0, NPAIR) as p:
                    def this(s):
                        dve.wait_ge(s, p + 2)
                    pd = ds(p, 1)
                    dve.wait_ge(lora_read, p * SEG + 2)
                    dve.tensor_copy(pp[:, :], par[:, pd, :].rearrange("p a n -> p (a n)")).then_inc(pp_ready, 1)
                    dve.wait_ge(pp_ready, p + 1)
                    dve.wait_ge(k_loaded, p * 16 + 16)
                    dve.tensor_scalar(KK[:, :], k[:, :], pp[:, 2:3], 2.0 ** 15, ALU.mult, ALU.mult).then_inc(kk0_ready, 1)
                    for s in range(SEG):
                        dve.wait_ge(head_done, p * (2 * SEG) + (s + 2))
                        dve.tensor_scalar(N[:, seg[s]], head_bank[:, s % 2, 0:SW], 1e-24, None, ALU.max).then_inc(head_read, 1)
                    dve.wait_ge(lora_read, p * SEG + (SEG + 2))
                    dve.tensor_scalar(W[:, :], W[:, :], -exp(-0.5), None, ALU.mult).then_inc(lw_ready, 1)
                    this(lw_ready)
                    dve.tensor_tensor_scan(L[:, :], keep[:, :], W[:, :], 0.0, ALU.mult, ALU.add).then_inc(sum_ready, 1)
                    this(sum_ready)
                    dve.wait_ge(alpha_stored, p * 16 + 16)
                    dve.tensor_tensor(X1[:, :], L[:, :], W[:, :], ALU.subtract).then_inc(before_ready, 1)
                    this(before_ready)
                    dve.tensor_scalar(W[:, :], A[:, :], pp[:, 3:4], pp[:, 4:5], ALU.mult, ALU.add).then_inc(t1_ready, 1)
                    this(t1_ready)
                    dve.tensor_tensor(k[:, :], k[:, :], W[:, :], ALU.mult).then_inc(kp_ready, 1)
                    this(rn_ready)
                    dve.tensor_tensor(KK[:, :], KK[:, :], N[:, :], ALU.mult).then_inc(kk_ready, 1)
                    this(kk_ready)
                    dve.tensor_tensor(A[:, :], A[:, :], KK[:, :], ALU.mult).then_inc(b_ready, 1)
                    this(kp_ready)
                    dve.wait_ge(r_loaded, p * 16 + 16)
                    dve.scalar_tensor_tensor(RK[:, :], r[:, :], pp[:, 5:6], k[:, :], ALU.mult, ALU.mult).then_inc(rk_ready, 1)
                    this(lam_before_ready)
                    dve.tensor_tensor(X1[:, :], X1[:, :], KK[:, :], ALU.mult).then_inc(alpha_ready, 1)
                    this(lam_ready)
                    dve.tensor_copy(g.lam_p[:, pd, :].rearrange("p a c -> p (a c)"), X2[:, C - 1:NP:C])
                    dve.tensor_copy(g.lam_s[:, pd, :].rearrange("p a c -> p (a c)"), X2[:, NP + DS - 1:T:DS]).then_inc(ends_ready, 1)
                    this(ends_ready)
                    dve.tensor_tensor(X2[:, :], X2[:, :], r[:, :], ALU.mult).then_inc(rho_ready, 1)
                    this(lam_inv_ready)
                    this(b_ready)
                    dve.tensor_tensor(A[:, :], A[:, :], X3[:, :], ALU.mult).then_inc(beta_ready, 1)
                    this(beta_ready)
                    dve.tensor_tensor(X3[:, :], X3[:, :], k[:, :], ALU.mult).then_inc(kappa_ready, 1)
                    dve.wait_ge(v_loaded, p * 16 + 16)
                    dve.wait_ge(bonus_stored, p * 16 + 16)
                    for s in range(SEG):
                        dve.wait_ge(head_done, p * (2 * SEG) + (SEG + s + 2))
                        dve.tensor_tensor(B[:, seg[s]], head_bank[:, s % 2, 0:SW], v[:, seg[s]], ALU.mult).then_inc(head_read, 1)


def recurrence(nc, g):
    LEVELS = 5
    with Phase(nc, "wkv") as ph:
        z = ph.sb("z", [P, 2, 4, NPAIR, C])
        v = ph.sb("v", [P, 2, NPAIR, C])
        masks = ph.sb("masks", [P, 2, 5, C])
        doubling = ph.sb("doubling", [P, LEVELS, C], I32)
        eye = ph.sb("eye", [P, C])
        seq = ph.sb("seq", [P, DB])
        state = ph.sb("state", [P, NPAIR, HD])
        grown = ph.sb("grown", [P, NPAIR, HD])
        tt = ph.sb("tt", [P, NPAIR, C])
        zt = ph.sb("zt", [P, NPAIR, C])
        ws = ph.sb("ws", [P, NPAIR, HD])
        us = ph.sb("us", [P, NPAIR, HD])
        qt, rt, vt = (ph.sb(n, [P, 2, NPAIR, C]) for n in ("qt", "rt", "vt"))
        ys = ph.sb("ys", [P, 2, NPAIR, C])
        BD = [P, NPAIR, 2, C]
        beta_bd, kappa_bd, v_bd, a_bd, t_bd, u_bd, state_bd = single = [
            ph.sb(n, BD) for n in ("beta_bd", "kappa_bd", "v_bd", "a_bd", "t_bd", "u_bd", "state_bd")]
        alpha_bd, bt_bd, tt_bd, vt_bd, betat_bd, kappat_bd = double = [
            ph.sb(n, [P, 2] + BD[1:]) for n in ("alpha_bd", "bt_bd", "tt_bd", "vt_bd", "betat_bd", "kappat_bd")]
        bank = ph.psum("bank", [P, 8, NPAIR, C])
        states_s = ph.sb("states_s", [P, NPAIR, DB, HD])
        picked = ph.sb("picked", [P, DB, HD])
        read_s = ph.sb("read_s", [P, NPAIR, HD])
        T_BANK, Z_BANK, X_BANK, B3, B4, W_BANK, Y_BANK, S_BANK = range(8)

        z_loaded, v_loaded = ([ph.sem(f"{n}_loaded{u}") for u in range(2)] for n in ("z", "v"))
        y_stored = [ph.sem("y_stored0"), ph.sem("y_stored1")]
        consts_loaded, state_stored, cleared, expanded, aq_done, br_done, a_done, vt_done, betat_done, kappat_done, \
            t_done, z_done, x_done, tt_ready, q_ready, br_ready, a_ready, vt_ready, betat_ready, kappat_ready, \
            t_ready, z_ready, tt_bd_ready, vt_bd_ready, w_done, w_ready, u_done, u_ready, u_bd_ready, y_done, y_ready, \
            s_done, grown_ready, state_ready, state_bd_ready, cross_done, masked, cross_read, cross_picked, masked_tt, bv_ready = (
                ph.sem(n) for n in (
                    "consts_loaded", "state_stored", "cleared", "expanded", "aq_done", "br_done", "a_done", "vt_done",
                    "betat_done", "kappat_done", "t_done", "z_done", "x_done", "tt_ready", "q_ready", "br_ready",
                    "a_ready", "vt_ready", "betat_ready", "kappat_ready", "t_ready", "z_ready", "tt_bd_ready",
                    "vt_bd_ready", "w_done", "w_ready", "u_done", "u_ready", "u_bd_ready", "y_done", "y_ready",
                    "s_done", "grown_ready", "state_ready", "state_bd_ready", "cross_done", "masked", "cross_read",
                    "cross_picked", "masked_tt", "bv_ready"))
        half = [slice(0, HD), slice(HD, P)]
        NPC = NCH - 1

        def spread(copy, dst, src):
            copy(dst[half[0], :, 0, :], src[half[0]])
            return copy(dst[half[1], :, 1, :], src[half[1]])

        def over_pairs(m, n=NPAIR):
            return m.unsqueeze(1).to_broadcast([m.shape[0], n, m.shape[1]])
        passed, dve_passed = ph.sem("passed"), ph.sem("dve_passed")

        with ph.block() as block:
            @block.sync
            def _(sp):
                for dst, src in ((masks, g.masks), (doubling, g.doubling), (eye, g.eye), (seq, g.seq), (states_s, g.state_s)):
                    sp.dma_start(dst[:], src).then_inc(consts_loaded, 16)
                sp.sem_inc(y_stored[0], 16)
                sp.sem_inc(y_stored[1], 16)

                def load(c, u):
                    sp.wait_ge(y_done, c + 1)
                    sp.dma_start(z[:, u].rearrange("p i a t -> p (i a t)"),
                                 g.zc[ds(c, 1)].rearrange("c p i a t -> p (c i a t)")).then_inc(z_loaded[u], 16)
                    sp.dma_start(v[:, u], g.xm[2 * NPAIR:3 * NPAIR, :, ds(c * C, C)].rearrange("a p t -> p a t")).then_inc(v_loaded[u], 16)

                def store(c, u):
                    sp.wait_ge(consts_loaded, 80)
                    sp.wait_ge(y_ready, c + 2)
                    sp.dma_start(g.y[:, :, ds(c * C, C)].rearrange("a p t -> p a t"), ys[:, u]).then_inc(y_stored[u], 16)

                load(0, 0)
                with sp.Fori(0, NPC // 2) as i:
                    for u in range(2):
                        load(i * 2 + (u + 1), 1 - u)
                        store(i * 2 + u, u)
                sp.wait_ge(state_ready, NPC + 1)
                sp.dma_start(g.wkv_p, state[:, :, :]).then_inc(state_stored, 16)
                store(NPC, 0)
                sp.wait_ge(bv_ready, NPAIR + 1)
                sp.dma_start(g.wkv_s, states_s[:, :, :, :]).then_inc(state_stored, 16)
                sp.wait_ge(state_stored, 32)
                sp.wait_ge(y_stored[0], 16 * (NPC // 2) + 32)
                sp.wait_ge(y_stored[1], 16 * (NPC // 2) + 16)

            @block.gpsimd
            def _(pool):
                for t in (*single, state):
                    pool.memset(t[:], 0.0)
                for t in double:
                    op = pool.memset(t[:], 0.0)
                op.then_inc(cleared, 1)
                pool.wait_ge(cleared, 1)
                pool.sem_inc(state_bd_ready, 1)
                pool.sem_inc(tt_bd_ready, 1)

                def prepare(c, u):
                    pool.wait_ge(z_loaded[u], c * 8 + (16 - 8 * u))
                    pool.wait_ge(v_loaded[u], c * 8 + (16 - 8 * u))
                    pool.wait_ge(kappat_done, c + 1)
                    pool.wait_ge(w_done, c + 1)
                    pool.sem_inc(passed, 1)
                    for dst, src in ((alpha_bd[:, u], z[:, u, 0]), (beta_bd, z[:, u, 2]), (kappa_bd, z[:, u, 3]), (v_bd, v[:, u])):
                        op = spread(pool.tensor_copy, dst, src)
                    op.then_inc(expanded, 1)

                def spread_tt(c, u, l):
                    pool.wait_ge(tt_ready, c * (LEVELS + 1) + (LEVELS + 2 + l))
                    if l == 0:
                        pool.wait_ge(u_done, c + 1)
                    pool.sem_inc(passed, 1)
                    spread(pool.tensor_copy, tt_bd[:, u], tt).then_inc(tt_bd_ready, 1)

                def spread_vt(c, u):
                    pool.wait_ge(vt_ready, c + 1)
                    pool.wait_ge(y_done, c + 1)
                    pool.sem_inc(passed, 1)
                    spread(pool.tensor_copy, vt_bd[:, u], vt[:, u]).then_inc(vt_bd_ready, 1)

                def advance_u(c):
                    pool.wait_ge(u_ready, c + 2)
                    pool.wait_ge(y_done, c + 2)
                    pool.sem_inc(passed, 1)
                    spread(pool.tensor_copy, u_bd, us).then_inc(u_bd_ready, 1)

                def advance_state(c):
                    pool.wait_ge(state_ready, c + 2)
                    pool.wait_ge(y_done, c + 3)
                    pool.sem_inc(passed, 1)
                    spread(pool.tensor_copy, state_bd, state).then_inc(state_bd_ready, 1)

                def ahead(c, u, advance=None):
                    prepare(c, u)
                    if advance is None:
                        spread_tt(c, u, 0)
                        spread_vt(c, u)
                        for l in range(1, LEVELS + 1):
                            spread_tt(c, u, l)
                        return
                    spread_tt(c, u, 0)
                    spread_vt(c, u)
                    spread_tt(c, u, 1)
                    advance_u(advance)
                    spread_tt(c, u, 2)
                    spread_tt(c, u, 3)
                    advance_state(advance)
                    spread_tt(c, u, 4)
                    spread_tt(c, u, 5)

                ahead(0, 0)
                with pool.Fori(0, NPC // 2 - 1) as i:
                    ahead(i * 2 + 1, 1, i * 2)
                    ahead(i * 2 + 2, 0, i * 2 + 1)
                ahead(NPC - 1, 1, NPC - 2)
                ahead(NPC, 0, NPC - 1)
                pool.wait_ge(cleared, 1)
                pool.wait_ge(kappat_done, NPC + 2)
                pool.sem_inc(passed, 1)
                spread(pool.tensor_copy, beta_bd, z[:, 0, 1]).then_inc(expanded, 1)
                advance_u(NPC)
                pool.wait_ge(cleared, 1)
                pool.wait_ge(cross_picked, 2 * NPAIR + 1)
                pool.wait_ge(expanded, NPC + 2)
                pool.sem_inc(passed, 1)
                spread(pool.tensor_copy, state_bd, read_s).then_inc(state_bd_ready, 1)

            @block.tensor
            def _(pe):
                for s, n in ((kappat_done, 1), (w_done, 2), (u_done, 2), (y_done, 2), (s_done, 2)):
                    pe.sem_inc(s, n)
                pe.wait_ge(cleared, 1)
                pe.wait_ge(consts_loaded, 80)

                def pairs(out, *terms):
                    for a in range(NPAIR):
                        for n, (lhs, rhs) in enumerate(terms):
                            mm = pe.matmul(out(a), lhs[:, a].rearrange("p h t -> p (h t)"), rhs(a),
                                           start=n == 0, stop=n == len(terms) - 1)
                    return mm

                def flat(b):
                    return lambda a: bank[:, b, a, :]

                def wide(b):
                    return lambda a: bank[:, b + a // 4, 2 * (a % 4):2 * (a % 4) + 2, :]

                def products(c, u):
                    pe.wait_ge(expanded, c + 1)
                    pe.wait_ge(tt_ready, c * (LEVELS + 1) + (LEVELS + 1))
                    pairs(wide(T_BANK), (beta_bd, lambda a: z[:, u, 0:2, a, :])).then_inc(aq_done, 1)
                    pe.wait_ge(kappat_ready, c + 1)
                    pairs(wide(X_BANK), (kappa_bd, lambda a: z[:, u, 0:2, a, :])).then_inc(br_done, 1)
                    pe.wait_ge(betat_ready, c + 1)
                    pairs(flat(B4), (alpha_bd[:, u], lambda a: z[:, u, 2, a, :])).then_inc(a_done, 1)

                def turn_v_beta(c):
                    pe.wait_ge(br_ready, c + 1)
                    pairs(flat(B3), (v_bd, lambda a: eye[:, :])).then_inc(vt_done, 1)
                    pe.wait_ge(a_ready, c + 1)
                    pairs(flat(B4), (beta_bd, lambda a: eye[:, :])).then_inc(betat_done, 1)

                def turn_kappa(c):
                    pe.wait_ge(vt_ready, c + 1)
                    pairs(flat(B3), (kappa_bd, lambda a: eye[:, :])).then_inc(kappat_done, 1)

                def level(c, u, l):
                    pe.wait_ge(tt_ready, c * (LEVELS + 1) + (LEVELS + 2 + l))
                    pe.wait_ge(a_ready, c + 1)
                    pairs(flat(Z_BANK), (a_bd, lambda a: tt[:, a, :])).then_inc(z_done, 1)
                    pe.wait_ge(tt_bd_ready, c * (LEVELS + 1) + (l + 2))
                    pairs(flat(T_BANK), (tt_bd[:, u], lambda a: eye[:, :])).then_inc(t_done, 1)

                def level_close(c, l):
                    pe.wait_ge(t_ready, c * LEVELS + (l + 1))
                    pe.wait_ge(z_ready, c * LEVELS + (l + 1))
                    pairs(flat(X_BANK), (t_bd, lambda a: zt[:, a, :])).then_inc(x_done, 1)

                def w_products(c, u):
                    pe.wait_ge(vt_ready, c + 1)
                    pe.wait_ge(state_ready, c + 1)
                    pe.wait_ge(u_ready, c + 1)
                    pairs(flat(W_BANK), (bt_bd[:, u], lambda a: vt[:, u, a, :]),
                          (alpha_bd[:, u], lambda a: state[:, a, :])).then_inc(w_done, 1)

                def u_products(c, u):
                    pe.wait_ge(tt_bd_ready, c * (LEVELS + 1) + (LEVELS + 2))
                    pe.wait_ge(w_ready, c + 1)
                    pairs(flat(W_BANK), (tt_bd[:, u], lambda a: ws[:, a, :])).then_inc(u_done, 1)

                def state_products(c, u):
                    pe.wait_ge(u_ready, c + 2)
                    pe.wait_ge(kappat_ready, c + 2)
                    pe.wait_ge(betat_ready, c + 2)
                    pairs(flat(S_BANK), (kappat_bd[:, u], lambda a: vt[:, u, a, :]),
                          (betat_bd[:, u], lambda a: us[:, a, :])).then_inc(s_done, 1)

                def y_products(c, u, read):
                    pe.wait_ge(vt_bd_ready, c + 1)
                    pe.wait_ge(state_bd_ready, c + 1)
                    pe.wait_ge(u_bd_ready, c + 1)
                    pe.wait_ge(q_ready, c + 1)
                    pe.wait_ge(y_ready, c + 1)
                    pairs(flat(Y_BANK), (vt_bd[:, u], lambda a: rt[:, u, a, :]), (state_bd, read),
                          (u_bd, lambda a: qt[:, u, a, :])).then_inc(y_done, 1)

                def ahead(c, u, advance=None):
                    def back(step, *a):
                        if advance is not None:
                            step(advance, 1 - u, *a)
                    back(w_products)
                    products(c, u)
                    back(u_products)
                    turn_v_beta(c)
                    level(c, u, 0)
                    turn_kappa(c)
                    level_close(c, 0)
                    back(state_products)
                    level(c, u, 1)
                    level_close(c, 1)
                    level(c, u, 2)
                    back(y_products, lambda a: z[:, 1 - u, 1, a, :])
                    level_close(c, 2)
                    level(c, u, 3)
                    level_close(c, 3)
                    level(c, u, 4)
                    level_close(c, 4)

                ahead(0, 0)
                with pe.Fori(0, NPC // 2 - 1) as i:
                    ahead(i * 2 + 1, 1, i * 2)
                    ahead(i * 2 + 2, 0, i * 2 + 1)
                ahead(NPC - 1, 1, NPC - 2)
                ahead(NPC, 0, NPC - 1)

                c = NPC
                pe.wait_ge(expanded, c + 2)
                pe.wait_ge(u_ready, c + 1)
                for n, lhs in enumerate((alpha_bd[:, 0], beta_bd)):
                    for a in range(NPAIR):
                        pe.wait_ge(masked, n * NPAIR + a + 1)
                        pe.matmul(bank[:, W_BANK].rearrange("p a t -> p (a t)"), lhs[:, a].rearrange("p h t -> p (h t)"),
                                  states_s[:, a].rearrange("p b v -> p (b v)"), start=True, stop=True).then_inc(cross_done, 1)
                pe.wait_ge(masked, 2 * NPAIR + 1)
                pairs(flat(W_BANK), (bt_bd[:, 0], lambda a: vt[:, 0, a, :])).then_inc(w_done, 1)
                u_products(c, 0)
                pe.wait_ge(state_bd_ready, c + 2)
                y_products(c, 0, lambda a: eye[:, :])
                pe.wait_ge(kappat_ready, c + 2)
                pe.wait_ge(betat_ready, c + 2)
                for a in range(NPAIR):
                    pe.wait_ge(grown_ready, NPC + a)
                    pe.wait_ge(cross_read, 2 * a + 2)
                    pe.matmul(bank[:, S_BANK].rearrange("p a t -> p (a t)"), kappat_bd[:, 0, a].rearrange("p h t -> p (h t)"),
                              z[:, 0].rearrange("p i a t -> p (i a t)")[:, 0:DB * HD], start=True, stop=False)
                    pe.matmul(bank[:, S_BANK].rearrange("p a t -> p (a t)"), betat_bd[:, 0, a].rearrange("p h t -> p (h t)"),
                              z[:, 0].rearrange("p i a t -> p (i a t)")[:, DB * HD:2 * DB * HD], start=False, stop=True).then_inc(s_done, 1)

            @block.scalar
            def _(act):
                act.sem_inc(betat_ready, 1)
                act.sem_inc(kappat_ready, 1)
                act.sem_inc(y_ready, 1)
                act.wait_ge(cleared, 1)

                def turn_v_beta(c, u):
                    act.wait_ge(vt_done, c + 1)
                    act.wait_ge(y_done, c + 1)
                    act.copy(vt[:, u], bank[:, B3]).then_inc(vt_ready, 1)
                    act.wait_ge(betat_done, c + 1)
                    spread(lambda o, x: act.mul(o, x, -1.0), betat_bd[:, u], bank[:, B4]).then_inc(betat_ready, 1)

                def turn_kappa(c, u):
                    act.wait_ge(kappat_done, c + 2)
                    spread(act.copy, kappat_bd[:, u], bank[:, B3]).then_inc(kappat_ready, 1)

                def level(c, l):
                    act.wait_ge(t_done, c * LEVELS + (l + 1))
                    spread(act.copy, t_bd, bank[:, T_BANK]).then_inc(t_ready, 1)

                def advance_y(c, u):
                    act.wait_ge(y_done, c + 3)
                    act.wait_ge(y_stored[u], c * 8 + (16 - 8 * u))
                    act.copy(ys[:, u], bank[:, Y_BANK]).then_inc(y_ready, 1)

                def ahead(c, u, advance=None):
                    turn_v_beta(c, u)
                    level(c, 0)
                    turn_kappa(c, u)
                    level(c, 1)
                    level(c, 2)
                    if advance is not None:
                        advance_y(advance, 1 - u)
                    level(c, 3)
                    level(c, 4)

                ahead(0, 0)
                with act.Fori(0, NPC // 2 - 1) as i:
                    ahead(i * 2 + 1, 1, i * 2)
                    ahead(i * 2 + 2, 0, i * 2 + 1)
                ahead(NPC - 1, 1, NPC - 2)
                ahead(NPC, 0, NPC - 1)
                advance_y(NPC, 0)

            @block.vector
            def _(dve):
                dve.sem_inc(tt_ready, LEVELS + 1)
                dve.sem_inc(u_ready, 1)
                dve.sem_inc(state_ready, 1)
                dve.wait_ge(cleared, 1)
                dve.wait_ge(consts_loaded, 80)
                wide_aq = bank[:, T_BANK:T_BANK + 2].rearrange("p b (a w) t -> p (b a) w t", w=2)
                wide_br = bank[:, X_BANK:X_BANK + 2].rearrange("p b (a w) t -> p (b a) w t", w=2)

                def products(c, u, m):
                    dve.wait_ge(aq_done, c + 1)
                    dve.wait_ge(tt_bd_ready, c * (LEVELS + 1) + 1)
                    dve.tensor_tensor(tt[:, :, :], wide_aq[:, :, 0, :], over_pairs(masks[:, m, 0]), ALU.mult).then_inc(masked_tt, 1)
                    dve.wait_ge(y_done, c + 1)
                    dve.tensor_tensor(qt[:, u], wide_aq[:, :, 1, :], over_pairs(masks[:, m, 1]), ALU.mult).then_inc(q_ready, 1)
                    dve.wait_ge(masked_tt, c + 1)
                    dve.tensor_tensor(tt[:, :, :], tt[:, :, :], over_pairs(eye[:, :]), ALU.add).then_inc(tt_ready, 1)
                    dve.wait_ge(br_done, c + 1)
                    for h in range(2):
                        dve.tensor_tensor(bt_bd[half[h], u, :, h, :], wide_br[half[h], :, 0, :], over_pairs(masks[half[h], m, 2]), ALU.mult)
                    dve.tensor_tensor(rt[:, u], wide_br[:, :, 1, :], over_pairs(masks[:, m, 3]), ALU.mult).then_inc(br_ready, 1)
                    dve.wait_ge(a_done, c + 1)
                    for h in range(2):
                        op = dve.tensor_tensor(a_bd[half[h], :, h, :], bank[half[h], B4], over_pairs(masks[half[h], m, 4]), ALU.mult)
                    op.then_inc(a_ready, 1)

                def level_z(c, l):
                    dve.wait_ge(z_done, c * LEVELS + (l + 1))
                    dve.tensor_copy(zt[:, :, :], bank[:, Z_BANK]).then_inc(z_ready, 1)

                def level_x(c, l):
                    dve.wait_ge(x_done, c * LEVELS + (l + 1))
                    dve.sem_inc(dve_passed, 1)
                    dve.copy_predicated(tt[:, :, :], over_pairs(doubling[:, l]), bank[:, X_BANK]).then_inc(tt_ready, 1)

                def advance_w(c):
                    dve.wait_ge(w_done, c + 3)
                    dve.tensor_copy(ws[:, :, :], bank[:, W_BANK]).then_inc(w_ready, 1)

                def advance_u(c):
                    dve.wait_ge(u_done, c + 3)
                    dve.tensor_copy(us[:, :, :], bank[:, W_BANK]).then_inc(u_ready, 1)

                def advance_state(c):
                    dve.wait_ge(s_done, c + 3)
                    dve.tensor_tensor(grown[:, :, :], bank[:, S_BANK], state[:, :, :], ALU.add).then_inc(grown_ready, 1)
                    dve.wait_ge(grown_ready, c + 1)
                    dve.wait_ge(state_bd_ready, c + 1)
                    dve.tensor_tensor(state[:, :, :], grown[:, :, :], g.lam_p[:, :, ds(c, 1)].to_broadcast([P, NPAIR, HD]),
                                      ALU.mult).then_inc(state_ready, 1)

                def ahead(c, u, m=0, advance=None):
                    def back(step):
                        if advance is not None:
                            step(advance)
                    back(advance_w)
                    products(c, u, m)
                    back(advance_u)
                    level_z(c, 0)
                    level_x(c, 0)
                    back(advance_state)
                    for l in range(1, LEVELS):
                        level_z(c, l)
                        level_x(c, l)

                ahead(0, 0)
                with dve.Fori(0, NPC // 2 - 1) as i:
                    ahead(i * 2 + 1, 1, 0, i * 2)
                    ahead(i * 2 + 2, 0, 0, i * 2 + 1)
                ahead(NPC - 1, 1, 0, NPC - 2)
                ahead(NPC, 0, 1, NPC - 1)

                c = NPC
                by_seq = seq[:, :].unsqueeze(2).to_broadcast([P, DB, HD])
                dve.sem_inc(masked, 1)
                dve.sem_inc(cross_picked, 1)
                for n, out in enumerate((ws, read_s)):
                    for a in range(NPAIR):
                        k = n * NPAIR + a
                        dve.wait_ge(cross_done, k + 1)
                        dve.wait_ge(cross_picked, k + 1)
                        dve.tensor_tensor(picked[:, :, :], bank[:, W_BANK], by_seq, ALU.mult).then_inc(masked, 1)
                        dve.wait_ge(masked, k + 2)
                        dve.tensor_reduce(out[:, a, :], picked[:, :, :].rearrange("p b v -> p v b"), AX.X, ALU.add).then_inc(cross_picked, 1)
                dve.wait_ge(cross_picked, 2 * NPAIR + 1)
                dve.wait_ge(w_done, c + 3)
                dve.tensor_tensor(ws[:, :, :], bank[:, W_BANK], ws[:, :, :], ALU.add).then_inc(w_ready, 1)
                advance_u(c)
                dve.sem_inc(bv_ready, 1)
                dve.wait_ge(u_ready, c + 2)
                dve.wait_ge(y_done, c + 3)
                zf = z[:, 0].rearrange("p i a t -> p (i a t)")
                for a in range(NPAIR):
                    if a:
                        dve.wait_ge(s_done, NPC + 2 + a)
                    for j, x in enumerate((vt[:, 0, a, :], us[:, a, :])):
                        dve.tensor_tensor(zf[:, j * DB * HD:(j + 1) * DB * HD].rearrange("p (b v) -> p b v", b=DB),
                                          x.unsqueeze(1).to_broadcast([P, DB, HD]), by_seq, ALU.mult).then_inc(cross_read, 1)
                    dve.wait_ge(s_done, NPC + 3 + a)
                    dve.tensor_tensor(picked[:, :, :], bank[:, S_BANK], states_s[:, a], ALU.add).then_inc(grown_ready, 1)
                    dve.wait_ge(grown_ready, NPC + a + 1)
                    dve.tensor_tensor(states_s[:, a], picked[:, :, :],
                                      g.lam_s[:, a, :].unsqueeze(2).to_broadcast([P, DB, HD]), ALU.mult).then_inc(bv_ready, 1)


def finish_mixing(nc, g):
    with Phase(nc, "finish") as ph:
        buf = {n: ph.sb(n, [P, 2, T]) for n in ("y", "bonus", "gate")}
        sq = ph.sb("sq", [P, T])
        rstd = ph.sb("rstd", [P, T])
        heads = ph.sb("heads", [P, P])
        means = ph.sb("means", [P, P])
        par = ph.sb("par", [P, 4, NPAIR])
        pp = ph.sb("pp", [P, 2])
        eps = ph.sb("eps", [P, 2])
        bank = ph.psum("bank", [P, SEG, 512])
        loaded = [ph.sem("loaded0"), ph.sem("loaded1")]
        par_loaded, consts_set, pp_ready, mean_done, centred, squared, var_done, ln_ready, rstd_ready, scaled, biased, \
            mixed_ready, conv_mean, conv_centred, conv_squared, conv_var, conv_ln, conv_rstd, conv_scaled, conv_sig, \
            conv_ready = (
                ph.sem(n) for n in (
                    "par_loaded", "consts_set", "pp_ready", "mean_done", "centred", "squared", "var_done", "ln_ready",
                    "rstd_ready", "scaled", "biased", "mixed_ready", "conv_mean", "conv_centred", "conv_squared",
                    "conv_var", "conv_ln", "conv_rstd", "conv_scaled", "conv_sig", "conv_ready"))
        seg = [slice(s * SW, (s + 1) * SW) for s in range(SEG)]
        y, bonus, gate = buf["y"], buf["bonus"], buf["gate"]

        with ph.block() as block:
            @block.sync
            def _(sp):
                sp.dma_start(par[:, :, :], g.norm_par).then_inc(par_loaded, 16)
                with sp.Fori(0, NPAIR // 2) as i:
                    for u in range(2):
                        sp.wait_ge(mixed_ready, i * 2 + (u + 1))
                        for x, src in ((y, g.y), (bonus, g.bonus), (gate, g.go)):
                            sp.dma_start(x[:, u], src[ds(i * 2 + u, 1)].rearrange("a p t -> p (a t)")).then_inc(loaded[u], 16)

            @block.tensor
            def _(pe):
                pe.wait_ge(consts_set, 5)
                with pe.Fori(0, NPAIR // 2) as i:
                    for u in range(2):
                        p = i * 2 + u
                        pe.wait_ge(loaded[u], i * 48 + 48)
                        pe.wait_ge(ln_ready, p + 1)
                        for s in range(SEG):
                            mm = pe.matmul(bank[:, s, 0:SW], heads[:, :], y[:, u, seg[s]], start=True, stop=True)
                        mm.then_inc(mean_done, 1)
                        pe.wait_ge(squared, p + 1)
                        for s in range(SEG):
                            mm = pe.matmul(bank[:, s, 0:SW], heads[:, :], sq[:, seg[s]], start=True, stop=True)
                        mm.then_inc(var_done, 1)
                pe.wait_ge(ln_ready, NPAIR + 1)
                for s in range(SEG):
                    for b in range(CB):
                        mm = pe.matmul(bank[:, s, 0:SW], means[:, :], g.conv[:, b, seg[s]], start=b == 0, stop=b == CB - 1)
                mm.then_inc(conv_mean, 1)
                for s in range(SEG):
                    for b in range(CB):
                        pe.wait_ge(conv_squared, s * CB + b + 1)
                        pe.matmul(bank[:, s, 0:SW], means[:, :], sq[:, (b % 2) * SW:(b % 2 + 1) * SW],
                                  start=b == 0, stop=b == CB - 1).then_inc(conv_var, 1)

            @block.scalar
            def _(act):
                act.sem_inc(ln_ready, 1)
                act.wait_ge(consts_set, 5)
                with act.Fori(0, NPAIR // 2) as i:
                    for u in range(2):
                        p = i * 2 + u
                        act.wait_ge(centred, p + 1)
                        act.activation(sq[:, :], y[:, u], ACT.Square).then_inc(squared, 1)
                        act.wait_ge(var_done, p + 1)
                        act.wait_ge(scaled, p + 1)
                        act.activation(rstd[:, :].rearrange("p (s n) -> p s n", s=SEG), bank[:, :, 0:SW], ACT.Ln,
                                       bias=eps[:, 0:1]).then_inc(ln_ready, 1)
                        act.wait_ge(ln_ready, p + 2)
                        act.activation(rstd[:, :], rstd[:, :], ACT.Exp, scale=-0.5).then_inc(rstd_ready, 1)
                act.wait_ge(conv_centred, 1)
                for s in range(SEG):
                    for b in range(CB):
                        if s * CB + b >= 2:
                            act.wait_ge(conv_var, s * CB + b - 1)
                        act.activation(sq[:, (b % 2) * SW:(b % 2 + 1) * SW], g.conv[:, b, seg[s]], ACT.Square).then_inc(conv_squared, 1)
                act.wait_ge(conv_var, SEG * CB)
                act.wait_ge(scaled, NPAIR + 1)
                act.activation(rstd[:, :].rearrange("p (s n) -> p s n", s=SEG), bank[:, :, 0:SW], ACT.Ln,
                               bias=eps[:, 1:2]).then_inc(conv_ln, 1)
                act.wait_ge(conv_ln, 1)
                act.activation(rstd[:, :], rstd[:, :], ACT.Exp, scale=-0.5).then_inc(conv_rstd, 1)
                for b in range(CB):
                    act.wait_ge(conv_scaled, b + 1)
                    if b:
                        act.wait_ge(conv_ready, b)
                    act.activation(sq[:, :], g.conv[:, b, :], ACT.Sigmoid, bias=par[:, 3, b:b + 1]).then_inc(conv_sig, 1)

            @block.vector
            def _(dve):
                dve.memset(means[:, :], 1.0 / CW).then_inc(consts_set, 1)
                dve.memset(heads[:, :], 0.0).then_inc(consts_set, 1)
                dve.memset(eps[:, 0:1], GN_EPS)
                dve.memset(eps[:, 1:2], LN_EPS).then_inc(consts_set, 1)
                dve.wait_ge(consts_set, 3)
                for h in range(2):
                    dve.memset(heads[h * HD:(h + 1) * HD, h * HD:(h + 1) * HD], 1.0 / HD).then_inc(consts_set, 1)
                dve.sem_inc(mixed_ready, 2)
                dve.sem_inc(scaled, 1)
                dve.wait_ge(par_loaded, 16)
                with dve.Fori(0, NPAIR // 2) as i:
                    for u in range(2):
                        p = i * 2 + u
                        yu = y[:, u]
                        dve.tensor_copy(pp[:, :], par[:, 0:2, ds(p, 1)].rearrange("p n a -> p (n a)")).then_inc(pp_ready, 1)
                        dve.wait_ge(mean_done, p + 1)
                        dve.wait_ge(loaded[u], i * 48 + 48)
                        dve.tensor_tensor(yu.rearrange("p (s n) -> p s n", s=SEG), yu.rearrange("p (s n) -> p s n", s=SEG),
                                          bank[:, :, 0:SW], ALU.subtract).then_inc(centred, 1)
                        dve.wait_ge(rstd_ready, p + 1)
                        dve.wait_ge(pp_ready, p + 1)
                        dve.scalar_tensor_tensor(yu, yu, pp[:, 0:1], rstd[:, :], ALU.mult, ALU.mult).then_inc(scaled, 1)
                        dve.wait_ge(scaled, p + 2)
                        dve.scalar_tensor_tensor(yu, yu, pp[:, 1:2], bonus[:, u], ALU.add, ALU.add).then_inc(biased, 1)
                        dve.wait_ge(biased, p + 1)
                        dve.tensor_tensor(g.mixed[:, ds(p, 1), :].rearrange("p a t -> p (a t)"), yu, gate[:, u], ALU.mult).then_inc(mixed_ready, 1)
                dve.wait_ge(conv_mean, 1)
                for b in range(CB):
                    x = g.conv[:, b, :].rearrange("p (s n) -> p s n", s=SEG)
                    op = dve.tensor_tensor(x, x, bank[:, :, 0:SW], ALU.subtract)
                op.then_inc(conv_centred, 1)
                dve.wait_ge(conv_rstd, 1)
                for b in range(CB):
                    dve.scalar_tensor_tensor(g.conv[:, b, :], g.conv[:, b, :], par[:, 2, b:b + 1], rstd[:, :],
                                             ALU.mult, ALU.mult).then_inc(conv_scaled, 1)
                for b in range(CB):
                    dve.wait_ge(conv_sig, b + 1)
                    dve.scalar_tensor_tensor(g.conv[:, b, :], g.conv[:, b, :], par[:, 3, b:b + 1], sq[:, :],
                                             ALU.add, ALU.mult).then_inc(conv_ready, 1)


def mix_branches(nc, g):
    with Phase(nc, "branch") as ph:
        w = ph.sb("w", [P, 2, KC + CB, P])
        gate = ph.sb("gate", [P, 2, 2, T])
        m = ph.sb("m", [P, 2, NT * P])
        part = ph.sb("part", [P, 2, QW])
        bias = ph.sb("bias", [P, KC])
        bb = ph.sb("bb", [P, 2])
        bank = ph.psum("bank", [P, 2, 2, 512])
        w_loaded = [ph.sem("w_loaded0"), ph.sem("w_loaded1")]
        gate_loaded = [ph.sem("gate_loaded0"), ph.sem("gate_loaded1")]
        bias_loaded, bank_ready, bank_free, bb_ready, gated_ready, m_ready, m_free = (
            ph.sem(n) for n in ("bias_loaded", "bank_ready", "bank_free", "bb_ready", "gated_ready",
                                "m_ready", "m_free"))
        m_stored = ph.pool_dma_sem("m_stored")

        with ph.block() as block:
            @block.sync
            def _(sp):
                sp.dma_start(bias[:, :], g.conv_out_b).then_inc(bias_loaded, 16)
                with sp.Fori(0, KC // 2) as i:
                    for u in range(2):
                        cb = i * 2 + u
                        sp.wait_ge(m_ready, cb + 1)
                        sp.dma_start(w[:, u], g.w_branch[ds(cb, 1)].rearrange("a p k c -> p (a k) c")).then_inc(w_loaded[u], 16)
                        for n in range(2):
                            sp.dma_start(gate[:, u, n], g.gates[ds(cb + n * KC, 1)].rearrange("a p t -> p (a t)")).then_inc(gate_loaded[u], 16)

            @block.gpsimd
            def _(pool):
                with pool.Fori(0, KC // 2) as i:
                    for u in range(2):
                        cb = i * 2 + u
                        pool.wait_ge(m_ready, cb + 3)
                        pool.dma_start(g.m[ds(cb, 1)].rearrange("a p t -> p (a t)"), m[:, u]).then_inc(m_stored, 16)
                        pool.wait_ge(m_stored, cb * 16 + 16)
                        pool.sem_inc(m_free, 1)

            @block.tensor
            def _(pe):
                with pe.Fori(0, KC // 2) as i:
                    for u in range(2):
                        cb = i * 2 + u
                        pe.wait_ge(w_loaded[u], i * 16 + 16)
                        for q in range(Q):
                            n = min(QW, T - q * QW)
                            k = cb * Q + q
                            pe.wait_ge(bank_free, k + 1)
                            for src, b, k0, kn in ((g.mixed, 0, 0, KC), (g.conv, 1, KC, CB)):
                                for kc in range(kn):
                                    mm = pe.matmul(bank[:, b, (q + u) % 2, 0:n], w[:, u, k0 + kc, :], src[:, kc, q * QW:q * QW + n],
                                                   start=kc == 0, stop=kc == kn - 1)
                            mm.then_inc(bank_ready, 1)

            @block.vector
            def _(dve):
                dve.sem_inc(bank_free, 2)
                dve.sem_inc(m_ready, 2)
                dve.sem_inc(m_free, 2)
                dve.memset(m[:, :, T:NT * P], 0.0)
                dve.wait_ge(bias_loaded, 16)
                with dve.Fori(0, KC // 2) as i:
                    for u in range(2):
                        cb = i * 2 + u
                        dve.tensor_copy(bb[:, u:u + 1], bias[:, ds(cb, 1)]).then_inc(bb_ready, 1)
                        dve.wait_ge(bb_ready, cb + 1)
                        dve.wait_ge(gate_loaded[u], i * 32 + 32)
                        dve.wait_ge(m_free, cb + 1)
                        for q in range(Q):
                            n = min(QW, T - q * QW)
                            k = cb * Q + q
                            cols = slice(q * QW, q * QW + n)
                            dve.wait_ge(bank_ready, k + 1)
                            dve.scalar_tensor_tensor(part[:, 0, 0:n], bank[:, 1, (q + u) % 2, 0:n], bb[:, u:u + 1],
                                                     gate[:, u, 0, cols], ALU.add, ALU.mult)
                            dve.tensor_tensor(part[:, 1, 0:n], bank[:, 0, (q + u) % 2, 0:n], gate[:, u, 1, cols], ALU.mult).then_inc(bank_free, 1)
                            dve.wait_ge(bank_free, k + 3)
                            dve.tensor_tensor(m[:, u, cols], part[:, 0, 0:n], part[:, 1, 0:n], ALU.add).then_inc(gated_ready, 1)
                            dve.wait_ge(gated_ready, k + 1)
                        dve.sem_inc(m_ready, 1)


def route(nc, g):
    with Phase(nc, "route") as ph:
        w_o = ph.sb("w_o", [P, KC, D])
        rw = ph.sb("rw", [P, KC, NG + NE])
        rb = ph.sb("rb", [P, NG + NE])
        gain = ph.sb("gain", [P, D])
        ident = ph.sb("ident", [P, P])
        earlier = ph.sb("earlier", [P, P])
        ones = ph.sb("ones", [P, P])
        m = ph.sb("m", [P, 2, KC, P])
        x = ph.sb("x", [P, 2, D])
        x2 = ph.sb("x2", [P, 2, D])
        h = ph.sb("h", [P, 2, D])
        hT = ph.sb("hT", [P, KC, P])
        junk = ph.sb("junk", [P, D])
        ss, ms, lms, rstd, nmax, esum, g_one = (ph.sb(n, [P, 1]) for n in (
            "ss", "ms", "lms", "rstd", "nmax", "esum", "g_one"))
        logits = ph.sb("logits", [P, NG + NE])
        glog = ph.sb("glog", [P, 8])
        top, etop, e_exp = (ph.sb(n, [P, 8]) for n in ("top", "etop", "e_exp"))
        gexp = ph.sb("gexp", [P, NG])
        gidx, eidx = (ph.sb(n, [P, 8], U32) for n in ("gidx", "eidx"))
        gid = ph.sb("gid", [P, 1])
        ghot = ph.sb("ghot", [P, NG])
        chosen = ph.sb("chosen", [P, EPG])
        ids = ph.sb("ids", [P, NE])
        hot = ph.sb("hot", [P, 2, NE])
        both = ph.sb("both", [P, NE])
        base = ph.sb("base", [P, NE])
        rank = ph.sb("rank", [P, NE])
        at = ph.sb("at", [P, 2, NE])
        valid = ph.sb("valid", [P, 1])
        expert = ph.sb("expert", [P, NT, 2])
        ranks = ph.sb("ranks", [P, NT, 2])
        dest = ph.sb("dest", [P, NT, 2])
        allhot = ph.sb("allhot", [P, NT * 2, NE])
        count_i = ph.sb("count_i", [P, NE], I32)
        padded, ends, starts, zeros = (ph.sb(n, [P, NE]) for n in ("padded", "ends", "starts", "zeros"))
        blocks = ph.sb("blocks", [P, NBLK])
        filled = ph.sb("filled", [P, NBLK, NE])
        block_of = ph.sb("block_of", [P, NBLK])
        token = ph.sb("token", [P, NT], I32)
        nothing = ph.sb("nothing", [P, NBLK + 1], I32)
        spare = ph.sb("spare", [P, 2])
        bank = ph.psum("bank", [P, 8, 512])
        m_loaded, x_loaded, x2_stored, h_stored = ([ph.sem(f"{n}{u}") for u in range(2)] for n in
                                                   ("m_loaded", "x_loaded", "x2_stored", "h_stored"))
        consts_loaded, consts_set, out_done, x2_ready, h_ready, squared, ln_ready, rstd_ready, turned, hT_ready, \
            logits_done, counts_done, gexp_ready, eexp_ready, routed, tile_done, dest_ready, nothing_set, \
            ms_ready, nmax_ready, e_diff_ready, hot_ready, valid_set = (
                ph.sem(n) for n in (
                    "consts_loaded", "consts_set", "out_done", "x2_ready", "h_ready", "squared",
                    "ln_ready", "rstd_ready", "turned", "hT_ready", "logits_done", "counts_done", "gexp_ready",
                    "eexp_ready", "routed", "tile_done", "dest_ready", "nothing_set",
                    "ms_ready", "nmax_ready", "e_diff_ready", "hot_ready", "valid_set"))
        LINKS = 22
        NCONST = 6
        table_cleared, scattered, ids_stored = (ph.pool_dma_sem(n) for n in ("table_cleared", "scattered", "ids_stored"))
        passed = ph.sem("passed")

        with ph.block() as block:
            @block.sync
            def _(sp):
                for dst, src in ((w_o, g.w_o), (rw, g.router_w), (ident, g.ident), (earlier, g.earlier)):
                    sp.dma_start(dst[:], src).then_inc(consts_loaded, 16)
                sp.dma_start(rb[:, :], g.router_b.to_broadcast([P, NG + NE])).then_inc(consts_loaded, 16)
                sp.dma_start(gain[:, :], g.norm2.to_broadcast([P, D])).then_inc(consts_loaded, 16)
                for s in (*x2_stored, *h_stored):
                    sp.sem_inc(s, 16)

                def load(t, u):
                    sp.wait_ge(x2_ready, t + 1)
                    sp.dma_start(m[:, u], g.m[:, :, ds(t * P, P)].rearrange("k p t -> p k t")).then_inc(m_loaded[u], 16)
                    sp.dma_start(x[:, u], g.x[ds(t * P, P)]).then_inc(x_loaded[u], 16)

                def store(t, u):
                    sp.wait_ge(x2_ready, t + 3)
                    sp.dma_start(g.x2[ds(t * P, P)], x2[:, u]).then_inc(x2_stored[u], 16)
                    sp.wait_ge(h_ready, t + 1)
                    sp.dma_start(g.h[ds(t * P, P)], h[:, u]).then_inc(h_stored[u], 16)

                load(0, 0)
                with sp.Fori(0, NT // 2) as i:
                    for u in range(2):
                        load(i * 2 + (u + 1), 1 - u)
                        store(i * 2 + u, u)
                store(NT - 1, 0)
                for s, n in ((x2_stored, 0), (h_stored, 0)):
                    sp.wait_ge(s[0], 16 + 16 * (NT // 2 + 1))
                    sp.wait_ge(s[1], 16 + 16 * (NT // 2))

            @block.tensor
            def _(pe):
                pe.wait_ge(consts_loaded, 16 * NCONST)
                pe.wait_ge(consts_set, 1)

                def tile(t, u):
                    pe.wait_ge(m_loaded[u], t * 8 + (16 - 8 * u))
                    pe.wait_ge(x2_ready, t + 2)
                    for n in range(2):
                        for kc in range(KC):
                            mm = pe.matmul(bank[:, n], m[:, u, kc, :], w_o[:, kc, n * 512:(n + 1) * 512], start=kc == 0, stop=kc == KC - 1)
                    mm.then_inc(out_done, 1)
                    pe.wait_ge(h_ready, t + 1)
                    pe.wait_ge(hT_ready, t + 1)
                    for kc in range(KC):
                        mm = pe.transpose(bank[:, 2 + kc // 4, (kc % 4) * P:(kc % 4 + 1) * P], h[:, u, kc * P:(kc + 1) * P], ident[:, :])
                    mm.then_inc(turned, 1)
                    pe.wait_ge(hT_ready, t + 2)
                    pe.wait_ge(routed, t * LINKS + 1)
                    for kc in range(KC):
                        mm = pe.matmul(bank[:, 4, 0:NG + NE], hT[:, kc, :], rw[:, kc, :], start=kc == 0, stop=kc == KC - 1)
                    mm.then_inc(logits_done, 1)
                    pe.wait_ge(tile_done, t + 1)
                    pe.matmul(bank[:, 5, 0:NE], earlier[:, :], both[:, :], start=True, stop=True)
                    pe.matmul(bank[:, 6, 0:NE], ones[:, :], both[:, :], start=True, stop=True).then_inc(counts_done, 1)

                with pe.Fori(0, NT // 2) as i:
                    for u in range(2):
                        tile(i * 2 + u, u)
                tile(NT - 1, 0)

            @block.scalar
            def _(act):
                act.sem_inc(hT_ready, 1)

                def tile(t, u):
                    act.wait_ge(x2_ready, t + 3)
                    act.activation(junk[:, :], x2[:, u], ACT.Square, accum_out=ss[:, :]).then_inc(squared, 1)
                    act.wait_ge(ms_ready, t + 1)
                    act.activation(lms[:, :], ms[:, :], ACT.Ln).then_inc(ln_ready, 1)
                    act.wait_ge(ln_ready, t + 1)
                    act.activation(rstd[:, :], lms[:, :], ACT.Exp, scale=-0.5).then_inc(rstd_ready, 1)
                    act.wait_ge(turned, t + 1)
                    act.copy(hT[:, :, :].rearrange("p k t -> p (k t)"), bank[:, 2:4].rearrange("p b t -> p (b t)")).then_inc(hT_ready, 1)
                    act.wait_ge(nmax_ready, t + 1)
                    act.activation(gexp[:, :], logits[:, 0:NG], ACT.Exp, bias=nmax[:, :], accum_out=esum[:, :]).then_inc(gexp_ready, 1)
                    act.wait_ge(e_diff_ready, t + 1)
                    act.activation(e_exp[:, 0:1], etop[:, 2:3], ACT.Exp).then_inc(eexp_ready, 1)

                with act.Fori(0, NT // 2) as i:
                    for u in range(2):
                        tile(i * 2 + u, u)
                tile(NT - 1, 0)

            @block.gpsimd
            def _(pool):
                pool.iota(ids[:, :], [[1, NE]], base=0, channel_multiplier=0, allow_small_or_imprecise_dtypes=True)
                pool.iota(blocks[:, :], [[EB, NBLK]], base=0, channel_multiplier=0, allow_small_or_imprecise_dtypes=True)
                pool.iota(spare[:, :], [[-(T % P), 2]], base=NBLK * EB, channel_multiplier=1, allow_small_or_imprecise_dtypes=True)
                pool.iota(token[:, :], [[P, NT]], base=0, channel_multiplier=1)
                pool.memset(nothing[:, :], 0).then_inc(nothing_set, 1)
                pool.wait_ge(nothing_set, 1)
                pool.dma_start(g.row_token.rearrange("(p n) a -> p (n a)", p=P), nothing[:, :]).then_inc(table_cleared, 16)
                pool.wait_ge(table_cleared, 16)
                pool.wait_ge(dest_ready, 1)
                for t in range(NT):
                    for s in range(2):
                        pool.indirect_dma_start(g.row_token, bass.IndirectOffsetOnAxis(ap=g.dest_i[:, t, s:s + 1], axis=0),
                                                token[:, t:t + 1], None).then_inc(scattered, 16)
                pool.wait_ge(scattered, 16 * 2 * NT)
                with nc.allow_non_contiguous_dma(reason="a block's rows go over the partitions"):
                    pool.dma_start(g.row_of[:, :], g.row_token[0:NBLK * EB].rearrange("(n p) a -> p (n a)", p=P)).then_inc(ids_stored, 16)
                pool.wait_ge(ids_stored, 16)

            @block.vector
            def _(dve):
                dve.sem_inc(x2_ready, 2)
                dve.sem_inc(routed, 1)
                dve.memset(zeros[:, :], 1.0)
                dve.memset(base[:, :], 0.0)
                dve.memset(glog[:, :], -3.0e38)
                dve.memset(valid[:, :], 0.0)
                dve.memset(ones[:, :], 1.0).then_inc(consts_set, 1)
                dve.wait_ge(consts_set, 1)
                dve.memset(valid[0:T % P, :], 1.0).then_inc(valid_set, 1)
                dve.wait_ge(nothing_set, 1)
                dve.wait_ge(consts_loaded, 16 * NCONST)
                dve.wait_ge(valid_set, 1)

                def tile(t, u, partial=False):
                    n = [0]

                    def link(op, before_max=False):
                        op.then_inc(routed, 1)
                        n[0] += 1
                        dve.wait_ge(routed, t * LINKS + (n[0] + 1))
                        if before_max:
                            dve.sem_inc(passed, 1)

                    dve.wait_ge(out_done, t + 1)
                    dve.wait_ge(x_loaded[u], t * 8 + (16 - 8 * u))
                    dve.wait_ge(x2_stored[u], t * 8 + (16 - 8 * u))
                    dve.tensor_tensor(x2[:, u], bank[:, 0:2].rearrange("p b t -> p (b t)"), x[:, u], ALU.add).then_inc(x2_ready, 1)
                    dve.wait_ge(squared, t + 1)
                    dve.tensor_scalar(ms[:, :], ss[:, :], 1.0 / D, NORM_EPS, ALU.mult, ALU.add).then_inc(ms_ready, 1)
                    dve.wait_ge(rstd_ready, t + 1)
                    dve.wait_ge(h_stored[u], t * 8 + (16 - 8 * u))
                    dve.scalar_tensor_tensor(h[:, u], x2[:, u], rstd[:, :], gain[:, :], ALU.mult, ALU.mult).then_inc(h_ready, 1)
                    dve.wait_ge(logits_done, t + 1)
                    link(dve.tensor_tensor(logits[:, :], bank[:, 4, 0:NG + NE], rb[:, :], ALU.add))
                    link(dve.tensor_copy(glog[:, 0:NG], logits[:, 0:NG]), before_max=True)
                    link(dve.max(top[:, :], glog[:, :]), before_max=True)
                    link(dve.max_index(gidx[:, :], top[:, :], glog[:, :]))
                    dve.tensor_scalar(nmax[:, :], top[:, 0:1], -1.0, None, ALU.mult).then_inc(nmax_ready, 1)
                    link(dve.tensor_copy(gid[:, :], gidx[:, 0:1]))
                    link(dve.tensor_scalar(ghot[:, :], ids[:, 0:NG], gid[:, :], None, ALU.is_equal))
                    le = logits[:, NG:].rearrange("p (n e) -> p n e", n=NG)
                    link(dve.tensor_scalar(chosen[:, :], le[:, 0], ghot[:, 0:1], None, ALU.mult))
                    for k in range(1, NG):
                        link(dve.scalar_tensor_tensor(chosen[:, :], le[:, k], ghot[:, k:k + 1], chosen[:, :], ALU.mult, ALU.add), before_max=k == NG - 1)
                    link(dve.max(etop[:, :], chosen[:, :]), before_max=True)
                    link(dve.max_index(eidx[:, :], etop[:, :], chosen[:, :]))
                    link(dve.tensor_tensor(etop[:, 2:3], etop[:, 1:2], etop[:, 0:1], ALU.subtract))
                    dve.tensor_scalar(gid[:, :], gid[:, :], float(EPG), None, ALU.mult).then_inc(e_diff_ready, 1)
                    dve.wait_ge(e_diff_ready, t + 1)
                    ex = expert[:, ds(t, 1), :].rearrange("p a s -> p (a s)")
                    link(dve.tensor_copy(ex, eidx[:, 0:2]))
                    link(dve.tensor_scalar(ex, ex, gid[:, :], None, ALU.add))
                    for s in range(2):
                        dve.tensor_scalar(hot[:, s], ids[:, :], expert[:, ds(t, 1), s], None, ALU.is_equal).then_inc(hot_ready, 1)
                    dve.wait_ge(hot_ready, t * 2 + 2)
                    link(dve.tensor_tensor(both[:, :], hot[:, 0], hot[:, 1], ALU.add))
                    if partial:
                        dve.tensor_scalar(both[:, :], both[:, :], valid[:, :], None, ALU.mult).then_inc(tile_done, 1)
                    else:
                        dve.sem_inc(tile_done, 1)
                    dve.wait_ge(gexp_ready, t + 1)
                    dve.wait_ge(eexp_ready, t + 1)
                    link(dve.tensor_scalar(g_one[:, :], e_exp[:, 0:1], 1.0, None, ALU.add))
                    link(dve.tensor_tensor(esum[:, :], esum[:, :], g_one[:, :], ALU.mult))
                    gt = g.gate_of[:, ds(t, 1), :].rearrange("p a s -> p (a s)")
                    link(dve.reciprocal(gt[:, 0:1], esum[:, :]))
                    dve.tensor_tensor(gt[:, 1:2], gt[:, 0:1], e_exp[:, 0:1], ALU.mult)
                    dve.wait_ge(counts_done, t + 1)
                    link(dve.tensor_tensor(rank[:, :], bank[:, 5, 0:NE], base[:, :], ALU.add))
                    link(dve.tensor_tensor(at[:, :, :], hot[:, :, :], rank[:, :].unsqueeze(1).to_broadcast([P, 2, NE]), ALU.mult))
                    dve.tensor_reduce(ranks[:, ds(t, 1), :].rearrange("p a s -> p (a s)"), at[:, :, :], AX.X, ALU.add)
                    link(dve.tensor_tensor(base[:, :], bank[:, 6, 0:NE], base[:, :], ALU.add))
                    assert n[0] == LINKS, n[0]

                with dve.Fori(0, NT // 2) as i:
                    for u in range(2):
                        tile(i * 2 + u, u)
                tile(NT - 1, 0, partial=True)

                n = [NT * LINKS + 1]

                def link(op):
                    op.then_inc(routed, 1)
                    n[0] += 1
                    dve.wait_ge(routed, n[0])

                link(dve.tensor_scalar(count_i[:, :], base[:, :], float(EB - 1), None, ALU.add))
                link(dve.tensor_scalar(count_i[:, :], count_i[:, :], 7, 7, ALU.logical_shift_right, ALU.logical_shift_left))
                link(dve.tensor_copy(padded[:, :], count_i[:, :]))
                link(dve.tensor_tensor_scan(ends[:, :], zeros[:, :], padded[:, :], 0.0, ALU.mult, ALU.add))
                link(dve.tensor_tensor(starts[:, :], ends[:, :], padded[:, :], ALU.subtract))
                ex = expert[:, :, :].rearrange("p t s -> p (t s)")
                link(dve.tensor_tensor(allhot[:, :, :], ids[:, :].unsqueeze(1).to_broadcast([P, 2 * NT, NE]),
                                       ex.unsqueeze(2).to_broadcast([P, 2 * NT, NE]), ALU.is_equal))
                link(dve.tensor_tensor(allhot[:, :, :], allhot[:, :, :], starts[:, :].unsqueeze(1).to_broadcast([P, 2 * NT, NE]), ALU.mult))
                link(dve.tensor_reduce(dest[:, :, :].rearrange("p t s -> p (t s)"), allhot[:, :, :], AX.X, ALU.add))
                link(dve.tensor_tensor(dest[:, :, :], dest[:, :, :], ranks[:, :, :], ALU.add))
                last = dest[:, NT - 1, :]
                link(dve.tensor_tensor(last, last, spare[:, :], ALU.subtract))
                link(dve.tensor_scalar(last, last, valid[:, :], None, ALU.mult))
                link(dve.tensor_tensor(last, last, spare[:, :], ALU.add))
                link(dve.tensor_copy(g.dest_i[:, :, :], dest[:, :, :]))
                dve.sem_inc(dest_ready, 1)
                link(dve.tensor_tensor(filled[:, :, :], blocks[:, :].unsqueeze(2).to_broadcast([P, NBLK, NE]),
                                       ends[:, :].unsqueeze(1).to_broadcast([P, NBLK, NE]), ALU.is_ge))
                link(dve.tensor_reduce(block_of[:, :], filled[:, :, :], AX.X, ALU.add))
                link(dve.tensor_scalar(block_of[:, :], block_of[:, :], float(NE - 1), None, ALU.min))
                link(dve.tensor_copy(g.block_expert[:, :], block_of[:, :]))


def run_experts(nc, g):
    DEPTH = 2
    HW = 2 * DE
    with Phase(nc, "expert") as ph:
        w = ph.sb("w", [P, DEPTH, KC * HW])
        wd = ph.sb("wd", [P, DEPTH, 2 * D])
        ident = ph.sb("ident", [P, P])
        rows = ph.sb("rows", [P, DEPTH], I32)
        x = ph.sb("x", [P, DEPTH, D])
        xT = ph.sb("xT", [P, KC, P])
        sig = ph.sb("sig", [P, DE])
        act_h = ph.sb("act_h", [P, DE])
        hT = ph.sb("hT", [P, 2, P])
        out = ph.sb("out", [P, DEPTH, D])
        zero = ph.sb("zero", [P, D])
        bank = ph.psum("bank", [P, 8, 512])
        w_loaded, wd_loaded, out_stored = ([ph.sem(f"{n}{u}") for u in range(DEPTH)] for n in ("w_loaded", "wd_loaded", "out_stored"))
        ident_loaded, rows_ready, turned, xT_ready, up_done, sig_ready, gated, h_ready, h_turned, hT_ready, \
            down_done, out_ready, zero_set, half_out = (
                ph.sem(n) for n in ("ident_loaded", "rows_ready", "turned", "xT_ready", "up_done",
                                    "sig_ready", "gated", "h_ready", "h_turned", "hT_ready", "down_done", "out_ready",
                                    "zero_set", "half_out"))
        zero_stored, gathered = (ph.pool_dma_sem(n) for n in ("zero_stored", "gathered"))
        passed = ph.sem("passed")

        with ph.block() as block:
            @block.sync
            def _(sp):
                sp.dma_start(ident[:, :], g.ident).then_inc(ident_loaded, 16)
                with sp.Fori(0, NBLK // 2) as i:
                    for u in range(2):
                        b = i * 2 + u
                        e = sp.value_load(g.block_expert[0:1, ds(b, 1)], min_val=0, max_val=NE - 1)
                        sp.wait_ge(up_done, b + 1)
                        sp.dma_start(w[:, u], g.w_up[ds(e, 1)].rearrange("a p n -> p (a n)")).then_inc(w_loaded[u], 16)
                        sp.wait_ge(down_done, b + 1)
                        sp.dma_start(wd[:, u], g.w_down[ds(e, 1)].rearrange("a p n -> p (a n)")).then_inc(wd_loaded[u], 16)

            @block.gpsimd
            def _(pool):
                pool.memset(zero[:, :], 0.0).then_inc(zero_set, 1)
                pool.wait_ge(zero_set, 1)
                pool.dma_start(g.yb[NBLK * EB:], zero[:, :]).then_inc(zero_stored, 16)
                pool.wait_ge(zero_stored, 16)
                with pool.Fori(0, NBLK // 2) as i:
                    for u in range(2):
                        b = i * 2 + u
                        pool.wait_ge(turned, b + 1)
                        pool.sem_inc(passed, 1)
                        pool.tensor_copy(rows[:, u:u + 1], g.row_of[:, ds(b, 1)]).then_inc(rows_ready, 1)
                        pool.wait_ge(rows_ready, b + 1)
                        pool.sem_inc(passed, 1)
                        pool.indirect_dma_start(x[:, u], None, g.h, bass.IndirectOffsetOnAxis(ap=rows[:, u:u + 1], axis=0)).then_inc(gathered, 16)
                        pool.wait_ge(gathered, b * 16 + 16)

            @block.tensor
            def _(pe):
                for s in (turned, up_done, down_done):
                    pe.sem_inc(s, 2)
                pe.wait_ge(ident_loaded, 16)
                with pe.Fori(0, NBLK // 2) as i:
                    for u in range(2):
                        b = i * 2 + u
                        pe.wait_ge(gathered, b * 16 + 16)
                        pe.wait_ge(xT_ready, b + 1)
                        for kc in range(KC):
                            mm = pe.transpose(bank[:, kc // 4, (kc % 4) * P:(kc % 4 + 1) * P], x[:, u, kc * P:(kc + 1) * P], ident[:, :])
                        mm.then_inc(turned, 1)
                        pe.wait_ge(xT_ready, b + 2)
                        pe.wait_ge(w_loaded[u], i * 16 + 16)
                        pe.wait_ge(h_ready, b + 1)
                        for kc in range(KC):
                            mm = pe.matmul(bank[:, 2], xT[:, kc, :], w[:, u, kc * HW:(kc + 1) * HW], start=kc == 0, stop=kc == KC - 1)
                        mm.then_inc(up_done, 1)
                        pe.wait_ge(h_ready, b + 2)
                        for f in range(2):
                            mm = pe.transpose(bank[:, 3, f * P:(f + 1) * P], act_h[:, f * P:(f + 1) * P], ident[:, :])
                        mm.then_inc(h_turned, 1)
                        pe.wait_ge(hT_ready, b + 1)
                        pe.wait_ge(wd_loaded[u], i * 16 + 16)
                        pe.wait_ge(out_ready, b + 1)
                        for n in range(2):
                            for f in range(2):
                                mm = pe.matmul(bank[:, 4 + n], hT[:, f, :], wd[:, u, f * D + n * 512:f * D + (n + 1) * 512], start=f == 0, stop=f == 1)
                        mm.then_inc(down_done, 1)

            @block.scalar
            def _(act):
                act.sem_inc(out_ready, 1)
                for u in range(2):
                    act.sem_inc(out_stored[u], 16)
                with act.Fori(0, NBLK // 2) as i:
                    for u in range(2):
                        b = i * 2 + u
                        act.wait_ge(up_done, b + 3)
                        act.activation(sig[:, :], bank[:, 2, 0:DE], ACT.Sigmoid).then_inc(sig_ready, 1)
                        act.wait_ge(down_done, b + 3)
                        act.wait_ge(out_stored[u], i * 16 + 16)
                        act.copy(out[:, u], bank[:, 4:6].rearrange("p b n -> p (b n)")).then_inc(out_ready, 1)
                        act.wait_ge(out_ready, b + 2)
                        act.dma_start(g.yb[ds(b * EB, EB)], out[:, u]).then_inc(out_stored[u], 16)
                for u in range(2):
                    act.wait_ge(out_stored[u], 16 + 16 * (NBLK // 2))

            @block.vector
            def _(dve):
                dve.sem_inc(xT_ready, 1)
                dve.sem_inc(h_ready, 1)
                with dve.Fori(0, NBLK // 2) as i:
                    for u in range(2):
                        b = i * 2 + u
                        dve.wait_ge(turned, b + 3)
                        dve.wait_ge(up_done, b + 2)
                        dve.tensor_copy(xT[:, :, :].rearrange("p k t -> p (k t)"), bank[:, 0:2].rearrange("p b t -> p (b t)")).then_inc(xT_ready, 1)
                        dve.wait_ge(sig_ready, b + 1)
                        dve.tensor_tensor(sig[:, :], bank[:, 2, 0:DE], sig[:, :], ALU.mult).then_inc(gated, 1)
                        dve.wait_ge(gated, b + 1)
                        dve.tensor_tensor(act_h[:, :], bank[:, 2, DE:HW], sig[:, :], ALU.mult).then_inc(h_ready, 1)
                        dve.wait_ge(h_turned, b + 1)
                        dve.tensor_copy(hT[:, :, :].rearrange("p k t -> p (k t)"), bank[:, 3, 0:2 * P]).then_inc(hT_ready, 1)


def combine(nc, g):
    with Phase(nc, "combine") as ph:
        gain = ph.sb("gain", [P, D])
        x2 = ph.sb("x2", [P, 2, D])
        rows = ph.sb("rows", [P, 2, 2], I32)
        e0, e1 = (ph.sb(n, [P, 2, D]) for n in ("e0", "e1"))
        out = ph.sb("out", [P, 2, D])
        junk = ph.sb("junk", [P, D])
        ss, ms, lms, rstd = (ph.sb(n, [P, 1]) for n in ("ss", "ms", "lms", "rstd"))
        x2_loaded, out_stored = ([ph.sem(f"{n}{u}") for u in range(2)] for n in ("x2_loaded", "out_stored"))
        gain_loaded, rows_ready, first_added, added, squared, ms_ready, ln_ready, rstd_ready, out_ready, consts = (
            ph.sem(n) for n in ("gain_loaded", "rows_ready", "first_added", "added", "squared",
                                "ms_ready", "ln_ready", "rstd_ready", "out_ready", "consts"))
        gathered0, gathered1 = (ph.pool_dma_sem(n) for n in ("gathered0", "gathered1"))
        passed = ph.sem("passed")

        with ph.block() as block:
            def tiles(eng, tile):
                with eng.Fori(0, NT // 2) as i:
                    for u in range(2):
                        tile(i * 2 + u, u, P)
                tile(NT - 1, 0, T - (NT - 1) * P)

            @block.sync
            def _(sp):
                sp.dma_start(gain[:, :], g.norm_f.to_broadcast([P, D])).then_inc(gain_loaded, 16)
                sp.sem_inc(out_stored[0], 16)
                sp.sem_inc(out_stored[1], 16)

                def load(t, u):
                    sp.wait_ge(out_ready, t + 1)
                    sp.dma_start(x2[:, u], g.x2[ds(t * P, P)]).then_inc(x2_loaded[u], 16)

                def store(t, u, n):
                    sp.wait_ge(out_ready, t + 3)
                    sp.dma_start(g.y_out[ds(t * P, n)], out[0:n, u]).then_inc(out_stored[u], 16)

                load(0, 0)
                with sp.Fori(0, NT // 2) as i:
                    for u in range(2):
                        load(i * 2 + (u + 1), 1 - u)
                        store(i * 2 + u, u, P)
                store(NT - 1, 0, T - (NT - 1) * P)
                sp.wait_ge(out_stored[0], 16 + 16 * (NT // 2 + 1))
                sp.wait_ge(out_stored[1], 16 + 16 * (NT // 2))

            @block.gpsimd
            def _(pool):
                pool.memset(junk[:, 0:1], 0.0).then_inc(consts, 1)

                def tile(t, u, n):
                    pool.wait_ge(added, t + 1)
                    pool.sem_inc(passed, 1)
                    pool.tensor_copy(rows[:, u], g.dest_i[:, ds(t, 1), :].rearrange("p a s -> p (a s)")).then_inc(rows_ready, 1)
                    pool.wait_ge(rows_ready, t + 1)
                    pool.sem_inc(passed, 1)
                    for s, (e, done) in enumerate(((e0, gathered0), (e1, gathered1))):
                        pool.indirect_dma_start(e[:, u], None, g.yb, bass.IndirectOffsetOnAxis(ap=rows[:, u, s:s + 1], axis=0)).then_inc(done, 16)
                    pool.wait_ge(gathered0, t * 16 + 16)
                    pool.wait_ge(gathered1, t * 16 + 16)
                tiles(pool, tile)

            @block.scalar
            def _(act):
                def tile(t, u, n):
                    act.wait_ge(added, t + 3)
                    act.activation(junk[:, :], out[:, u], ACT.Square, accum_out=ss[:, :]).then_inc(squared, 1)
                    act.wait_ge(ms_ready, t + 1)
                    act.activation(lms[:, :], ms[:, :], ACT.Ln).then_inc(ln_ready, 1)
                    act.wait_ge(ln_ready, t + 1)
                    act.activation(rstd[:, :], lms[:, :], ACT.Exp, scale=-0.5).then_inc(rstd_ready, 1)
                act.wait_ge(consts, 1)
                tiles(act, tile)

            @block.vector
            def _(dve):
                dve.sem_inc(added, 2)
                dve.sem_inc(out_ready, 2)
                dve.wait_ge(gain_loaded, 16)

                def tile(t, u, n):
                    dve.wait_ge(x2_loaded[u], t * 8 + (16 - 8 * u))
                    dve.wait_ge(gathered0, t * 16 + 16)
                    dve.wait_ge(out_stored[u], t * 8 + (16 - 8 * u))
                    dve.scalar_tensor_tensor(out[:, u], e0[:, u], g.gate_of[:, ds(t, 1), 0], x2[:, u], ALU.mult, ALU.add).then_inc(first_added, 1)
                    dve.wait_ge(gathered1, t * 16 + 16)
                    dve.wait_ge(first_added, t + 1)
                    dve.scalar_tensor_tensor(out[:, u], e1[:, u], g.gate_of[:, ds(t, 1), 1], out[:, u], ALU.mult, ALU.add).then_inc(added, 1)
                    dve.wait_ge(squared, t + 1)
                    dve.tensor_scalar(ms[:, :], ss[:, :], 1.0 / D, NORM_EPS, ALU.mult, ALU.add).then_inc(ms_ready, 1)
                    dve.wait_ge(rstd_ready, t + 1)
                    dve.scalar_tensor_tensor(out[:, u], out[:, u], rstd[:, :], gain[:, :], ALU.mult, ALU.mult).then_inc(out_ready, 1)
                tiles(dve, tile)


PHASES = [norm_inputs, project_glu, project_rwkv, project_gates, prepare_recurrence, recurrence, finish_mixing,
          mix_branches, route, run_experts, combine]


def hybrid_step(nc, ins, outs):
    g = Tensors(ins, outs)

    def scratch(name, shape, dt=F32):
        return nc.dram_tensor(name, shape, dt, kind="Internal").ap()

    g.xm = scratch("xm", [RWB, P, T])
    g.gates = scratch("gates", [2 * KC, P, T])
    g.zc = scratch("zc", [NCH, P, 4, NPAIR, C])
    g.y = scratch("y", [NPAIR, P, T])
    g.go = scratch("go", [NPAIR, P, T])
    g.bonus = scratch("bonus", [NPAIR, P, T])
    g.m = scratch("m", [KC, P, NT * P])
    g.x2 = scratch("x2", [NT * P, D])
    g.h = scratch("h", [NT * P, D])
    g.row_token = scratch("row_token", [(NBLK + 1) * EB, 1], I32)
    g.yb = scratch("yb", [(NBLK + 1) * EB, D])
    with ExitStack() as late:
        def kept(ctx, name, shape, dt=F32):
            return ctx.enter_context(nc.sbuf_tensor(name, shape, dt))

        g.row_of = kept(late, "row_of", [P, NBLK], I32)
        g.block_expert = kept(late, "block_expert", [P, NBLK], I32)
        g.dest_i = kept(late, "dest_i", [P, NT, 2], I32)
        g.gate_of = kept(late, "gate_of", [P, NT, 2])
        with ExitStack() as ctx:
            g.conv = kept(ctx, "conv", [P, CB, T])
            with ExitStack() as early:
                g.glu_p = kept(early, "glu_p", [P, CB, HIST + NP])
                g.glu_s = kept(early, "glu_s", [P, CB, DB, HIST + DS])
                g.hist_s = kept(early, "hist_s", [P, CB, DB, HIST])
                g.u = kept(early, "u", [P, KC, TC])
                for phase in PHASES[:4]:
                    phase(nc, g)
            g.lam_p = kept(ctx, "lam_p", [P, NPAIR, NCH - 1])
            g.lam_s = kept(ctx, "lam_s", [P, NPAIR, DB])
            for phase in PHASES[4:6]:
                phase(nc, g)
            g.mixed = kept(ctx, "mixed", [P, NPAIR, T])
            for phase in PHASES[6:8]:
                phase(nc, g)
        for phase in PHASES[8:]:
            phase(nc, g)


def kernel(**inputs):
    import numpy as np
    import concourse.bacc as bacc
    from concourse.bass_utils import run_bass_kernel_spmd

    f = {k: np.asarray(v) for k, v in inputs.items()}
    f = {k: v[0] if k not in ("x_prompt", "x_sample", "final_norm_g") else v for k, v in f.items()}

    def by_channel(v):
        return np.ascontiguousarray(v.reshape(-1, P).T)

    x = np.concatenate([f["x_prompt"][0], f["x_sample"].reshape(NS, D)])
    arrays = {
        "xT": np.ascontiguousarray(np.concatenate([x, f["state_shift"]]).T).reshape(KC, P, TC),
        "norm1": by_channel(f["norm1_g"]),
        "w_in": np.ascontiguousarray(f["w_in"].reshape(KC, P, -1, P).transpose(2, 1, 0, 3)),
        "state_conv": np.ascontiguousarray(f["state_conv"].reshape(DB, HIST, CB, P).transpose(3, 2, 0, 1)),
        "conv_w": np.ascontiguousarray(f["conv_dw_w"].reshape(CK, CB, P).transpose(2, 1, 0)),
        "conv_b": by_channel(f["conv_dw_b"]),
        "mu": by_channel(f["rwkv_mu"]),
        "rwkv_par": np.ascontiguousarray(np.stack(
            [by_channel(f[n]) for n in ("rwkv_w0", "rwkv_a0", "rwkv_k_k", "rwkv_k_a", "rwkv_k_a", "rwkv_r_k")], axis=2)),
        "lora": np.ascontiguousarray(np.stack([
            np.concatenate([f["rwkv_w2"], np.zeros_like(f["rwkv_w2"])]),
            np.concatenate([np.zeros_like(f["rwkv_a2"]), f["rwkv_a2"]]), f["rwkv_g2"]])
            .reshape(3, P, NPAIR, P).transpose(2, 1, 0, 3)),
    }
    arrays |= {
        "norm_par": np.ascontiguousarray(np.stack(
            [by_channel(f["rwkv_gn_g"]), by_channel(f["rwkv_gn_b"]),
             *(np.pad(by_channel(f[n]), ((0, 0), (0, NPAIR - CB))) for n in ("conv_ln_g", "conv_ln_b"))], axis=1)),
        "w_branch": np.ascontiguousarray(np.concatenate([f["rwkv_out_w"], f["conv_out_w"]])
                                         .reshape(KC + CB, P, KC, P).transpose(2, 1, 0, 3)),
        "conv_out_b": by_channel(f["conv_out_b"]),
        "w_o": np.ascontiguousarray(f["w_o"].reshape(KC, P, D).transpose(1, 0, 2)),
        "router_w": np.ascontiguousarray(np.concatenate([f["router_group_w"], f["router_expert_w"]], axis=1)
                                         .reshape(KC, P, NG + NE).transpose(1, 0, 2)),
        "router_b": np.concatenate([f["router_group_b"], f["router_expert_b"]])[None],
        "norm2": f["norm2_g"][None], "norm_f": f["final_norm_g"][None],
        "x": np.concatenate([x, np.zeros((NT * P - T, D), x.dtype)]),
        "w_up": np.ascontiguousarray(np.concatenate([f["expert_w_gate"], f["expert_w_up"]], axis=2)
                                     .reshape(NE, KC, P, 2 * DE).transpose(0, 2, 1, 3)).reshape(NE, P, KC * 2 * DE),
        "w_down": np.ascontiguousarray(f["expert_w_down"].reshape(NE, 2, P, D).transpose(0, 2, 1, 3)).reshape(NE, P, 2 * D),
        "ident": np.eye(P, dtype=np.float32), "earlier": np.triu(np.ones((P, P), np.float32), 1),
    }
    j, t = np.arange(C)[:, None], np.arange(C)[None, :]
    same = j // DS == t // DS
    pair_step = (j % 2 == 0) & (t == j + 1)
    both = lambda m: np.concatenate([m, m]).astype(np.float32)
    arrays |= {
        "masks": np.stack([np.stack([both(-1.0 * (pair_step & s)), both(-1.0 * ((j <= t) & s)), both((j < t) & s),
                                     both((j <= t) & s), both(-1.0 * ((t < j) & s))], axis=1)
                           for s in (same | True, same)], axis=1),
        "doubling": np.stack([both((j // (2 * m) == t // (2 * m)) & (j % (2 * m) < m) & (t % (2 * m) >= m))
                              for m in (2, 4, 8, 16, 32)], axis=1).astype(np.int32),
        "eye": both(j == t),
        "seq": both(j // DS == np.arange(DB)[None, :]),
        "state_s": np.ascontiguousarray(f["state_wkv"].reshape(DB, NPAIR, 2, HD, HD).transpose(2, 4, 1, 0, 3)
                                        .reshape(P, NPAIR, DB, HD)),
    }
    shapes = {
        "y_out": (T, D),
        "wkv_p": (P, NPAIR, HD), "wkv_s": (P, NPAIR, DB, HD),
        "shift_p": (P, KC, 1), "shift_s": (P, KC, DB), "conv_p": (P, CB, HIST), "conv_s": (P, CB, DB, HIST),
    }
    nc = bacc.Bacc("TRN2", target_bir_lowering=False, num_devices=1)
    ins = {k: nc.dram_tensor(f"in_{k}", a.shape, mybir.dt.from_np(a.dtype), kind="ExternalInput").ap()
           for k, a in arrays.items()}
    outs = {k: nc.dram_tensor(f"out_{k}", s, F32, kind="ExternalOutput").ap() for k, s in shapes.items()}
    hybrid_step(nc, ins, outs)
    r = run_bass_kernel_spmd(nc, [{f"in_{k}": a for k, a in arrays.items()}], core_ids=[0])
    o = {k: np.asarray(r.results[0][f"out_{k}"]) for k in shapes}

    def channels_last(v):
        return np.ascontiguousarray(np.moveaxis(v, (1, 0), (-2, -1))).reshape(*v.shape[2:], -1)

    wkv_p = o["wkv_p"].reshape(2, HD, NPAIR, HD).transpose(2, 0, 3, 1).reshape(1, 1, 2 * NPAIR, HD, HD)
    wkv_s = o["wkv_s"].reshape(2, HD, NPAIR, DB, HD).transpose(3, 2, 0, 4, 1).reshape(1, DB, 2 * NPAIR, HD, HD)
    return (o["y_out"][None, :NP], o["y_out"][NP:].reshape(DB, DS, D),
            channels_last(o["conv_p"])[None, None], channels_last(o["shift_p"])[None], np.ascontiguousarray(wkv_p),
            channels_last(o["conv_s"])[None], channels_last(o["shift_s"])[None], np.ascontiguousarray(wkv_s))
```

```python
from contextlib import ExitStack
from math import exp

import concourse.bass as bass
from concourse import mybir

P = 128
D = 1024
KC = D // P
NP = 2048
DB, DS = 8, 8
NS = DB * DS
T = NP + NS
TC = T + DB
CW = D // 2
CB = CW // P
CK = 31
HIST = CK - 1
HD = 64
NPAIR = D // P
C = 64
NCH = T // C
RWB = 26
Q, QW = 5, TC // 5
SEG, SW = 6, T // 6
NG, NE, EPG = 4, 32, 8
DE = 256
EB = 128
NBLK = (2 * T + NE * (EB - 1)) // EB
NT = (T + P - 1) // P

ALU = mybir.AluOpType
ACT = mybir.ActivationFunctionType
AX = mybir.AxisListType
F32 = mybir.dt.float32
F32R = mybir.dt.float32r
I32 = mybir.dt.int32
U32 = mybir.dt.uint32
NORM_EPS, LN_EPS, GN_EPS = 1e-6, 1e-5, 64e-5
ds = bass.ds


class Tensors:

    def __init__(self, ins, outs):
        self.xT, self.norm1, self.w_in, self.state_conv, self.conv_w, self.conv_b = (ins[n] for n in ("xT", "norm1", "w_in", "state_conv", "conv_w", "conv_b"))
        self.mu, self.rwkv_par, self.lora, self.norm_par, self.w_branch, self.conv_out_b = (ins[n] for n in ("mu", "rwkv_par", "lora", "norm_par", "w_branch", "conv_out_b"))
        self.w_o, self.router_w, self.router_b, self.norm2, self.x, self.w_up = (ins[n] for n in ("w_o", "router_w", "router_b", "norm2", "x", "w_up"))
        self.w_down, self.ident, self.masks, self.doubling, self.eye, self.seq = (ins[n] for n in ("w_down", "ident", "masks", "doubling", "eye", "seq"))
        self.state_s, self.norm_f, self.earlier = (ins[n] for n in ("state_s", "norm_f", "earlier"))
        self.y_out, self.wkv_p, self.wkv_s, self.shift_p, self.shift_s, self.conv_p = (outs[n] for n in ("y_out", "wkv_p", "wkv_s", "shift_p", "shift_s", "conv_p"))
        self.conv_s = outs["conv_s"]


class Phase:

    def __init__(self, nc, name):
        self.nc, self.name, self.ctx, self.sems = nc, name, ExitStack(), []

    def __enter__(self):
        return self

    def __exit__(self, *a):
        for s in self.sems:
            self.nc.gpsimd.sem_clear(s)
        self.ctx.close()

    def sb(self, name, shape, dt=F32):
        return self.ctx.enter_context(self.nc.sbuf_tensor(f"{self.name}_{name}", shape, dt))

    def psum(self, name, shape, dt=F32):
        return self.ctx.enter_context(self.nc.psum_tensor(f"{self.name}_{name}", shape, dt))

    def sem(self, name):
        self.sems.append(self.ctx.enter_context(self.nc.semaphore(f"{self.name}_{name}")))
        return self.sems[-1]

    def pool_dma_sem(self, name):
        return self.nc.alloc_semaphore(f"{self.name}_{name}")

    def block(self):
        return self.nc.Block()


def norm_inputs(nc, g):
    with Phase(nc, "norm") as ph:
        ones = ph.sb("ones", [P, P])
        raw_shift = ph.sb("raw_shift", [P, KC, DB])
        sq = ph.sb("sq", [P, 2, KC, SW])
        ms = ph.sb("ms", [P, 2, SW])
        rms = ph.sb("rms", [P, 2, SW])
        rstd = ph.sb("rstd", [P, 2, SW])
        gain = ph.sb("gain", [P, KC])
        total = ph.psum("total", [P, 2, 512])
        x_loaded, gain_loaded, out_stored = ph.sem("x_loaded"), ph.sem("gain_loaded"), ph.sem("out_stored")
        ones_set, squared, summed, ms_ready, rms_ready, rstd_ready, scaled = (
            ph.sem(n) for n in ("ones_set", "squared", "summed", "ms_ready", "rms_ready", "rstd_ready", "scaled"))
        with ph.block() as block:
            @block.sync
            def _(sp):
                for kc in range(KC):
                    sp.dma_start(g.u[:, kc, :], g.xT[kc]).then_inc(x_loaded, 16)
                sp.dma_start(gain[:, :], g.norm1).then_inc(gain_loaded, 16)
                sp.wait_ge(scaled, SEG)
                with nc.allow_non_contiguous_dma(reason="one column per channel"):
                    sp.dma_start(g.shift_p, g.u[:, :, NP - 1:NP]).then_inc(out_stored, 16)
                    for kc in range(KC):
                        sp.dma_start(g.shift_s[:, kc], g.u[:, kc, NP + DS - 1:T:DS]).then_inc(out_stored, 16)
                sp.wait_ge(out_stored, 16 * (1 + KC))

            @block.scalar
            def _(act):
                act.wait_ge(x_loaded, 16 * KC)
                with act.Fori(0, SEG // 2) as i:
                    for u in range(2):
                        s = i * 2 + u
                        act.wait_ge(summed, s + 1)
                        act.activation(sq[:, u], g.u[:, :, ds(s * SW, SW)], ACT.Square).then_inc(squared, 1)
                        act.wait_ge(ms_ready, s + 1)
                        act.activation(rms[:, u], ms[:, u], ACT.Sqrt).then_inc(rms_ready, 1)

            @block.tensor
            def _(pe):
                pe.sem_inc(summed, 2)
                pe.wait_ge(ones_set, 1)
                with pe.Fori(0, SEG // 2) as i:
                    for u in range(2):
                        s = i * 2 + u
                        pe.wait_ge(squared, s + 1)
                        pe.wait_ge(ms_ready, s) if u else pe.wait_ge(ms_ready, i * 2)
                        for kc in range(KC):
                            mm = pe.matmul(total[:, u, 0:SW], ones[:, :], sq[:, u, kc], start=kc == 0, stop=kc == KC - 1)
                        mm.then_inc(summed, 1)

            @block.vector
            def _(dve):
                dve.memset(ones[:, :], 1.0).then_inc(ones_set, 1)
                dve.wait_ge(x_loaded, 16 * KC)
                dve.wait_ge(gain_loaded, 16)
                with dve.Fori(0, SEG // 2) as i:
                    for u in range(2):
                        s = i * 2 + u
                        dve.wait_ge(summed, s + 3)
                        dve.tensor_scalar(ms[:, u], total[:, u, 0:SW], 1.0 / D, NORM_EPS, ALU.mult, ALU.add).then_inc(ms_ready, 1)
                        dve.wait_ge(rms_ready, s + 1)
                        dve.reciprocal(rstd[:, u], rms[:, u]).then_inc(rstd_ready, 1)
                        dve.wait_ge(rstd_ready, s + 1)
                        for kc in range(KC):
                            cols = g.u[:, kc, ds(s * SW, SW)]
                            op = dve.scalar_tensor_tensor(cols, cols, gain[:, kc:kc + 1], rstd[:, u], ALU.mult, ALU.mult)
                        op.then_inc(scaled, 1)


def project_block(pe, bank, w, u, waits, bank_ready):
    for q in range(Q):
        waits(q)
        for kc in range(KC):
            mm = pe.matmul(bank[:, q, 0:QW], w[:, kc, :], u[:, kc, q * QW:(q + 1) * QW],
                           start=kc == 0, stop=kc == KC - 1)
        mm.then_inc(bank_ready, 1)


def project_glu(nc, g):
    with Phase(nc, "glu") as ph:
        w = ph.sb("w", [P, 2, KC, P])
        sig = ph.sb("sig", [P, TC])
        bank = ph.psum("bank", [P, Q, 512])
        w_loaded = [ph.sem("gate_w_loaded"), ph.sem("value_w_loaded")]
        gate_ready, value_ready, sig_ready, glu_ready, zeroed, hist_loaded, stored = (
            ph.sem(n) for n in ("gate_ready", "value_ready", "sig_ready", "glu_ready", "zeroed",
                                "hist_loaded", "stored"))
        last = Q - 1
        tail = NP - last * QW
        with ph.block() as block:
            @block.sync
            def _(sp):
                sp.dma_start(g.hist_s[:, :, :, :], g.state_conv).then_inc(hist_loaded, 16)
                with sp.Fori(0, CB) as cb:
                    for u in range(2):
                        sp.wait_ge((gate_ready, value_ready)[u], cb * Q + 1)
                        sp.dma_start(w[:, u], g.w_in[ds(cb + CB * (1 - u), 1)].rearrange("a p k c -> p (a k) c")).then_inc(w_loaded[u], 16)
                sp.wait_ge(glu_ready, Q * CB + Q)
                sp.wait_ge(hist_loaded, 16)
                sp.wait_ge(zeroed, 2)
                with nc.allow_non_contiguous_dma(reason="the last 30 rows of each sequence"):
                    sp.dma_start(g.conv_p, g.glu_p[:, :, NP:NP + HIST]).then_inc(stored, 16)
                    for cb in range(CB):
                        sp.dma_start(g.conv_s[:, cb], g.glu_s[:, cb, :, DS:DS + HIST]).then_inc(stored, 16)
                sp.wait_ge(stored, 16 * (1 + CB))

            @block.tensor
            def _(pe):
                pe.sem_inc(gate_ready, 1)
                pe.sem_inc(value_ready, 1)
                with pe.Fori(0, CB) as cb:
                    pe.wait_ge(w_loaded[0], cb * 16 + 16)
                    project_block(pe, bank, w[:, 0], g.u, lambda q: pe.wait_ge(glu_ready, cb * Q + (q + 1)), gate_ready)
                    pe.wait_ge(w_loaded[1], cb * 16 + 16)
                    project_block(pe, bank, w[:, 1], g.u, lambda q: pe.wait_ge(sig_ready, cb * Q + (q + 1)), value_ready)

            @block.scalar
            def _(act):
                with act.Fori(0, CB) as cb:
                    for q in range(Q):
                        act.wait_ge(gate_ready, cb * Q + (q + 2))
                        act.wait_ge(glu_ready, cb * Q + (q + 1))
                        act.activation(sig[:, q * QW:(q + 1) * QW], bank[:, q, 0:QW], ACT.Sigmoid).then_inc(sig_ready, 1)

            @block.vector
            def _(dve):
                dve.sem_inc(glu_ready, Q)
                dve.memset(g.glu_p[:, :, 0:HIST], 0.0).then_inc(zeroed, 1)
                dve.wait_ge(hist_loaded, 16)
                dve.tensor_copy(g.glu_s[:, :, :, 0:HIST], g.hist_s[:, :, :, :]).then_inc(zeroed, 1)
                with dve.Fori(0, CB) as cb:
                    for q in range(Q):
                        dve.wait_ge(value_ready, cb * Q + (q + 2))
                        dve.wait_ge(sig_ready, cb * Q + (q + 1))
                        n = tail if q == last else QW
                        s0 = q * QW
                        op = dve.tensor_tensor(g.glu_p[:, ds(cb, 1), HIST + s0:HIST + s0 + n].rearrange("p a n -> p (a n)"),
                                               bank[:, q, 0:n], sig[:, s0:s0 + n], ALU.mult)
                        if q == last:
                            op = dve.tensor_tensor(
                                g.glu_s[:, ds(cb, 1), :, HIST:HIST + DS].rearrange("p a b n -> p (a b) n"),
                                bank[:, q, n:n + NS].rearrange("p (b n) -> p b n", n=DS),
                                sig[:, NP:T].rearrange("p (b n) -> p b n", n=DS), ALU.mult)
                        op.then_inc(glu_ready, 1)


def project_rwkv(nc, g):
    with Phase(nc, "mix") as ph:
        w = ph.sb("w", [P, 2, KC, P])
        row = ph.sb("row", [P, 2, 1 + TC])
        diff = ph.sb("diff", [P, 2, T])
        xm = ph.sb("xm", [P, 2, T])
        mu = ph.sb("mu", [P, RWB])
        bank = ph.psum("bank", [P, Q, 512])
        w_loaded = [ph.sem("w_loaded0"), ph.sem("w_loaded1")]
        xm_stored, xm_free = ph.pool_dma_sem("xm_stored"), ph.sem("xm_free")
        bank_ready = [ph.sem("bank_ready0"), ph.sem("bank_ready1")]
        row_ready, zeroed, mu_loaded, shifted, xm_ready, diff_ready, seq_ready = (
            ph.sem(n) for n in ("row_ready", "zeroed", "mu_loaded", "shifted",
                                "xm_ready", "diff_ready", "seq_ready"))
        with ph.block() as block:
            @block.sync
            def _(sp):
                sp.dma_start(mu[:, :], g.mu).then_inc(mu_loaded, 16)
                with sp.Fori(0, RWB // 2) as i:
                    for u in range(2):
                        sp.wait_ge(bank_ready[u], i * Q + 1)
                        sp.dma_start(w[:, u], g.w_in[ds(i * 2 + (u + 2 * CB), 1)].rearrange("a p k c -> p (a k) c")).then_inc(w_loaded[u], 16)

            @block.tensor
            def _(pe):
                pe.sem_inc(bank_ready[0], 1)
                pe.sem_inc(bank_ready[1], 1)
                with pe.Fori(0, RWB // 2) as i:
                    for u in range(2):
                        pe.wait_ge(w_loaded[u], i * 16 + 16)
                        project_block(pe, bank, w[:, u], g.u,
                                      lambda q: pe.wait_ge(row_ready, i * (2 * Q) + (u * Q + q + 1)), bank_ready[u])

            @block.scalar
            def _(act):
                act.sem_inc(row_ready, Q)
                act.wait_ge(zeroed, 1)
                with act.Fori(0, RWB // 2) as i:
                    for u in range(2):
                        act.wait_ge(xm_ready, i * 2 + (u + 1))
                        for q in range(Q):
                            act.wait_ge(bank_ready[u], i * Q + (q + 2))
                            act.copy(row[:, u, 1 + q * QW:1 + (q + 1) * QW], bank[:, q, 0:QW]).then_inc(row_ready, 1)

            @block.vector
            def _(dve):
                dve.sem_inc(xm_ready, 2)
                dve.memset(row[:, :, 0:1], 0.0).then_inc(zeroed, 1)
                dve.wait_ge(mu_loaded, 16)
                dve.wait_ge(zeroed, 1)
                with dve.Fori(0, RWB // 2) as i:
                    for u in range(2):
                        n = i * 2 + u
                        dve.wait_ge(row_ready, n * Q + 2 * Q)
                        now = row[:, u, 1:1 + T]
                        dve.tensor_tensor(diff[:, u], row[:, u, 0:T], now, ALU.subtract).then_inc(diff_ready, 1)
                        dve.wait_ge(diff_ready, n + 1)
                        dve.tensor_tensor(diff[:, u, NP:T:DS], row[:, u, 1 + T:1 + TC], row[:, u, 1 + NP:1 + T:DS],
                                          ALU.subtract).then_inc(seq_ready, 1)
                        dve.wait_ge(seq_ready, n + 1)
                        dve.wait_ge(xm_free, n + 1)
                        dve.scalar_tensor_tensor(xm[:, u], diff[:, u], mu[:, ds(n, 1)], now, ALU.mult, ALU.add).then_inc(xm_ready, 1)

            @block.gpsimd
            def _(pool):
                pool.sem_inc(xm_free, 2)
                with pool.Fori(0, RWB // 2) as i:
                    for u in range(2):
                        pool.wait_ge(xm_ready, i * 2 + (u + 3))
                        pool.dma_start(g.xm[ds(i * 2 + u, 1)].rearrange("a p t -> p (a t)"), xm[:, u]).then_inc(xm_stored, 16)
                        pool.wait_ge(xm_stored, i * 32 + (u + 1) * 16)
                        pool.sem_inc(xm_free, 1)


def project_gates(nc, g):
    with Phase(nc, "gate") as ph:
        w = ph.sb("w", [P, 2, KC, P])
        row = ph.sb("row", [P, 2, T])
        taps = ph.sb("taps", [P, CB, CK])
        bias = ph.sb("bias", [P, CB])
        bank = ph.psum("bank", [P, Q, 512])
        w_loaded = [ph.sem("w_loaded0"), ph.sem("w_loaded1")]
        row_stored, row_free = ph.pool_dma_sem("row_stored"), ph.sem("row_free")
        bank_ready = [ph.sem("bank_ready0"), ph.sem("bank_ready1")]
        row_ready, taps_loaded, tapped = (
            ph.sem(n) for n in ("row_ready", "taps_loaded", "tapped"))
        NB = 2 * KC
        with ph.block() as block:
            @block.sync
            def _(sp):
                sp.dma_start(taps[:, :, :], g.conv_w).then_inc(taps_loaded, 16)
                sp.dma_start(bias[:, :], g.conv_b).then_inc(taps_loaded, 16)
                with sp.Fori(0, NB // 2) as i:
                    for u in range(2):
                        sp.wait_ge(bank_ready[u], i * Q + 1)
                        sp.dma_start(w[:, u], g.w_in[ds(i * 2 + (u + 2 * CB + RWB), 1)].rearrange("a p k c -> p (a k) c")).then_inc(w_loaded[u], 16)

            @block.tensor
            def _(pe):
                pe.sem_inc(bank_ready[0], 1)
                pe.sem_inc(bank_ready[1], 1)
                with pe.Fori(0, NB // 2) as i:
                    for u in range(2):
                        pe.wait_ge(w_loaded[u], i * 16 + 16)
                        project_block(pe, bank, w[:, u], g.u,
                                      lambda q: pe.wait_ge(row_ready, i * (2 * Q) + (u * Q + q + 1)), bank_ready[u])

            @block.scalar
            def _(act):
                act.sem_inc(row_ready, Q)
                with act.Fori(0, NB // 2) as i:
                    for u in range(2):
                        act.wait_ge(row_free, i * 2 + (u + 1))
                        for q in range(Q):
                            n = min(QW, T - q * QW)
                            act.wait_ge(bank_ready[u], i * Q + (q + 2))
                            act.activation(row[:, u, q * QW:q * QW + n], bank[:, q, 0:n], ACT.Sigmoid).then_inc(row_ready, 1)

            @block.vector
            def _(dve):
                dve.wait_ge(taps_loaded, 32)
                with dve.Fori(0, CB) as cb:
                    def full(j, sample):
                        if sample:
                            return g.glu_s[:, ds(cb, 1), :, ds(j, DS)].rearrange("p a b n -> p (a b) n")
                        return g.glu_p[:, ds(cb, 1), ds(j, NP)].rearrange("p a n -> p (a n)")

                    acc_p = g.conv[:, ds(cb, 1), 0:NP].rearrange("p a n -> p (a n)")
                    acc_s = g.conv[:, ds(cb, 1), NP:T].rearrange("p a (b n) -> p (a b) n", n=DS)
                    for acc, sample in ((acc_p, 0), (acc_s, 1)):
                        dve.tensor_scalar(acc, full(0, sample), taps[:, ds(cb, 1), 0], bias[:, ds(cb, 1)],
                                          ALU.mult, ALU.add).then_inc(tapped, 1)
                    with dve.Fori(0, HIST) as j:
                        for acc, sample in ((acc_p, 0), (acc_s, 1)):
                            dve.wait_ge(tapped, cb * (2 * CK) + j * 2 + (sample + 1))
                            dve.scalar_tensor_tensor(acc, full(j + 1, sample), taps[:, ds(cb, 1), ds(j + 1, 1)].rearrange("p a j -> p (a j)"),
                                                     acc, ALU.mult, ALU.add).then_inc(tapped, 1)

            @block.gpsimd
            def _(pool):
                pool.sem_inc(row_free, 2)
                with pool.Fori(0, NB // 2) as i:
                    for u in range(2):
                        pool.wait_ge(row_ready, i * (2 * Q) + (u + 2) * Q)
                        pool.dma_start(g.gates[ds(i * 2 + u, 1)].rearrange("a p t -> p (a t)"), row[:, u]).then_inc(row_stored, 16)
                        pool.wait_ge(row_stored, i * 32 + (u + 1) * 16)
                        pool.sem_inc(row_free, 1)


def prepare_recurrence(nc, g):
    with Phase(nc, "prep") as ph:
        lora_in = ph.sb("lora_in", [P, T])
        gate_in = ph.sb("gate_in", [P, T])
        keep = ph.sb("keep", [P, T])
        rows = {n: ph.sb(n, [P, T]) for n in
                ("r", "k", "v", "W", "L", "X1", "X2", "X3", "A", "N", "KK", "G", "RK", "B")}
        r, k, v, W, L, X1, X2, X3, A, N, KK, G, RK, B = rows.values()
        heads = ph.sb("heads", [P, P])
        lora_w = ph.sb("lora_w", [P, 3, P])
        par = ph.sb("par", [P, NPAIR, 6])
        pp = ph.sb("pp", [P, 6])
        lora_bank = ph.psum("lora_bank", [P, 3, 2, 512])
        head_bank = ph.psum("head_bank", [P, 2, 512])
        r_loaded, k_loaded, v_loaded, lora_loaded, par_loaded, in_loaded = (
            ph.pool_dma_sem(n) for n in ("r_loaded", "k_loaded", "v_loaded", "lora_loaded", "par_loaded", "in_loaded"))
        consts_set, in_ready, keep_set, pp_ready, g_stored, alpha_stored, rho_stored, beta_stored, kappa_stored, bonus_stored = (
            ph.sem(n) for n in ("consts_set", "in_ready", "keep_set", "pp_ready", "g_stored", "alpha_stored", "rho_stored",
                                "beta_stored", "kappa_stored", "bonus_stored"))
        sq_ready, lw_ready, sum_ready, before_ready, kk0_ready, rn_ready, kk_ready, t1_ready, kp_ready, b_ready, \
            lam_ready, lam_before_ready, lam_inv_ready, alpha_ready, rho_ready, rk_ready, kappa_ready, beta_ready, \
            ends_ready, ln_ready = credit = [ph.sem(n) for n in (
                "sq_ready", "lw_ready", "sum_ready", "before_ready", "kk0_ready", "rn_ready", "kk_ready", "t1_ready",
                "kp_ready", "b_ready", "lam_ready", "lam_before_ready", "lam_inv_ready", "alpha_ready", "rho_ready",
                "rk_ready", "kappa_ready", "beta_ready", "ends_ready", "ln_ready")]
        lora_done, lora_read, head_done, head_read = (
            ph.sem(n) for n in ("lora_done", "lora_read", "head_done", "head_read"))
        seg = [slice(s * SW, (s + 1) * SW) for s in range(SEG)]
        stores = ((g_stored, 16), (alpha_stored, 16), (rho_stored, 16), (beta_stored, 16), (kappa_stored, 16), (bonus_stored, 16))

        with ph.block() as block:
            @block.gpsimd
            def _(pool):
                pool.dma_start(par[:, :, :], g.rwkv_par).then_inc(par_loaded, 16)
                pool.dma_start(lora_in[:, :], g.xm[RWB - 2]).then_inc(in_loaded, 16)
                pool.dma_start(gate_in[:, :], g.xm[RWB - 1]).then_inc(in_loaded, 16)
                with pool.Fori(0, NPAIR) as p:
                    def this(s):
                        pool.wait_ge(s, p + 1)
                    pool.wait_ge(lora_done, p * SEG + 1)
                    pool.dma_start(lora_w[:, :, :], g.lora[ds(p, 1)].rearrange("a p k c -> p (a k) c")).then_inc(lora_loaded, 16)
                    this(rk_ready)
                    this(kappa_ready)
                    pool.dma_start(k[:, :], g.xm[ds(p + NPAIR, 1)].rearrange("a p t -> p (a t)")).then_inc(k_loaded, 16)
                    this(rho_ready)
                    this(rk_ready)
                    pool.dma_start(r[:, :], g.xm[ds(p, 1)].rearrange("a p t -> p (a t)")).then_inc(r_loaded, 16)
                    pool.wait_ge(head_read, p * (2 * SEG) + 2)
                    pool.dma_start(v[:, :], g.xm[ds(p + 2 * NPAIR, 1)].rearrange("a p t -> p (a t)")).then_inc(v_loaded, 16)

            @block.sync
            def _(sp):
                for s, n in stores:
                    sp.sem_inc(s, n)
                with sp.Fori(0, NPAIR) as p:
                    def chunked(i):
                        return g.zc[:, :, i, ds(p, 1), :].rearrange("c p a t -> p c (a t)")

                    def row(x):
                        return x[:, :].rearrange("p (c t) -> p c t", t=C)
                    sp.wait_ge(lora_read, p * SEG + (SEG + 2))
                    sp.dma_start(g.go[ds(p, 1)].rearrange("a p t -> p (a t)"), G[:, :]).then_inc(g_stored, 16)
                    for ready, i, x, stored in ((alpha_ready, 0, X1, alpha_stored), (rho_ready, 1, X2, rho_stored),
                                                (kappa_ready, 3, X3, kappa_stored), (beta_ready, 2, A, beta_stored)):
                        sp.wait_ge(ready, p + 2)
                        sp.dma_start(chunked(i), row(x)).then_inc(stored, 16)
                    sp.wait_ge(head_read, p * (2 * SEG) + (2 * SEG + 2))
                    sp.dma_start(g.bonus[ds(p, 1)].rearrange("a p t -> p (a t)"), B[:, :]).then_inc(bonus_stored, 16)
                for s, n in stores:
                    sp.wait_ge(s, n + 16 * NPAIR)

            @block.tensor
            def _(pe):
                pe.sem_inc(lora_done, 1)
                pe.sem_inc(head_done, 1)
                pe.wait_ge(consts_set, 3)
                pe.wait_ge(in_ready, 2)
                with pe.Fori(0, NPAIR) as p:
                    pe.wait_ge(lora_loaded, p * 16 + 16)
                    for s in range(SEG):
                        pe.wait_ge(lora_read, p * SEG + (s + 1))
                        for j, x in enumerate((lora_in, lora_in, gate_in)):
                            mm = pe.matmul(lora_bank[:, j, s % 2, 0:SW], lora_w[:, j, :], x[:, seg[s]], start=True, stop=True)
                        mm.then_inc(lora_done, 1)
                    for h, (ready, x) in enumerate(((sq_ready, RK), (rk_ready, RK))):
                        pe.wait_ge(ready, p + 2)
                        for s in range(SEG):
                            pe.wait_ge(head_read, p * (2 * SEG) + (h * SEG + s + 1))
                            pe.matmul(head_bank[:, s % 2, 0:SW], heads[:, :], x[:, seg[s]], start=True, stop=True).then_inc(head_done, 1)

            @block.scalar
            def _(act):
                for s in (sq_ready, lam_ready, lam_before_ready, lam_inv_ready, rn_ready, ln_ready):
                    act.sem_inc(s, 1)
                act.sem_inc(lora_read, 2)
                act.wait_ge(in_loaded, 32)
                act.activation(lora_in[0:C, :], lora_in[0:C, :], ACT.Tanh).then_inc(in_ready, 1)
                act.activation(gate_in[:, :], gate_in[:, :], ACT.Sigmoid).then_inc(in_ready, 1)
                act.wait_ge(par_loaded, 16)
                with act.Fori(0, NPAIR) as p:
                    def last(s):
                        act.wait_ge(s, p + 1)
                    act.wait_ge(k_loaded, p * 16 + 16)
                    act.wait_ge(head_done, p * (2 * SEG) + 1)
                    act.wait_ge(pp_ready, p + 1)
                    act.activation(RK[:, :], k[:, :], ACT.Square, scale=pp[:, 2:3]).then_inc(sq_ready, 1)
                    last(before_ready)
                    last(sum_ready)
                    act.wait_ge(beta_stored, p * 16 + 16)
                    act.wait_ge(g_stored, p * 16 + 16)
                    for s in range(SEG):
                        act.wait_ge(lora_done, p * SEG + (s + 2))
                        act.activation(W[:, seg[s]], lora_bank[:, 0, s % 2, 0:SW], ACT.Sigmoid, bias=pp[:, 0:1])
                        act.activation(A[:, seg[s]], lora_bank[:, 1, s % 2, 0:SW], ACT.Sigmoid, bias=pp[:, 1:2])
                        act.copy(G[:, seg[s]], lora_bank[:, 2, s % 2, 0:SW]).then_inc(lora_read, 1)
                    act.wait_ge(head_read, p * (2 * SEG) + (SEG + 2))
                    act.activation(N[:, :], N[:, :], ACT.Ln, scale=2.0 ** 30).then_inc(ln_ready, 1)
                    act.wait_ge(ln_ready, p + 2)
                    act.activation(N[:, :], N[:, :], ACT.Exp, scale=-0.5).then_inc(rn_ready, 1)
                    act.wait_ge(before_ready, p + 2)
                    act.activation(X1[:, :], X1[:, :], ACT.Exp).then_inc(lam_before_ready, 1)
                    act.wait_ge(rho_stored, p * 16 + 16)
                    act.activation(X2[:, :], L[:, :], ACT.Exp).then_inc(lam_ready, 1)
                    act.wait_ge(kappa_stored, p * 16 + 16)
                    act.activation(X3[:, :], L[:, :], ACT.Exp, scale=-1.0).then_inc(lam_inv_ready, 1)

            @block.vector
            def _(dve):
                for s in credit:
                    if s not in (sq_ready, lam_ready, lam_before_ready, lam_inv_ready, rn_ready, ln_ready):
                        dve.sem_inc(s, 1)
                dve.sem_inc(head_read, 2)
                dve.memset(heads[:, :], 0.0).then_inc(consts_set, 1)
                dve.wait_ge(consts_set, 1)
                for h in range(2):
                    o = dve.memset(heads[h * HD:(h + 1) * HD, h * HD:(h + 1) * HD], 1.0).then_inc(consts_set, 1)
                dve.memset(keep[:, :], 1.0).then_inc(keep_set, 1)
                dve.wait_ge(keep_set, 1)
                dve.memset(keep[:, 0:NP:C], 0.0)
                dve.memset(keep[:, NP:T:DS], 0.0).then_inc(keep_set, 1)
                dve.wait_ge(par_loaded, 16)
                dve.tensor_scalar(par[:, :, 4], par[:, :, 3], -1.0, 1.0, ALU.mult, ALU.add).then_inc(keep_set, 1)
                dve.wait_ge(keep_set, 3)
                with dve.Fori(0, NPAIR) as p:
                    def this(s):
                        dve.wait_ge(s, p + 2)
                    pd = ds(p, 1)
                    dve.wait_ge(lora_read, p * SEG + 2)
                    dve.tensor_copy(pp[:, :], par[:, pd, :].rearrange("p a n -> p (a n)")).then_inc(pp_ready, 1)
                    dve.wait_ge(pp_ready, p + 1)
                    dve.wait_ge(k_loaded, p * 16 + 16)
                    dve.tensor_scalar(KK[:, :], k[:, :], pp[:, 2:3], 2.0 ** 15, ALU.mult, ALU.mult).then_inc(kk0_ready, 1)
                    for s in range(SEG):
                        dve.wait_ge(head_done, p * (2 * SEG) + (s + 2))
                        dve.tensor_scalar(N[:, seg[s]], head_bank[:, s % 2, 0:SW], 1e-24, None, ALU.max).then_inc(head_read, 1)
                    dve.wait_ge(lora_read, p * SEG + (SEG + 2))
                    dve.tensor_scalar(W[:, :], W[:, :], -exp(-0.5), None, ALU.mult).then_inc(lw_ready, 1)
                    this(lw_ready)
                    dve.tensor_tensor_scan(L[:, :], keep[:, :], W[:, :], 0.0, ALU.mult, ALU.add).then_inc(sum_ready, 1)
                    this(sum_ready)
                    dve.wait_ge(alpha_stored, p * 16 + 16)
                    dve.tensor_tensor(X1[:, :], L[:, :], W[:, :], ALU.subtract).then_inc(before_ready, 1)
                    this(before_ready)
                    dve.tensor_scalar(W[:, :], A[:, :], pp[:, 3:4], pp[:, 4:5], ALU.mult, ALU.add).then_inc(t1_ready, 1)
                    this(t1_ready)
                    dve.tensor_tensor(k[:, :], k[:, :], W[:, :], ALU.mult).then_inc(kp_ready, 1)
                    this(rn_ready)
                    dve.tensor_tensor(KK[:, :], KK[:, :], N[:, :], ALU.mult).then_inc(kk_ready, 1)
                    this(kk_ready)
                    dve.tensor_tensor(A[:, :], A[:, :], KK[:, :], ALU.mult).then_inc(b_ready, 1)
                    this(kp_ready)
                    dve.wait_ge(r_loaded, p * 16 + 16)
                    dve.scalar_tensor_tensor(RK[:, :], r[:, :], pp[:, 5:6], k[:, :], ALU.mult, ALU.mult).then_inc(rk_ready, 1)
                    this(lam_before_ready)
                    dve.tensor_tensor(X1[:, :], X1[:, :], KK[:, :], ALU.mult).then_inc(alpha_ready, 1)
                    this(lam_ready)
                    dve.tensor_copy(g.lam_p[:, pd, :].rearrange("p a c -> p (a c)"), X2[:, C - 1:NP:C])
                    dve.tensor_copy(g.lam_s[:, pd, :].rearrange("p a c -> p (a c)"), X2[:, NP + DS - 1:T:DS]).then_inc(ends_ready, 1)
                    this(ends_ready)
                    dve.tensor_tensor(X2[:, :], X2[:, :], r[:, :], ALU.mult).then_inc(rho_ready, 1)
                    this(lam_inv_ready)
                    this(b_ready)
                    dve.tensor_tensor(A[:, :], A[:, :], X3[:, :], ALU.mult).then_inc(beta_ready, 1)
                    this(beta_ready)
                    dve.tensor_tensor(X3[:, :], X3[:, :], k[:, :], ALU.mult).then_inc(kappa_ready, 1)
                    dve.wait_ge(v_loaded, p * 16 + 16)
                    dve.wait_ge(bonus_stored, p * 16 + 16)
                    for s in range(SEG):
                        dve.wait_ge(head_done, p * (2 * SEG) + (SEG + s + 2))
                        dve.tensor_tensor(B[:, seg[s]], head_bank[:, s % 2, 0:SW], v[:, seg[s]], ALU.mult).then_inc(head_read, 1)


def recurrence(nc, g):
    LEVELS = 5
    with Phase(nc, "wkv") as ph:
        z = ph.sb("z", [P, 2, 4, NPAIR, C])
        rho = ph.sb("rho", [P, 2, NPAIR, C])
        v = ph.sb("v", [P, 2, NPAIR, C])
        masks = ph.sb("masks", [P, 2, 5, C])
        doubling = ph.sb("doubling", [P, LEVELS, C], I32)
        eye = ph.sb("eye", [P, C])
        ident = ph.sb("ident", [P, P])
        seq = ph.sb("seq", [P, DB])
        state = ph.sb("state", [P, NPAIR, HD])
        grown = ph.sb("grown", [P, NPAIR, HD])
        tt = ph.sb("tt", [P, NPAIR, C])
        zt = ph.sb("zt", [P, NPAIR, C])
        ws = ph.sb("ws", [P, NPAIR, HD])
        us = ph.sb("us", [P, NPAIR, HD])
        qt, rt, vt = (ph.sb(n, [P, 2, NPAIR, C]) for n in ("qt", "rt", "vt"))
        ys = ph.sb("ys", [P, 2, NPAIR, C])
        BD = [P, NPAIR, 2, C]
        beta_bd, kappa_bd, v_bd, a_bd, t_bd, u_bd, state_bd = single = [
            ph.sb(n, BD) for n in ("beta_bd", "kappa_bd", "v_bd", "a_bd", "t_bd", "u_bd", "state_bd")]
        alpha_bd, bt_bd, tt_bd, vt_bd, betat_bd, kappat_bd = double = [
            ph.sb(n, [P, 2] + BD[1:]) for n in ("alpha_bd", "bt_bd", "tt_bd", "vt_bd", "betat_bd", "kappat_bd")]
        bank = ph.psum("bank", [P, 8, NPAIR, C])
        states_s = ph.sb("states_s", [P, NPAIR, DB, HD])
        picked = ph.sb("picked", [P, DB, HD])
        read_s = ph.sb("read_s", [P, NPAIR, HD])
        T_BANK, Z_BANK, X_BANK, TURN_BANK, W_BANK, YS_BANK = 0, 2, 3, 4, 6, 7

        z_loaded, v_loaded = ([ph.sem(f"{n}_loaded{u}") for u in range(2)] for n in ("z", "v"))
        y_stored = [ph.sem("y_stored0"), ph.sem("y_stored1")]
        rho_loaded = [ph.sem("rho_loaded0"), ph.sem("rho_loaded1")]
        tt_bd_ready = [ph.sem("tt_bd_ready0"), ph.sem("tt_bd_ready1")]
        consts_loaded, state_stored, cleared, expanded, aq_done, br_done, a_done, vt_done, betat_done, kappat_done, \
            t_done, z_done, x_done, tt_ready, q_ready, br_ready, a_ready, vt_ready, betat_ready, kappat_ready, \
            t_ready, z_ready, vt_bd_ready, w_done, w_ready, u_done, u_ready, u_bd_ready, y_done, y_ready, \
            s_done, grown_ready, state_ready, state_bd_ready, cross_done, masked, cross_read, cross_picked, masked_tt, bv_ready = (
                ph.sem(n) for n in (
                    "consts_loaded", "state_stored", "cleared", "expanded", "aq_done", "br_done", "a_done", "vt_done",
                    "betat_done", "kappat_done", "t_done", "z_done", "x_done", "tt_ready", "q_ready", "br_ready",
                    "a_ready", "vt_ready", "betat_ready", "kappat_ready", "t_ready", "z_ready",
                    "vt_bd_ready", "w_done", "w_ready", "u_done", "u_ready", "u_bd_ready", "y_done", "y_ready",
                    "s_done", "grown_ready", "state_ready", "state_bd_ready", "cross_done", "masked", "cross_read",
                    "cross_picked", "masked_tt", "bv_ready"))
        half = [slice(0, HD), slice(HD, P)]
        NPC = NCH - 1

        def spread(copy, dst, src):
            copy(dst[half[0], :, 0, :], src[half[0]])
            return copy(dst[half[1], :, 1, :], src[half[1]])

        def over_pairs(m, n=NPAIR):
            return m.unsqueeze(1).to_broadcast([m.shape[0], n, m.shape[1]])
        passed, dve_passed = ph.sem("passed"), ph.sem("dve_passed")

        with ph.block() as block:
            @block.sync
            def _(sp):
                for dst, src in ((masks, g.masks), (doubling, g.doubling), (eye, g.eye), (seq, g.seq), (states_s, g.state_s), (ident, g.ident)):
                    sp.dma_start(dst[:], src).then_inc(consts_loaded, 16)
                sp.sem_inc(y_stored[0], 16)
                sp.sem_inc(y_stored[1], 16)

                def load(c, u):
                    sp.wait_ge(expanded, c + 1)
                    sp.wait_ge(a_done, c + 1)
                    sp.dma_start(z[:, u].rearrange("p i a t -> p (i a t)"),
                                 g.zc[ds(c, 1)].rearrange("c p i a t -> p (c i a t)")).then_inc(z_loaded[u], 16)
                    sp.dma_start(v[:, u], g.xm[2 * NPAIR:3 * NPAIR, :, ds(c * C, C)].rearrange("a p t -> p a t")).then_inc(v_loaded[u], 16)

                def load_rho(c, u):
                    sp.wait_ge(y_done, c + 1)
                    sp.dma_start(rho[:, u], g.zc[ds(c, 1), :, 1].rearrange("c p a t -> p (c a) t")).then_inc(rho_loaded[u], 16)

                def store(c, u):
                    sp.wait_ge(consts_loaded, 96)
                    sp.wait_ge(y_ready, c + 2)
                    sp.dma_start(g.y[:, :, ds(c * C, C)].rearrange("a p t -> p a t"), ys[:, u]).then_inc(y_stored[u], 16)

                load(0, 0)
                load_rho(0, 0)
                load(1, 1)
                load_rho(1, 1)
                with sp.Fori(0, NPC // 2 - 1) as i:
                    for u in range(2):
                        load(i * 2 + (u + 2), u)
                        store(i * 2 + u, u)
                        load_rho(i * 2 + (u + 2), u)
                load(NPC, 0)
                store(NPC - 2, 0)
                load_rho(NPC, 0)
                store(NPC - 1, 1)
                sp.wait_ge(state_ready, NPC + 1)
                sp.dma_start(g.wkv_p, state[:, :, :]).then_inc(state_stored, 16)
                store(NPC, 0)
                sp.wait_ge(bv_ready, NPAIR + 1)
                sp.dma_start(g.wkv_s, states_s[:, :, :, :]).then_inc(state_stored, 16)
                sp.wait_ge(state_stored, 32)
                sp.wait_ge(y_stored[0], 16 * (NPC // 2) + 32)
                sp.wait_ge(y_stored[1], 16 * (NPC // 2) + 16)

            @block.gpsimd
            def _(pool):
                for t in (*single, state):
                    pool.memset(t[:], 0.0)
                for t in double:
                    op = pool.memset(t[:], 0.0)
                op.then_inc(cleared, 1)
                pool.wait_ge(cleared, 1)
                pool.sem_inc(state_bd_ready, 1)
                pool.sem_inc(expanded, 2)

                def prepare(c, u):
                    pool.wait_ge(z_loaded[u], c * 8 + (16 - 8 * u))
                    pool.wait_ge(v_loaded[u], c * 8 + (16 - 8 * u))
                    pool.wait_ge(kappat_done, c + 1)
                    pool.wait_ge(w_done, c + 1)
                    pool.sem_inc(passed, 1)
                    for dst, src in ((beta_bd, z[:, u, 2]), (kappa_bd, z[:, u, 3]), (alpha_bd[:, u], z[:, u, 0]), (v_bd, v[:, u])):
                        op = spread(pool.tensor_copy, dst, src)
                    op.then_inc(expanded, 1)

                def spread_vt(c, u):
                    pool.wait_ge(vt_ready, c + 1)
                    pool.wait_ge(y_done, c + 1)
                    pool.sem_inc(passed, 1)
                    spread(pool.tensor_copy, vt_bd[:, u], vt[:, u]).then_inc(vt_bd_ready, 1)

                def advance_u(c):
                    pool.wait_ge(u_ready, c + 2)
                    pool.wait_ge(y_done, c + 2)
                    pool.sem_inc(passed, 1)
                    spread(pool.tensor_copy, u_bd, us).then_inc(u_bd_ready, 1)

                def advance_state(c):
                    pool.wait_ge(state_ready, c + 2)
                    pool.wait_ge(y_done, c + 3)
                    pool.sem_inc(passed, 1)
                    spread(pool.tensor_copy, state_bd, state).then_inc(state_bd_ready, 1)

                def ahead(c, u, advance=None, more=True):
                    spread_vt(c, u)
                    if advance is not None:
                        advance_u(advance)
                    if more:
                        prepare(c + 1, 1 - u)
                    if advance is not None:
                        advance_state(advance)

                prepare(0, 0)
                ahead(0, 0)
                with pool.Fori(0, NPC // 2 - 1) as i:
                    ahead(i * 2 + 1, 1, i * 2)
                    ahead(i * 2 + 2, 0, i * 2 + 1)
                ahead(NPC - 1, 1, NPC - 2)
                ahead(NPC, 0, NPC - 1, more=False)
                pool.wait_ge(cleared, 1)
                pool.wait_ge(kappat_done, NPC + 2)
                pool.sem_inc(passed, 1)
                spread(pool.tensor_copy, beta_bd, z[:, 0, 1]).then_inc(expanded, 1)
                advance_u(NPC)
                pool.wait_ge(cleared, 1)
                pool.wait_ge(cross_picked, 2 * NPAIR + 1)
                pool.wait_ge(expanded, NPC + 4)
                pool.sem_inc(passed, 1)
                spread(pool.tensor_copy, state_bd, read_s).then_inc(state_bd_ready, 1)

            @block.tensor
            def _(pe):
                for s, n in ((kappat_done, 1), (w_done, 2), (u_done, 2), (y_done, 2), (s_done, 2), (a_done, 2)):
                    pe.sem_inc(s, n)
                pe.wait_ge(cleared, 1)
                pe.wait_ge(consts_loaded, 96)

                def pairs(b, *terms, rows=range(NPAIR), padded=True):
                    for a in rows:
                        n = 2 if padded and a < NPAIR - 1 else 1
                        for k, (lhs, rhs) in enumerate(terms):
                            mm = pe.matmul(bank[:, b, a:a + n].rearrange("p a t -> p (a t)"), lhs[:, a].rearrange("p h t -> p (h t)"),
                                           rhs[:, a:a + n].rearrange("p a t -> p (a t)"),
                                           start=k == 0, stop=k == len(terms) - 1)
                    return mm

                def double(b, lhs, rhs):
                    for a in range(NPAIR):
                        mm = pe.matmul(bank[:, b + a // 4, 2 * (a % 4):2 * (a % 4) + 2, :], lhs[:, a].rearrange("p h t -> p (h t)"),
                                       rhs[:, :, a, :], start=True, stop=True)
                    return mm

                def turn(b, x):
                    for a in range(NPAIR):
                        mm = pe.transpose(bank[:, b + a // 4, 2 * (a % 4):2 * (a % 4) + 2, :].rearrange("p h t -> p (h t)"),
                                          x[:, a].rearrange("p h t -> p (h t)"), ident[:, :])
                    return mm

                def products(c, u):
                    pe.wait_ge(expanded, c + 3)
                    pe.wait_ge(tt_ready, c * (LEVELS + 1) + (LEVELS + 1))
                    double(T_BANK, beta_bd, z[:, u, 0:2]).then_inc(aq_done, 1)
                    double(Z_BANK, kappa_bd, z[:, u, 0:2]).then_inc(br_done, 1)
                    pe.wait_ge(kappat_ready, c + 1)
                    pairs(TURN_BANK, (alpha_bd[:, u], z[:, u, 2])).then_inc(a_done, 1)

                def turn_v(c):
                    pe.wait_ge(a_ready, c + 1)
                    turn(TURN_BANK, v_bd).then_inc(vt_done, 1)

                def turn_beta(c):
                    pe.wait_ge(vt_ready, c + 1)
                    turn(TURN_BANK, beta_bd).then_inc(betat_done, 1)

                def turn_kappa(c):
                    pe.wait_ge(betat_ready, c + 2)
                    turn(TURN_BANK, kappa_bd).then_inc(kappat_done, 1)

                def level_z(c, l):
                    pe.wait_ge(tt_ready, c * (LEVELS + 1) + (LEVELS + 2 + l))
                    pe.wait_ge(a_ready, c + 1)
                    pairs(Z_BANK, (a_bd, tt)).then_inc(z_done, 1)

                def level_t(c, u, l):
                    for h in range(2):
                        pe.wait_ge(tt_bd_ready[h], c * (LEVELS + 1) + (l + 2))
                    turn(T_BANK, tt_bd[:, u]).then_inc(t_done, 1)

                def level_x(c, l):
                    pe.wait_ge(t_ready, c * LEVELS + (l + 1))
                    pe.wait_ge(z_ready, c * LEVELS + (l + 1))
                    pairs(X_BANK, (t_bd, zt)).then_inc(x_done, 1)

                def w_products(c, u):
                    pe.wait_ge(vt_ready, c + 1)
                    pe.wait_ge(state_ready, c + 1)
                    pe.wait_ge(u_ready, c + 1)
                    pairs(W_BANK, (bt_bd[:, u], vt[:, u]), (alpha_bd[:, u], state)).then_inc(w_done, 1)

                def u_products(c, u):
                    for h in range(2):
                        pe.wait_ge(tt_bd_ready[h], c * (LEVELS + 1) + (LEVELS + 2))
                    pe.wait_ge(w_ready, c + 1)
                    pairs(W_BANK, (tt_bd[:, u], ws)).then_inc(u_done, 1)

                def y_products(c, u, rows):
                    if rows[0] == 0:
                        pe.wait_ge(vt_bd_ready, c + 1)
                        pe.wait_ge(state_bd_ready, c + 1)
                        pe.wait_ge(u_bd_ready, c + 1)
                        pe.wait_ge(q_ready, c + 1)
                        pe.wait_ge(rho_loaded[u], c * 8 + (16 - 8 * u))
                        pe.wait_ge(grown_ready, c + 1)
                    mm = pairs(YS_BANK, (vt_bd[:, u], rt[:, u]), (state_bd, rho[:, u]), (u_bd, qt[:, u]), rows=rows)
                    if rows[-1] == NPAIR - 1:
                        mm.then_inc(y_done, 1)

                def state_products(c, u):
                    pe.wait_ge(u_ready, c + 2)
                    pe.wait_ge(kappat_ready, c + 2)
                    pe.wait_ge(betat_ready, c + 2)
                    pe.wait_ge(y_ready, c + 2)
                    pairs(YS_BANK, (kappat_bd[:, u], vt[:, u]), (betat_bd[:, u], us)).then_inc(s_done, 1)

                def ahead(c, u, advance=None):
                    def back(step, *a):
                        if advance is not None:
                            step(advance, 1 - u, *a)
                    products(c, u)
                    level_z(c, 0)
                    level_t(c, u, 0)
                    back(w_products)
                    level_x(c, 0)
                    turn_v(c)
                    level_z(c, 1)
                    turn_beta(c)
                    level_t(c, u, 1)
                    back(u_products)
                    level_x(c, 1)
                    turn_kappa(c)
                    level_z(c, 2)
                    level_t(c, u, 2)
                    back(y_products, range(0, 2))
                    level_x(c, 2)
                    back(y_products, range(2, 4))
                    level_z(c, 3)
                    level_t(c, u, 3)
                    back(y_products, range(4, 6))
                    level_x(c, 3)
                    back(y_products, range(6, 8))
                    level_z(c, 4)
                    level_t(c, u, 4)
                    back(state_products)
                    level_x(c, 4)

                ahead(0, 0)
                with pe.Fori(0, NPC // 2 - 1) as i:
                    ahead(i * 2 + 1, 1, i * 2)
                    ahead(i * 2 + 2, 0, i * 2 + 1)
                ahead(NPC - 1, 1, NPC - 2)
                ahead(NPC, 0, NPC - 1)

                c = NPC
                pe.wait_ge(expanded, c + 4)
                pe.wait_ge(u_ready, c + 1)
                for n, lhs in enumerate((alpha_bd[:, 0], beta_bd)):
                    for a in range(NPAIR):
                        pe.wait_ge(masked, n * NPAIR + a + 1)
                        pe.matmul(bank[:, W_BANK].rearrange("p a t -> p (a t)"), lhs[:, a].rearrange("p h t -> p (h t)"),
                                  states_s[:, a].rearrange("p b v -> p (b v)"), start=True, stop=True).then_inc(cross_done, 1)
                pe.wait_ge(masked, 2 * NPAIR + 1)
                pairs(W_BANK, (bt_bd[:, 0], vt[:, 0])).then_inc(w_done, 1)
                u_products(c, 0)
                pe.wait_ge(state_bd_ready, c + 2)
                pe.wait_ge(vt_bd_ready, c + 1)
                pe.wait_ge(u_bd_ready, c + 1)
                pe.wait_ge(q_ready, c + 1)
                pe.wait_ge(grown_ready, c + 1)
                pairs(YS_BANK, (vt_bd[:, 0], rt[:, 0]), (state_bd, eye[:, :].unsqueeze(1).to_broadcast([P, NPAIR, C])),
                      (u_bd, qt[:, 0]), padded=False).then_inc(y_done, 1)
                pe.wait_ge(y_ready, c + 2)
                pe.wait_ge(kappat_ready, c + 2)
                pe.wait_ge(betat_ready, c + 2)
                for a in range(NPAIR):
                    pe.wait_ge(grown_ready, NPC + a + 1)
                    pe.wait_ge(cross_read, 2 * a + 2)
                    pe.matmul(bank[:, YS_BANK].rearrange("p a t -> p (a t)"), kappat_bd[:, 0, a].rearrange("p h t -> p (h t)"),
                              z[:, 0].rearrange("p i a t -> p (i a t)")[:, 0:DB * HD], start=True, stop=False)
                    pe.matmul(bank[:, YS_BANK].rearrange("p a t -> p (a t)"), betat_bd[:, 0, a].rearrange("p h t -> p (h t)"),
                              z[:, 0].rearrange("p i a t -> p (i a t)")[:, DB * HD:2 * DB * HD], start=False, stop=True).then_inc(s_done, 1)

            @block.scalar
            def _(act):
                act.sem_inc(betat_ready, 1)
                act.sem_inc(kappat_ready, 1)
                act.sem_inc(y_ready, 1)
                act.sem_inc(tt_bd_ready[0], 1)
                act.wait_ge(cleared, 1)
                turned = bank[:, TURN_BANK:TURN_BANK + 2].rearrange("p b (a h) t -> p (b a) h t", h=2)
                turned_t = bank[:, T_BANK:T_BANK + 2].rearrange("p b (a h) t -> p (b a) h t", h=2)

                def gather(copy, dst, src, last):
                    for h in range(2):
                        op = copy(dst(h), src[half[h], :, h, :])
                    op.then_inc(last, 1)

                def turn_v(c, u):
                    act.wait_ge(vt_done, c + 1)
                    act.wait_ge(s_done, c + 1)
                    gather(act.copy, lambda h: vt[half[h], u], turned, vt_ready)

                def turn_beta(c, u):
                    act.wait_ge(betat_done, c + 1)
                    gather(lambda o, x: act.mul(o, x, -1.0), lambda h: betat_bd[half[h], u, :, h, :], turned, betat_ready)

                def turn_kappa(c, u):
                    act.wait_ge(kappat_done, c + 2)
                    gather(act.copy, lambda h: kappat_bd[half[h], u, :, h, :], turned, kappat_ready)

                def level_t(c, l):
                    act.wait_ge(t_done, c * LEVELS + (l + 1))
                    gather(act.copy, lambda h: t_bd[half[h], :, h, :], turned_t, t_ready)

                def spread_tt(c, u, l):
                    act.wait_ge(tt_ready, c * (LEVELS + 1) + (LEVELS + 2 + l))
                    if l == 0:
                        act.wait_ge(u_done, c + 1)
                    act.copy(tt_bd[half[0], u, :, 0, :], tt[half[0]]).then_inc(tt_bd_ready[0], 1)

                def advance_y(c, u):
                    act.wait_ge(y_done, c + 3)
                    act.wait_ge(y_stored[u], c * 8 + (16 - 8 * u))
                    act.copy(ys[:, u], bank[:, YS_BANK]).then_inc(y_ready, 1)

                def ahead(c, u, advance=None):
                    spread_tt(c, u, 0)
                    level_t(c, 0)
                    spread_tt(c, u, 1)
                    turn_v(c, u)
                    turn_beta(c, u)
                    level_t(c, 1)
                    spread_tt(c, u, 2)
                    turn_kappa(c, u)
                    level_t(c, 2)
                    spread_tt(c, u, 3)
                    level_t(c, 3)
                    spread_tt(c, u, 4)
                    if advance is not None:
                        advance_y(advance, 1 - u)
                    level_t(c, 4)
                    spread_tt(c, u, 5)

                ahead(0, 0)
                with act.Fori(0, NPC // 2 - 1) as i:
                    ahead(i * 2 + 1, 1, i * 2)
                    ahead(i * 2 + 2, 0, i * 2 + 1)
                ahead(NPC - 1, 1, NPC - 2)
                ahead(NPC, 0, NPC - 1)
                advance_y(NPC, 0)

            @block.vector
            def _(dve):
                dve.sem_inc(tt_ready, LEVELS + 1)
                dve.sem_inc(grown_ready, 1)
                dve.sem_inc(tt_bd_ready[1], 1)
                dve.sem_inc(u_ready, 1)
                dve.sem_inc(state_ready, 1)
                dve.wait_ge(cleared, 1)
                dve.wait_ge(consts_loaded, 96)
                wide_aq = bank[:, T_BANK:T_BANK + 2].rearrange("p b (a w) t -> p (b a) w t", w=2)
                wide_br = bank[:, Z_BANK:Z_BANK + 2].rearrange("p b (a w) t -> p (b a) w t", w=2)

                def spread_tt(c, u, l):
                    dve.wait_ge(tt_ready, c * (LEVELS + 1) + (LEVELS + 2 + l))
                    if l == 0:
                        dve.wait_ge(u_done, c + 1)
                    dve.tensor_copy(tt_bd[half[1], u, :, 1, :], tt[half[1]]).then_inc(tt_bd_ready[1], 1)

                def products(c, u, m):
                    dve.wait_ge(aq_done, c + 1)
                    for h in range(2):
                        dve.wait_ge(tt_bd_ready[h], c * (LEVELS + 1) + 1)
                    dve.tensor_tensor(tt[:, :, :], wide_aq[:, :, 0, :], over_pairs(masks[:, m, 0]), ALU.mult).then_inc(masked_tt, 1)
                    dve.wait_ge(y_done, c + 1)
                    dve.tensor_tensor(qt[:, u], wide_aq[:, :, 1, :], over_pairs(masks[:, m, 1]), ALU.mult).then_inc(q_ready, 1)
                    dve.wait_ge(masked_tt, c + 1)
                    dve.tensor_tensor(tt[:, :, :], tt[:, :, :], over_pairs(eye[:, :]), ALU.add).then_inc(tt_ready, 1)
                    spread_tt(c, u, 0)
                    dve.wait_ge(br_done, c + 1)
                    for h in range(2):
                        dve.tensor_tensor(bt_bd[half[h], u, :, h, :], wide_br[half[h], :, 0, :], over_pairs(masks[half[h], m, 2]), ALU.mult)
                    dve.tensor_tensor(rt[:, u], wide_br[:, :, 1, :], over_pairs(masks[:, m, 3]), ALU.mult).then_inc(br_ready, 1)
                    dve.wait_ge(a_done, c + 3)
                    for h in range(2):
                        op = dve.tensor_tensor(a_bd[half[h], :, h, :], bank[half[h], TURN_BANK], over_pairs(masks[half[h], m, 4]), ALU.mult)
                    op.then_inc(a_ready, 1)

                def level_z(c, l):
                    dve.wait_ge(z_done, c * LEVELS + (l + 1))
                    dve.tensor_copy(zt[:, :, :], bank[:, Z_BANK]).then_inc(z_ready, 1)

                def level_x(c, u, l):
                    dve.wait_ge(x_done, c * LEVELS + (l + 1))
                    dve.wait_ge(tt_bd_ready[1], c * (LEVELS + 1) + (l + 2))
                    dve.sem_inc(dve_passed, 1)
                    dve.copy_predicated(tt[:, :, :], over_pairs(doubling[:, l]), bank[:, X_BANK]).then_inc(tt_ready, 1)
                    spread_tt(c, u, l + 1)

                def advance_w(c):
                    dve.wait_ge(w_done, c + 3)
                    dve.tensor_copy(ws[:, :, :], bank[:, W_BANK]).then_inc(w_ready, 1)

                def advance_u(c):
                    dve.wait_ge(u_done, c + 3)
                    dve.tensor_copy(us[:, :, :], bank[:, W_BANK]).then_inc(u_ready, 1)

                def advance_state(c):
                    dve.wait_ge(s_done, c + 3)
                    dve.tensor_tensor(grown[:, :, :], bank[:, YS_BANK], state[:, :, :], ALU.add).then_inc(grown_ready, 1)
                    dve.wait_ge(grown_ready, c + 2)
                    dve.wait_ge(state_bd_ready, c + 1)
                    dve.tensor_tensor(state[:, :, :], grown[:, :, :], g.lam_p[:, :, ds(c, 1)].to_broadcast([P, NPAIR, HD]),
                                      ALU.mult).then_inc(state_ready, 1)

                def ahead(c, u, m=0, advance=None):
                    def back(step):
                        if advance is not None:
                            step(advance)
                    products(c, u, m)
                    level_z(c, 0)
                    back(advance_w)
                    level_x(c, u, 0)
                    level_z(c, 1)
                    back(advance_u)
                    level_x(c, u, 1)
                    for l in (2, 3):
                        level_z(c, l)
                        level_x(c, u, l)
                    level_z(c, 4)
                    back(advance_state)
                    level_x(c, u, 4)

                ahead(0, 0)
                with dve.Fori(0, NPC // 2 - 1) as i:
                    ahead(i * 2 + 1, 1, 0, i * 2)
                    ahead(i * 2 + 2, 0, 0, i * 2 + 1)
                ahead(NPC - 1, 1, 0, NPC - 2)
                ahead(NPC, 0, 1, NPC - 1)

                c = NPC
                by_seq = seq[:, :].unsqueeze(2).to_broadcast([P, DB, HD])
                dve.sem_inc(masked, 1)
                dve.sem_inc(cross_picked, 1)
                for n, out in enumerate((ws, read_s)):
                    for a in range(NPAIR):
                        k = n * NPAIR + a
                        dve.wait_ge(cross_done, k + 1)
                        dve.wait_ge(cross_picked, k + 1)
                        dve.tensor_tensor(picked[:, :, :], bank[:, W_BANK], by_seq, ALU.mult).then_inc(masked, 1)
                        dve.wait_ge(masked, k + 2)
                        dve.tensor_reduce(out[:, a, :], picked[:, :, :].rearrange("p b v -> p v b"), AX.X, ALU.add).then_inc(cross_picked, 1)
                dve.wait_ge(cross_picked, 2 * NPAIR + 1)
                dve.wait_ge(w_done, c + 3)
                dve.tensor_tensor(ws[:, :, :], bank[:, W_BANK], ws[:, :, :], ALU.add).then_inc(w_ready, 1)
                advance_u(c)
                dve.sem_inc(bv_ready, 1)
                dve.wait_ge(u_ready, c + 2)
                dve.wait_ge(y_done, c + 3)
                zf = z[:, 0].rearrange("p i a t -> p (i a t)")
                for a in range(NPAIR):
                    if a:
                        dve.wait_ge(s_done, NPC + 2 + a)
                    for j, x in enumerate((vt[:, 0, a, :], us[:, a, :])):
                        dve.tensor_tensor(zf[:, j * DB * HD:(j + 1) * DB * HD].rearrange("p (b v) -> p b v", b=DB),
                                          x.unsqueeze(1).to_broadcast([P, DB, HD]), by_seq, ALU.mult).then_inc(cross_read, 1)
                    dve.wait_ge(s_done, NPC + 3 + a)
                    dve.tensor_tensor(picked[:, :, :], bank[:, YS_BANK], states_s[:, a], ALU.add).then_inc(grown_ready, 1)
                    dve.wait_ge(grown_ready, NPC + a + 2)
                    dve.tensor_tensor(states_s[:, a], picked[:, :, :],
                                      g.lam_s[:, a, :].unsqueeze(2).to_broadcast([P, DB, HD]), ALU.mult).then_inc(bv_ready, 1)


def finish_mixing(nc, g):
    with Phase(nc, "finish") as ph:
        buf = {n: ph.sb(n, [P, 2, T]) for n in ("y", "bonus", "gate")}
        sq = ph.sb("sq", [P, T])
        rstd = ph.sb("rstd", [P, T])
        heads = ph.sb("heads", [P, P])
        means = ph.sb("means", [P, P])
        par = ph.sb("par", [P, 4, NPAIR])
        pp = ph.sb("pp", [P, 2])
        eps = ph.sb("eps", [P, 2])
        bank = ph.psum("bank", [P, SEG, 512])
        loaded = [ph.sem("loaded0"), ph.sem("loaded1")]
        par_loaded, consts_set, pp_ready, mean_done, centred, squared, var_done, ln_ready, rstd_ready, scaled, biased, \
            mixed_ready, conv_mean, conv_centred, conv_squared, conv_var, conv_ln, conv_rstd, conv_scaled, conv_sig, \
            conv_ready = (
                ph.sem(n) for n in (
                    "par_loaded", "consts_set", "pp_ready", "mean_done", "centred", "squared", "var_done", "ln_ready",
                    "rstd_ready", "scaled", "biased", "mixed_ready", "conv_mean", "conv_centred", "conv_squared",
                    "conv_var", "conv_ln", "conv_rstd", "conv_scaled", "conv_sig", "conv_ready"))
        seg = [slice(s * SW, (s + 1) * SW) for s in range(SEG)]
        y, bonus, gate = buf["y"], buf["bonus"], buf["gate"]

        with ph.block() as block:
            @block.sync
            def _(sp):
                sp.dma_start(par[:, :, :], g.norm_par).then_inc(par_loaded, 16)
                with sp.Fori(0, NPAIR // 2) as i:
                    for u in range(2):
                        sp.wait_ge(mixed_ready, i * 2 + (u + 1))
                        for x, src in ((y, g.y), (bonus, g.bonus), (gate, g.go)):
                            sp.dma_start(x[:, u], src[ds(i * 2 + u, 1)].rearrange("a p t -> p (a t)")).then_inc(loaded[u], 16)

            @block.tensor
            def _(pe):
                pe.wait_ge(consts_set, 5)
                with pe.Fori(0, NPAIR // 2) as i:
                    for u in range(2):
                        p = i * 2 + u
                        pe.wait_ge(loaded[u], i * 48 + 48)
                        pe.wait_ge(ln_ready, p + 1)
                        for s in range(SEG):
                            mm = pe.matmul(bank[:, s, 0:SW], heads[:, :], y[:, u, seg[s]], start=True, stop=True)
                        mm.then_inc(mean_done, 1)
                        pe.wait_ge(squared, p + 1)
                        for s in range(SEG):
                            mm = pe.matmul(bank[:, s, 0:SW], heads[:, :], sq[:, seg[s]], start=True, stop=True)
                        mm.then_inc(var_done, 1)
                pe.wait_ge(ln_ready, NPAIR + 1)
                for s in range(SEG):
                    for b in range(CB):
                        mm = pe.matmul(bank[:, s, 0:SW], means[:, :], g.conv[:, b, seg[s]], start=b == 0, stop=b == CB - 1)
                mm.then_inc(conv_mean, 1)
                for s in range(SEG):
                    for b in range(CB):
                        pe.wait_ge(conv_squared, s * CB + b + 1)
                        pe.matmul(bank[:, s, 0:SW], means[:, :], sq[:, (b % 2) * SW:(b % 2 + 1) * SW],
                                  start=b == 0, stop=b == CB - 1).then_inc(conv_var, 1)

            @block.scalar
            def _(act):
                act.sem_inc(ln_ready, 1)
                act.wait_ge(consts_set, 5)
                with act.Fori(0, NPAIR // 2) as i:
                    for u in range(2):
                        p = i * 2 + u
                        act.wait_ge(centred, p + 1)
                        act.activation(sq[:, :], y[:, u], ACT.Square).then_inc(squared, 1)
                        act.wait_ge(var_done, p + 1)
                        act.wait_ge(scaled, p + 1)
                        act.activation(rstd[:, :].rearrange("p (s n) -> p s n", s=SEG), bank[:, :, 0:SW], ACT.Ln,
                                       bias=eps[:, 0:1]).then_inc(ln_ready, 1)
                        act.wait_ge(ln_ready, p + 2)
                        act.activation(rstd[:, :], rstd[:, :], ACT.Exp, scale=-0.5).then_inc(rstd_ready, 1)
                act.wait_ge(conv_centred, 1)
                for s in range(SEG):
                    for b in range(CB):
                        if s * CB + b >= 2:
                            act.wait_ge(conv_var, s * CB + b - 1)
                        act.activation(sq[:, (b % 2) * SW:(b % 2 + 1) * SW], g.conv[:, b, seg[s]], ACT.Square).then_inc(conv_squared, 1)
                act.wait_ge(conv_var, SEG * CB)
                act.wait_ge(scaled, NPAIR + 1)
                act.activation(rstd[:, :].rearrange("p (s n) -> p s n", s=SEG), bank[:, :, 0:SW], ACT.Ln,
                               bias=eps[:, 1:2]).then_inc(conv_ln, 1)
                act.wait_ge(conv_ln, 1)
                act.activation(rstd[:, :], rstd[:, :], ACT.Exp, scale=-0.5).then_inc(conv_rstd, 1)
                for b in range(CB):
                    act.wait_ge(conv_scaled, b + 1)
                    if b:
                        act.wait_ge(conv_ready, b)
                    act.activation(sq[:, :], g.conv[:, b, :], ACT.Sigmoid, bias=par[:, 3, b:b + 1]).then_inc(conv_sig, 1)

            @block.vector
            def _(dve):
                dve.memset(means[:, :], 1.0 / CW).then_inc(consts_set, 1)
                dve.memset(heads[:, :], 0.0).then_inc(consts_set, 1)
                dve.memset(eps[:, 0:1], GN_EPS)
                dve.memset(eps[:, 1:2], LN_EPS).then_inc(consts_set, 1)
                dve.wait_ge(consts_set, 3)
                for h in range(2):
                    dve.memset(heads[h * HD:(h + 1) * HD, h * HD:(h + 1) * HD], 1.0 / HD).then_inc(consts_set, 1)
                dve.sem_inc(mixed_ready, 2)
                dve.sem_inc(scaled, 1)
                dve.wait_ge(par_loaded, 16)
                with dve.Fori(0, NPAIR // 2) as i:
                    for u in range(2):
                        p = i * 2 + u
                        yu = y[:, u]
                        dve.tensor_copy(pp[:, :], par[:, 0:2, ds(p, 1)].rearrange("p n a -> p (n a)")).then_inc(pp_ready, 1)
                        dve.wait_ge(mean_done, p + 1)
                        dve.wait_ge(loaded[u], i * 48 + 48)
                        dve.tensor_tensor(yu.rearrange("p (s n) -> p s n", s=SEG), yu.rearrange("p (s n) -> p s n", s=SEG),
                                          bank[:, :, 0:SW], ALU.subtract).then_inc(centred, 1)
                        dve.wait_ge(rstd_ready, p + 1)
                        dve.wait_ge(pp_ready, p + 1)
                        dve.scalar_tensor_tensor(yu, yu, pp[:, 0:1], rstd[:, :], ALU.mult, ALU.mult).then_inc(scaled, 1)
                        dve.wait_ge(scaled, p + 2)
                        dve.scalar_tensor_tensor(yu, yu, pp[:, 1:2], bonus[:, u], ALU.add, ALU.add).then_inc(biased, 1)
                        dve.wait_ge(biased, p + 1)
                        dve.tensor_tensor(g.mixed[:, ds(p, 1), :].rearrange("p a t -> p (a t)"), yu, gate[:, u], ALU.mult).then_inc(mixed_ready, 1)
                dve.wait_ge(conv_mean, 1)
                for b in range(CB):
                    x = g.conv[:, b, :].rearrange("p (s n) -> p s n", s=SEG)
                    op = dve.tensor_tensor(x, x, bank[:, :, 0:SW], ALU.subtract)
                op.then_inc(conv_centred, 1)
                dve.wait_ge(conv_rstd, 1)
                for b in range(CB):
                    dve.scalar_tensor_tensor(g.conv[:, b, :], g.conv[:, b, :], par[:, 2, b:b + 1], rstd[:, :],
                                             ALU.mult, ALU.mult).then_inc(conv_scaled, 1)
                for b in range(CB):
                    dve.wait_ge(conv_sig, b + 1)
                    dve.scalar_tensor_tensor(g.conv[:, b, :], g.conv[:, b, :], par[:, 3, b:b + 1], sq[:, :],
                                             ALU.add, ALU.mult).then_inc(conv_ready, 1)


def mix_branches(nc, g):
    with Phase(nc, "branch") as ph:
        w = ph.sb("w", [P, 2, KC + CB, P])
        gate = ph.sb("gate", [P, 2, 2, T])
        m = ph.sb("m", [P, 2, NT * P])
        part = ph.sb("part", [P, 2, QW])
        bias = ph.sb("bias", [P, KC])
        bb = ph.sb("bb", [P, 2])
        bank = ph.psum("bank", [P, 2, 2, 512])
        w_loaded = [ph.sem("w_loaded0"), ph.sem("w_loaded1")]
        gate_loaded = [ph.sem("gate_loaded0"), ph.sem("gate_loaded1")]
        bias_loaded, bank_ready, bank_free, bb_ready, gated_ready, m_ready, m_free = (
            ph.sem(n) for n in ("bias_loaded", "bank_ready", "bank_free", "bb_ready", "gated_ready",
                                "m_ready", "m_free"))
        m_stored = ph.pool_dma_sem("m_stored")

        with ph.block() as block:
            @block.sync
            def _(sp):
                sp.dma_start(bias[:, :], g.conv_out_b).then_inc(bias_loaded, 16)
                with sp.Fori(0, KC // 2) as i:
                    for u in range(2):
                        cb = i * 2 + u
                        sp.wait_ge(m_ready, cb + 1)
                        sp.dma_start(w[:, u], g.w_branch[ds(cb, 1)].rearrange("a p k c -> p (a k) c")).then_inc(w_loaded[u], 16)
                        for n in range(2):
                            sp.dma_start(gate[:, u, n], g.gates[ds(cb + n * KC, 1)].rearrange("a p t -> p (a t)")).then_inc(gate_loaded[u], 16)

            @block.gpsimd
            def _(pool):
                with pool.Fori(0, KC // 2) as i:
                    for u in range(2):
                        cb = i * 2 + u
                        pool.wait_ge(m_ready, cb + 3)
                        pool.dma_start(g.m[ds(cb, 1)].rearrange("a p t -> p (a t)"), m[:, u]).then_inc(m_stored, 16)
                        pool.wait_ge(m_stored, cb * 16 + 16)
                        pool.sem_inc(m_free, 1)

            @block.tensor
            def _(pe):
                with pe.Fori(0, KC // 2) as i:
                    for u in range(2):
                        cb = i * 2 + u
                        pe.wait_ge(w_loaded[u], i * 16 + 16)
                        for q in range(Q):
                            n = min(QW, T - q * QW)
                            k = cb * Q + q
                            pe.wait_ge(bank_free, k + 1)
                            for src, b, k0, kn in ((g.mixed, 0, 0, KC), (g.conv, 1, KC, CB)):
                                for kc in range(kn):
                                    mm = pe.matmul(bank[:, b, (q + u) % 2, 0:n], w[:, u, k0 + kc, :], src[:, kc, q * QW:q * QW + n],
                                                   start=kc == 0, stop=kc == kn - 1)
                            mm.then_inc(bank_ready, 1)

            @block.vector
            def _(dve):
                dve.sem_inc(bank_free, 2)
                dve.sem_inc(m_ready, 2)
                dve.sem_inc(m_free, 2)
                dve.memset(m[:, :, T:NT * P], 0.0)
                dve.wait_ge(bias_loaded, 16)
                with dve.Fori(0, KC // 2) as i:
                    for u in range(2):
                        cb = i * 2 + u
                        dve.tensor_copy(bb[:, u:u + 1], bias[:, ds(cb, 1)]).then_inc(bb_ready, 1)
                        dve.wait_ge(bb_ready, cb + 1)
                        dve.wait_ge(gate_loaded[u], i * 32 + 32)
                        dve.wait_ge(m_free, cb + 1)
                        for q in range(Q):
                            n = min(QW, T - q * QW)
                            k = cb * Q + q
                            cols = slice(q * QW, q * QW + n)
                            dve.wait_ge(bank_ready, k + 1)
                            dve.scalar_tensor_tensor(part[:, 0, 0:n], bank[:, 1, (q + u) % 2, 0:n], bb[:, u:u + 1],
                                                     gate[:, u, 0, cols], ALU.add, ALU.mult)
                            dve.tensor_tensor(part[:, 1, 0:n], bank[:, 0, (q + u) % 2, 0:n], gate[:, u, 1, cols], ALU.mult).then_inc(bank_free, 1)
                            dve.wait_ge(bank_free, k + 3)
                            dve.tensor_tensor(m[:, u, cols], part[:, 0, 0:n], part[:, 1, 0:n], ALU.add).then_inc(gated_ready, 1)
                            dve.wait_ge(gated_ready, k + 1)
                        dve.sem_inc(m_ready, 1)


def route(nc, g):
    with Phase(nc, "route") as ph:
        w_o = ph.sb("w_o", [P, KC, D])
        rw = ph.sb("rw", [P, KC, NG + NE])
        rb = ph.sb("rb", [P, NG + NE])
        gain = ph.sb("gain", [P, D])
        ident = ph.sb("ident", [P, P])
        earlier = ph.sb("earlier", [P, P])
        ones = ph.sb("ones", [P, P])
        w_hi, w_lo = (ph.sb(n, [P, KC, D], F32R) for n in ("w_hi", "w_lo"))
        m = ph.sb("m", [P, 2, KC, P])
        m_hi, m_lo = (ph.sb(n, [P, 2, KC, P], F32R) for n in ("m_hi", "m_lo"))
        x = ph.sb("x", [P, 2, D])
        x2 = ph.sb("x2", [P, 2, D])
        h = ph.sb("h", [P, 2, D])
        hT = ph.sb("hT", [P, KC, P])
        junk = ph.sb("junk", [P, D])
        ss, ms, lms, rstd, nmax, esum, g_one = (ph.sb(n, [P, 1]) for n in (
            "ss", "ms", "lms", "rstd", "nmax", "esum", "g_one"))
        logits = ph.sb("logits", [P, NG + NE])
        glog = ph.sb("glog", [P, 8])
        top, etop, e_exp = (ph.sb(n, [P, 8]) for n in ("top", "etop", "e_exp"))
        gexp = ph.sb("gexp", [P, NG])
        gidx, eidx = (ph.sb(n, [P, 8], U32) for n in ("gidx", "eidx"))
        gid = ph.sb("gid", [P, 1])
        ghot = ph.sb("ghot", [P, NG])
        chosen = ph.sb("chosen", [P, EPG])
        ids = ph.sb("ids", [P, NE])
        hot = ph.sb("hot", [P, 2, NE])
        both = ph.sb("both", [P, NE])
        base = ph.sb("base", [P, NE])
        rank = ph.sb("rank", [P, NE])
        at = ph.sb("at", [P, 2, NE])
        valid = ph.sb("valid", [P, 1])
        expert = ph.sb("expert", [P, NT, 2])
        ranks = ph.sb("ranks", [P, NT, 2])
        dest = ph.sb("dest", [P, NT, 2])
        allhot = ph.sb("allhot", [P, NT * 2, NE])
        count_i = ph.sb("count_i", [P, NE], I32)
        padded, ends, starts, each_one = (ph.sb(n, [P, NE]) for n in ("padded", "ends", "starts", "each_one"))
        blocks = ph.sb("blocks", [P, NBLK])
        filled = ph.sb("filled", [P, NBLK, NE])
        block_of, fresh, block_ones = (ph.sb(n, [P, NBLK]) for n in ("block_of", "fresh", "block_ones"))
        token = ph.sb("token", [P, NT], I32)
        nothing = ph.sb("nothing", [P, NBLK + 1], I32)
        spare = ph.sb("spare", [P, 2])
        bank = ph.psum("bank", [P, 8, 512])
        m_loaded, x_loaded, x2_stored, h_stored = ([ph.sem(f"{n}{u}") for u in range(2)] for n in
                                                   ("m_loaded", "x_loaded", "x2_stored", "h_stored"))
        consts_loaded, consts_set, out_done, x2_ready, h_ready, squared, ln_ready, rstd_ready, turned, hT_ready, \
            logits_done, counts_done, gexp_ready, eexp_ready, routed, tile_done, dest_ready, nothing_set, \
            ms_ready, nmax_ready, e_diff_ready, hot_ready, valid_set = (
                ph.sem(n) for n in (
                    "consts_loaded", "consts_set", "out_done", "x2_ready", "h_ready", "squared",
                    "ln_ready", "rstd_ready", "turned", "hT_ready", "logits_done", "counts_done", "gexp_ready",
                    "eexp_ready", "routed", "tile_done", "dest_ready", "nothing_set",
                    "ms_ready", "nmax_ready", "e_diff_ready", "hot_ready", "valid_set"))
        LINKS, CHOICE = 22, 19
        NCONST = 6
        table_cleared, scattered, ids_stored = (ph.pool_dma_sem(n) for n in ("table_cleared", "scattered", "ids_stored"))
        w_hi_ready, w_lo_ready, m_hi_ready, m_lo_ready, ranked = (ph.sem(n) for n in (
            "w_hi_ready", "w_lo_ready", "m_hi_ready", "m_lo_ready", "ranked"))
        OUT, TURNED, LOGITS, COUNTS = (0, 2), 4, 6, 7
        passed = ph.sem("passed")

        with ph.block() as block:
            @block.sync
            def _(sp):
                for dst, src in ((w_o, g.w_o), (rw, g.router_w), (ident, g.ident), (earlier, g.earlier)):
                    sp.dma_start(dst[:], src).then_inc(consts_loaded, 16)
                sp.dma_start(rb[:, :], g.router_b.to_broadcast([P, NG + NE])).then_inc(consts_loaded, 16)
                sp.dma_start(gain[:, :], g.norm2.to_broadcast([P, D])).then_inc(consts_loaded, 16)
                for s in (*x2_stored, *h_stored):
                    sp.sem_inc(s, 16)

                def load(t, u):
                    sp.wait_ge(m_lo_ready, t + 1)
                    sp.dma_start(m[:, u], g.m[:, :, ds(t * P, P)].rearrange("k p t -> p k t")).then_inc(m_loaded[u], 16)
                    sp.wait_ge(x2_ready, t + 1)
                    sp.dma_start(x[:, u], g.x[ds(t * P, P)]).then_inc(x_loaded[u], 16)

                def store(t, u):
                    sp.wait_ge(h_ready, t + 1)
                    sp.dma_start(g.x2[ds(t * P, P)], x2[:, u]).then_inc(x2_stored[u], 16)
                    sp.dma_start(g.h[ds(t * P, P)], h[:, u]).then_inc(h_stored[u], 16)

                load(0, 0)
                load(1, 1)
                with sp.Fori(0, NT // 2 - 1) as i:
                    for u in range(2):
                        load(i * 2 + (u + 2), u)
                        store(i * 2 + u, u)
                load(NT - 1, 0)
                for t in range(NT - 3, NT):
                    store(t, t % 2)
                for s, n in ((x2_stored, 0), (h_stored, 0)):
                    sp.wait_ge(s[0], 16 + 16 * (NT // 2 + 1))
                    sp.wait_ge(s[1], 16 + 16 * (NT // 2))

            @block.tensor
            def _(pe):
                pe.wait_ge(consts_loaded, 16 * NCONST)
                pe.wait_ge(consts_set, 1)

                def product(t, u, n):
                    if n == 0:
                        pe.wait_ge(m_lo_ready, t + 3)
                        pe.wait_ge(x2_ready, t + 1)
                    cols = slice(n * 512, (n + 1) * 512)
                    for kc in range(KC):
                        for k, (a, w) in enumerate(((m_hi, w_hi), (m_hi, w_lo), (m_lo, w_hi))):
                            mm = pe.matmul(bank[:, OUT[u] + n], a[:, u, kc, :], w[:, kc, cols],
                                           start=kc == 0 and k == 0, stop=kc == KC - 1 and k == 2)
                    if n == 1:
                        mm.then_inc(out_done, 1)

                def turn(t, u):
                    pe.wait_ge(h_ready, t + 1)
                    pe.wait_ge(hT_ready, t + 1)
                    for kc in range(KC):
                        mm = pe.transpose(bank[:, TURNED + kc // 4, (kc % 4) * P:(kc % 4 + 1) * P], h[:, u, kc * P:(kc + 1) * P], ident[:, :])
                    mm.then_inc(turned, 1)

                def count(t):
                    pe.wait_ge(tile_done, t + 1)
                    pe.matmul(bank[:, COUNTS, 0:NE], earlier[:, :], both[:, :], start=True, stop=True)
                    pe.matmul(bank[:, COUNTS, NE:2 * NE], ones[:, :], both[:, :], start=True, stop=True).then_inc(counts_done, 1)

                def score(t):
                    pe.wait_ge(hT_ready, t + 2)
                    pe.wait_ge(ranked, t + 1)
                    for kc in range(KC):
                        mm = pe.matmul(bank[:, LOGITS, 0:NG + NE], hT[:, kc, :], rw[:, kc, :], start=kc == 0, stop=kc == KC - 1)
                    mm.then_inc(logits_done, 1)

                def first():
                    pe.wait_ge(w_lo_ready, 2)
                    pe.sem_inc(ranked, 1)
                    product(0, 0, 0)
                    product(0, 0, 1)

                def step(t, u, ranks=True, split=True):
                    product(t + 1, 1 - u, 0)
                    if ranks:
                        count(t - 1)
                    turn(t, u)
                    product(t + 1, 1 - u, 1)
                    score(t)

                def last(t, u):
                    count(t - 1)
                    turn(t, u)
                    score(t)
                    count(t)

                first()
                step(0, 0, ranks=False)
                with pe.Fori(0, (NT - 3) // 2) as i:
                    step(i * 2 + 1, 1)
                    step(i * 2 + 2, 0)
                step(NT - 2, 1, split=False)
                last(NT - 1, 0)

            @block.scalar
            def _(act):
                act.sem_inc(hT_ready, 1)

                def split(t, u):
                    act.wait_ge(m_loaded[u], t * 8 + (16 - 8 * u))
                    act.wait_ge(out_done, t + 1)
                    act.copy(m_hi[:, u], m[:, u]).then_inc(m_hi_ready, 1)

                def rms(t, u):
                    act.wait_ge(x2_ready, t + 3)
                    act.activation(junk[:, :], x2[:, u], ACT.Square, accum_out=ss[:, :]).then_inc(squared, 1)
                    act.wait_ge(ms_ready, t + 1)
                    act.activation(lms[:, :], ms[:, :], ACT.Ln).then_inc(ln_ready, 1)
                    act.wait_ge(ln_ready, t + 1)
                    act.activation(rstd[:, :], lms[:, :], ACT.Exp, scale=-0.5).then_inc(rstd_ready, 1)

                def turn(t):
                    act.wait_ge(turned, t + 1)
                    act.copy(hT[:, :, :].rearrange("p k t -> p (k t)"), bank[:, TURNED:TURNED + 2].rearrange("p b t -> p (b t)")).then_inc(hT_ready, 1)

                def gates(t):
                    act.wait_ge(nmax_ready, t + 1)
                    act.activation(gexp[:, :], logits[:, 0:NG], ACT.Exp, bias=nmax[:, :], accum_out=esum[:, :]).then_inc(gexp_ready, 1)
                    act.wait_ge(e_diff_ready, t + 1)
                    act.activation(e_exp[:, 0:1], etop[:, 2:3], ACT.Exp).then_inc(eexp_ready, 1)

                def first():
                    act.sem_inc(out_done, 2)
                    act.wait_ge(consts_loaded, 16 * NCONST)
                    act.copy(w_hi[:, 0:KC // 2], w_o[:, 0:KC // 2]).then_inc(w_hi_ready, 1)
                    act.copy(w_hi[:, KC // 2:], w_o[:, KC // 2:]).then_inc(w_hi_ready, 1)
                    split(0, 0)
                    split(1, 1)
                    rms(0, 0)

                def step(t, u, ranks=True, split_on=True):
                    if split_on:
                        split(t + 2, u)
                    turn(t)
                    rms(t + 1, 1 - u)
                    gates(t)

                def last(t, u):
                    turn(t)
                    gates(t)

                first()
                step(0, 0, ranks=False)
                with act.Fori(0, (NT - 3) // 2) as i:
                    step(i * 2 + 1, 1)
                    step(i * 2 + 2, 0)
                step(NT - 2, 1, split_on=False)
                last(NT - 1, 0)

            @block.gpsimd
            def _(pool):
                pool.iota(ids[:, :], [[1, NE]], base=0, channel_multiplier=0, allow_small_or_imprecise_dtypes=True)
                pool.iota(blocks[:, :], [[EB, NBLK]], base=0, channel_multiplier=0, allow_small_or_imprecise_dtypes=True)
                pool.iota(spare[:, :], [[-(T % P), 2]], base=NBLK * EB, channel_multiplier=1, allow_small_or_imprecise_dtypes=True)
                pool.iota(token[:, :], [[P, NT]], base=0, channel_multiplier=1)
                pool.memset(nothing[:, :], 0).then_inc(nothing_set, 1)
                for u in range(2):
                    pool.sem_inc(m_lo_ready, 1)

                def split(t, u):
                    pool.wait_ge(m_hi_ready, t + 1)
                    pool.wait_ge(out_done, t + 1)
                    pool.tensor_tensor(m_lo[:, u], m[:, u], m_hi[:, u].bitcast(F32), ALU.subtract).then_inc(m_lo_ready, 1)

                split(0, 0)
                split(1, 1)
                with pool.Fori(0, NT // 2 - 1) as i:
                    for u in range(2):
                        split(i * 2 + (u + 2), u)
                split(NT - 1, 0)
                pool.wait_ge(nothing_set, 1)
                pool.dma_start(g.row_token.rearrange("(p n) a -> p (n a)", p=P), nothing[:, :]).then_inc(table_cleared, 16)
                pool.wait_ge(table_cleared, 16)
                pool.wait_ge(dest_ready, 1)
                for t in range(NT):
                    for s in range(2):
                        pool.indirect_dma_start(g.row_token, bass.IndirectOffsetOnAxis(ap=g.dest_i[:, t, s:s + 1], axis=0),
                                                token[:, t:t + 1], None).then_inc(scattered, 16)
                pool.wait_ge(scattered, 16 * 2 * NT)
                with nc.allow_non_contiguous_dma(reason="a block's rows go over the partitions"):
                    pool.dma_start(g.row_of[:, :], g.row_token[0:NBLK * EB].rearrange("(n p) a -> p (n a)", p=P)).then_inc(ids_stored, 16)
                pool.wait_ge(ids_stored, 16)

            @block.vector
            def _(dve):
                dve.sem_inc(x2_ready, 2)
                dve.sem_inc(routed, 1)
                dve.memset(each_one[:, :], 1.0)
                dve.memset(block_ones[:, :], 1.0)
                dve.memset(base[:, :], 0.0)
                dve.memset(glog[:, :], -3.0e38)
                dve.memset(valid[:, :], 0.0)
                dve.memset(ones[:, :], 1.0).then_inc(consts_set, 1)
                dve.wait_ge(consts_set, 1)
                dve.memset(valid[0:T % P, :], 1.0).then_inc(valid_set, 1)
                dve.wait_ge(nothing_set, 1)
                dve.wait_ge(consts_loaded, 16 * NCONST)
                dve.wait_ge(valid_set, 1)
                for n in range(2):
                    part = slice(n * KC // 2, (n + 1) * KC // 2)
                    dve.wait_ge(w_hi_ready, n + 1)
                    dve.tensor_tensor(w_lo[:, part], w_o[:, part], w_hi[:, part].bitcast(F32), ALU.subtract).then_inc(w_lo_ready, 1)
                n = [0]

                def links(t):
                    def link(op, before_max=False):
                        op.then_inc(routed, 1)
                        n[0] += 1
                        dve.wait_ge(routed, t * LINKS + (n[0] + 1))
                        if before_max:
                            dve.sem_inc(passed, 1)

                    return link

                def residual(t, u):
                    dve.wait_ge(out_done, t + 3)
                    dve.wait_ge(x_loaded[u], t * 8 + (16 - 8 * u))
                    dve.wait_ge(x2_stored[u], t * 8 + (16 - 8 * u))
                    dve.tensor_tensor(x2[:, u], bank[:, OUT[u]:OUT[u] + 2].rearrange("p b t -> p (b t)"), x[:, u], ALU.add).then_inc(x2_ready, 1)

                def mean_square(t):
                    dve.wait_ge(squared, t + 1)
                    dve.tensor_scalar(ms[:, :], ss[:, :], 1.0 / D, NORM_EPS, ALU.mult, ALU.add).then_inc(ms_ready, 1)

                def normalise(t, u):
                    dve.wait_ge(rstd_ready, t + 1)
                    dve.wait_ge(h_stored[u], t * 8 + (16 - 8 * u))
                    dve.scalar_tensor_tensor(h[:, u], x2[:, u], rstd[:, :], gain[:, :], ALU.mult, ALU.mult).then_inc(h_ready, 1)

                def choose(t, partial=False):
                    n[0] = 0
                    link = links(t)
                    dve.wait_ge(logits_done, t + 1)
                    link(dve.tensor_tensor(logits[:, :], bank[:, LOGITS, 0:NG + NE], rb[:, :], ALU.add))
                    link(dve.tensor_copy(glog[:, 0:NG], logits[:, 0:NG]), before_max=True)
                    link(dve.max(top[:, :], glog[:, :]), before_max=True)
                    link(dve.max_index(gidx[:, :], top[:, :], glog[:, :]))
                    dve.tensor_scalar(nmax[:, :], top[:, 0:1], -1.0, None, ALU.mult).then_inc(nmax_ready, 1)
                    link(dve.tensor_copy(gid[:, :], gidx[:, 0:1]))
                    link(dve.tensor_scalar(ghot[:, :], ids[:, 0:NG], gid[:, :], None, ALU.is_equal))
                    le = logits[:, NG:].rearrange("p (n e) -> p n e", n=NG)
                    link(dve.tensor_scalar(chosen[:, :], le[:, 0], ghot[:, 0:1], None, ALU.mult))
                    for k in range(1, NG):
                        link(dve.scalar_tensor_tensor(chosen[:, :], le[:, k], ghot[:, k:k + 1], chosen[:, :], ALU.mult, ALU.add), before_max=k == NG - 1)
                    link(dve.max(etop[:, :], chosen[:, :]), before_max=True)
                    link(dve.max_index(eidx[:, :], etop[:, :], chosen[:, :]))
                    link(dve.tensor_tensor(etop[:, 2:3], etop[:, 1:2], etop[:, 0:1], ALU.subtract))
                    dve.tensor_scalar(gid[:, :], gid[:, :], float(EPG), None, ALU.mult).then_inc(e_diff_ready, 1)
                    dve.wait_ge(e_diff_ready, t + 1)
                    ex = expert[:, ds(t, 1), :].rearrange("p a s -> p (a s)")
                    link(dve.tensor_copy(ex, eidx[:, 0:2]))
                    link(dve.tensor_scalar(ex, ex, gid[:, :], None, ALU.add))
                    for s in range(2):
                        dve.tensor_scalar(hot[:, s], ids[:, :], expert[:, ds(t, 1), s], None, ALU.is_equal).then_inc(hot_ready, 1)
                    dve.wait_ge(hot_ready, t * 2 + 2)
                    link(dve.tensor_tensor(both[:, :], hot[:, 0], hot[:, 1], ALU.add))
                    if partial:
                        dve.tensor_scalar(both[:, :], both[:, :], valid[:, :], None, ALU.mult).then_inc(tile_done, 1)
                    else:
                        dve.sem_inc(tile_done, 1)
                    dve.wait_ge(gexp_ready, t + 1)
                    dve.wait_ge(eexp_ready, t + 1)
                    link(dve.tensor_scalar(g_one[:, :], e_exp[:, 0:1], 1.0, None, ALU.add))
                    link(dve.tensor_tensor(esum[:, :], esum[:, :], g_one[:, :], ALU.mult))
                    gt = g.gate_of[:, ds(t, 1), :].rearrange("p a s -> p (a s)")
                    link(dve.reciprocal(gt[:, 0:1], esum[:, :]))
                    dve.tensor_tensor(gt[:, 1:2], gt[:, 0:1], e_exp[:, 0:1], ALU.mult)
                    assert n[0] == CHOICE, n[0]

                def rank_rows(t):
                    n[0] = CHOICE
                    link = links(t)
                    dve.wait_ge(counts_done, t + 1)
                    link(dve.tensor_tensor(rank[:, :], bank[:, COUNTS, 0:NE], base[:, :], ALU.add))
                    link(dve.tensor_tensor(at[:, :, :], hot[:, :, :], rank[:, :].unsqueeze(1).to_broadcast([P, 2, NE]), ALU.mult))
                    dve.tensor_reduce(ranks[:, ds(t, 1), :].rearrange("p a s -> p (a s)"), at[:, :, :], AX.X, ALU.add)
                    link(dve.tensor_tensor(base[:, :], bank[:, COUNTS, NE:2 * NE], base[:, :], ALU.add))
                    assert n[0] == LINKS, n[0]
                    dve.sem_inc(ranked, 1)

                def first():
                    residual(0, 0)
                    mean_square(0)
                    normalise(0, 0)

                def step(t, u, ranks=True, split=True):
                    residual(t + 1, 1 - u)
                    if ranks:
                        rank_rows(t - 1)
                    mean_square(t + 1)
                    choose(t)
                    normalise(t + 1, 1 - u)

                def last(t, u):
                    rank_rows(t - 1)
                    choose(t, partial=True)
                    rank_rows(t)

                first()
                step(0, 0, ranks=False)
                with dve.Fori(0, (NT - 3) // 2) as i:
                    step(i * 2 + 1, 1)
                    step(i * 2 + 2, 0)
                step(NT - 2, 1, split=False)
                last(NT - 1, 0)

                n[0] = NT * LINKS + 1

                def link(op):
                    op.then_inc(routed, 1)
                    n[0] += 1
                    dve.wait_ge(routed, n[0])

                link(dve.tensor_scalar(count_i[:, :], base[:, :], float(EB - 1), None, ALU.add))
                link(dve.tensor_scalar(count_i[:, :], count_i[:, :], 7, 7, ALU.logical_shift_right, ALU.logical_shift_left))
                link(dve.tensor_copy(padded[:, :], count_i[:, :]))
                link(dve.tensor_tensor_scan(ends[:, :], each_one[:, :], padded[:, :], 0.0, ALU.mult, ALU.add))
                link(dve.tensor_tensor(starts[:, :], ends[:, :], padded[:, :], ALU.subtract))
                ex = expert[:, :, :].rearrange("p t s -> p (t s)")
                link(dve.tensor_tensor(allhot[:, :, :], ids[:, :].unsqueeze(1).to_broadcast([P, 2 * NT, NE]),
                                       ex.unsqueeze(2).to_broadcast([P, 2 * NT, NE]), ALU.is_equal))
                link(dve.tensor_tensor(allhot[:, :, :], allhot[:, :, :], starts[:, :].unsqueeze(1).to_broadcast([P, 2 * NT, NE]), ALU.mult))
                link(dve.tensor_reduce(dest[:, :, :].rearrange("p t s -> p (t s)"), allhot[:, :, :], AX.X, ALU.add))
                link(dve.tensor_tensor(dest[:, :, :], dest[:, :, :], ranks[:, :, :], ALU.add))
                last = dest[:, NT - 1, :]
                link(dve.tensor_tensor(last, last, spare[:, :], ALU.subtract))
                link(dve.tensor_scalar(last, last, valid[:, :], None, ALU.mult))
                link(dve.tensor_tensor(last, last, spare[:, :], ALU.add))
                link(dve.tensor_copy(g.dest_i[:, :, :], dest[:, :, :]))
                dve.sem_inc(dest_ready, 1)
                link(dve.tensor_tensor(filled[:, :, :], blocks[:, :].unsqueeze(2).to_broadcast([P, NBLK, NE]),
                                       ends[:, :].unsqueeze(1).to_broadcast([P, NBLK, NE]), ALU.is_ge))
                link(dve.tensor_reduce(block_of[:, :], filled[:, :, :], AX.X, ALU.add))
                link(dve.tensor_scalar(block_of[:, :], block_of[:, :], float(NE - 1), None, ALU.min))
                link(dve.tensor_copy(g.block_expert[:, :], block_of[:, :]))
                link(dve.memset(fresh[:, 0:1], 1.0))
                link(dve.tensor_tensor(fresh[:, 1:], block_of[:, 1:], block_of[:, 0:NBLK - 1], ALU.not_equal))
                link(dve.tensor_copy(g.block_fresh[:, :], fresh[:, :]))
                link(dve.tensor_tensor_scan(block_of[:, :], block_ones[:, :], fresh[:, :], 0.0, ALU.mult, ALU.add))
                link(dve.tensor_copy(g.block_buffer[:, :], block_of[:, :]))
                link(dve.tensor_scalar(g.block_buffer[:, :], g.block_buffer[:, :], 1, None, ALU.bitwise_and))


def run_experts(nc, g):
    DEPTH = 2
    HW = 2 * DE
    with Phase(nc, "expert") as ph:
        w = ph.sb("w", [P, DEPTH, KC * HW])
        wd = ph.sb("wd", [P, DEPTH, 2 * D])
        ident = ph.sb("ident", [P, P])
        rows = ph.sb("rows", [P, DEPTH], I32)
        x = ph.sb("x", [P, DEPTH, D])
        xT = ph.sb("xT", [P, KC, P])
        sig = ph.sb("sig", [P, DE])
        act_h = ph.sb("act_h", [P, DE])
        hT = ph.sb("hT", [P, 2, P])
        out = ph.sb("out", [P, DEPTH, D])
        zero = ph.sb("zero", [P, D])
        bank = ph.psum("bank", [P, 8, 512])
        w_loaded, wd_loaded, out_stored = ([ph.sem(f"{n}{u}") for u in range(DEPTH)] for n in ("w_loaded", "wd_loaded", "out_stored"))
        ident_loaded, rows_ready, turned, xT_ready, up_done, sig_ready, gated, h_ready, h_turned, hT_ready, \
            down_done, out_ready, zero_set, half_out = (
                ph.sem(n) for n in ("ident_loaded", "rows_ready", "turned", "xT_ready", "up_done",
                                    "sig_ready", "gated", "h_ready", "h_turned", "hT_ready", "down_done", "out_ready",
                                    "zero_set", "half_out"))
        zero_stored, gathered = (ph.pool_dma_sem(n) for n in ("zero_stored", "gathered"))
        passed, sp_passed = ph.sem("passed"), ph.sem("sp_passed")

        with ph.block() as block:
            @block.sync
            def _(sp):
                sp.dma_start(ident[:, :], g.ident).then_inc(ident_loaded, 16)

                def load(b, u, dst, src, used, loaded):
                    e = sp.value_load(g.block_expert[0:1, ds(b, 1)], min_val=0, max_val=NE - 1)
                    buf = sp.value_load(g.block_buffer[0:1, ds(b, 1)], min_val=0, max_val=1)
                    fresh = sp.value_load(g.block_fresh[0:1, ds(b, 1)], min_val=0, max_val=1)
                    sp.wait_ge(used, b + 1)
                    sp.sem_inc(sp_passed, 1)
                    with sp.If(fresh == 1):
                        sp.dma_start(dst[:, ds(buf, 1)].rearrange("p a n -> p (a n)"), src[ds(e, 1)].rearrange("a p n -> p (a n)")).then_inc(loaded[u], 16)
                    with sp.Else():
                        sp.sem_inc(loaded[u], 16)

                load(0, 0, w, g.w_up, up_done, w_loaded)
                with sp.Fori(0, NBLK // 2 - 1) as i:
                    for u in range(2):
                        load(i * 2 + (u + 1), 1 - u, w, g.w_up, up_done, w_loaded)
                        load(i * 2 + u, u, wd, g.w_down, down_done, wd_loaded)
                load(NBLK - 1, 1, w, g.w_up, up_done, w_loaded)
                load(NBLK - 2, 0, wd, g.w_down, down_done, wd_loaded)
                load(NBLK - 1, 1, wd, g.w_down, down_done, wd_loaded)

            @block.gpsimd
            def _(pool):
                pool.memset(zero[:, :], 0.0).then_inc(zero_set, 1)
                pool.wait_ge(zero_set, 1)
                pool.dma_start(g.yb[NBLK * EB:], zero[:, :]).then_inc(zero_stored, 16)
                pool.wait_ge(zero_stored, 16)
                with pool.Fori(0, NBLK // 2) as i:
                    for u in range(2):
                        b = i * 2 + u
                        pool.wait_ge(turned, b + 1)
                        pool.sem_inc(passed, 1)
                        pool.tensor_copy(rows[:, u:u + 1], g.row_of[:, ds(b, 1)]).then_inc(rows_ready, 1)
                        pool.wait_ge(rows_ready, b + 1)
                        pool.sem_inc(passed, 1)
                        pool.indirect_dma_start(x[:, u], None, g.h, bass.IndirectOffsetOnAxis(ap=rows[:, u:u + 1], axis=0)).then_inc(gathered, 16)
                        pool.wait_ge(gathered, b * 16 + 16)

            @block.tensor
            def _(pe):
                for s in (turned, up_done, down_done):
                    pe.sem_inc(s, 2)
                pe.wait_ge(ident_loaded, 16)

                def turn(b, u):
                    pe.wait_ge(gathered, b * 16 + 16)
                    pe.wait_ge(xT_ready, b + 1)
                    for kc in range(KC):
                        mm = pe.transpose(bank[:, kc // 4, (kc % 4) * P:(kc % 4 + 1) * P], x[:, u, kc * P:(kc + 1) * P], ident[:, :])
                    mm.then_inc(turned, 1)

                def up(b, u):
                    buf = pe.value_load(g.block_buffer[0:1, ds(b, 1)], min_val=0, max_val=1)
                    pe.wait_ge(xT_ready, b + 2)
                    pe.wait_ge(w_loaded[u], b * 8 + (16 - 8 * u))
                    pe.wait_ge(h_ready, b + 1)
                    for kc in range(KC):
                        mm = pe.matmul(bank[:, 2], xT[:, kc, :], w[:, ds(buf, 1), kc * HW:(kc + 1) * HW].rearrange("p a n -> p (a n)"),
                                       start=kc == 0, stop=kc == KC - 1)
                    mm.then_inc(up_done, 1)

                def turn_h(b):
                    pe.wait_ge(h_ready, b + 2)
                    pe.wait_ge(hT_ready, b + 1)
                    for f in range(2):
                        mm = pe.transpose(bank[:, 3, f * P:(f + 1) * P], act_h[:, f * P:(f + 1) * P], ident[:, :])
                    mm.then_inc(h_turned, 1)

                def down(b, u):
                    buf = pe.value_load(g.block_buffer[0:1, ds(b, 1)], min_val=0, max_val=1)
                    pe.wait_ge(hT_ready, b + 2)
                    pe.wait_ge(wd_loaded[u], b * 8 + (16 - 8 * u))
                    pe.wait_ge(out_ready, b + 1)
                    for n in range(2):
                        for f in range(2):
                            mm = pe.matmul(bank[:, 4 + n], hT[:, f, :], wd[:, ds(buf, 1), f * D + n * 512:f * D + (n + 1) * 512].rearrange("p a n -> p (a n)"),
                                           start=f == 0, stop=f == 1)
                    mm.then_inc(down_done, 1)

                def step(b, u):
                    up(b, u)
                    turn(b + 1, 1 - u)
                    down(b - 1, 1 - u)
                    turn_h(b)

                turn(0, 0)
                up(0, 0)
                turn(1, 1)
                turn_h(0)
                with pe.Fori(0, NBLK // 2 - 1) as i:
                    step(i * 2 + 1, 1)
                    step(i * 2 + 2, 0)
                up(NBLK - 1, 1)
                down(NBLK - 2, 0)
                turn_h(NBLK - 1)
                down(NBLK - 1, 1)

            @block.scalar
            def _(act):
                act.sem_inc(out_ready, 1)
                for u in range(2):
                    act.sem_inc(out_stored[u], 16)

                def gate(b):
                    act.wait_ge(up_done, b + 3)
                    act.activation(sig[:, :], bank[:, 2, 0:DE], ACT.Sigmoid).then_inc(sig_ready, 1)

                def store(b, u):
                    act.wait_ge(down_done, b + 3)
                    act.wait_ge(out_stored[u], b * 8 + (16 - 8 * u))
                    act.copy(out[:, u], bank[:, 4:6].rearrange("p b n -> p (b n)")).then_inc(out_ready, 1)
                    act.wait_ge(out_ready, b + 2)
                    act.dma_start(g.yb[ds(b * EB, EB)], out[:, u]).then_inc(out_stored[u], 16)

                act.wait_ge(up_done, 3)
                act.activation(sig[:, :], bank[:, 2, 0:DE], ACT.Sigmoid).then_inc(sig_ready, 1)
                with act.Fori(0, NBLK // 2 - 1) as i:
                    gate(i * 2 + 1)
                    store(i * 2, 0)
                    gate(i * 2 + 2)
                    store(i * 2 + 1, 1)
                gate(NBLK - 1)
                store(NBLK - 2, 0)
                store(NBLK - 1, 1)
                for u in range(2):
                    act.wait_ge(out_stored[u], 16 + 16 * (NBLK // 2))

            @block.vector
            def _(dve):
                dve.sem_inc(xT_ready, 1)
                dve.sem_inc(h_ready, 1)
                dve.sem_inc(hT_ready, 1)

                def move_x(b):
                    dve.wait_ge(turned, b + 3)
                    dve.wait_ge(up_done, b + 2)
                    dve.tensor_copy(xT[:, :, :].rearrange("p k t -> p (k t)"), bank[:, 0:2].rearrange("p b t -> p (b t)")).then_inc(xT_ready, 1)

                def gate(b):
                    dve.wait_ge(sig_ready, b + 1)
                    dve.tensor_tensor(sig[:, :], bank[:, 2, 0:DE], sig[:, :], ALU.mult).then_inc(gated, 1)
                    dve.wait_ge(gated, b + 1)
                    dve.tensor_tensor(act_h[:, :], bank[:, 2, DE:HW], sig[:, :], ALU.mult).then_inc(h_ready, 1)

                def move_h(b):
                    dve.wait_ge(h_turned, b + 1)
                    dve.wait_ge(down_done, b + 2)
                    dve.tensor_copy(hT[:, :, :].rearrange("p k t -> p (k t)"), bank[:, 3, 0:2 * P]).then_inc(hT_ready, 1)

                move_x(0)
                with dve.Fori(0, NBLK // 2 - 1) as i:
                    for u in range(2):
                        gate(i * 2 + u)
                        move_x(i * 2 + (u + 1))
                        move_h(i * 2 + u)
                gate(NBLK - 2)
                move_x(NBLK - 1)
                move_h(NBLK - 2)
                gate(NBLK - 1)
                move_h(NBLK - 1)


def combine(nc, g):
    with Phase(nc, "combine") as ph:
        gain = ph.sb("gain", [P, D])
        x2 = ph.sb("x2", [P, 2, D])
        rows = ph.sb("rows", [P, 2, 2], I32)
        e0, e1 = (ph.sb(n, [P, 2, D]) for n in ("e0", "e1"))
        out = ph.sb("out", [P, 2, D])
        junk = ph.sb("junk", [P, D])
        ss, ms, lms, rstd = (ph.sb(n, [P, 1]) for n in ("ss", "ms", "lms", "rstd"))
        x2_loaded, out_stored = ([ph.sem(f"{n}{u}") for u in range(2)] for n in ("x2_loaded", "out_stored"))
        gain_loaded, rows_ready, first_added, added, squared, ms_ready, ln_ready, rstd_ready, out_ready, consts = (
            ph.sem(n) for n in ("gain_loaded", "rows_ready", "first_added", "added", "squared",
                                "ms_ready", "ln_ready", "rstd_ready", "out_ready", "consts"))
        gathered0, gathered1 = (ph.pool_dma_sem(n) for n in ("gathered0", "gathered1"))
        passed = ph.sem("passed")

        with ph.block() as block:
            def tiles(eng, tile):
                with eng.Fori(0, NT // 2) as i:
                    for u in range(2):
                        tile(i * 2 + u, u, P)
                tile(NT - 1, 0, T - (NT - 1) * P)

            @block.sync
            def _(sp):
                sp.dma_start(gain[:, :], g.norm_f.to_broadcast([P, D])).then_inc(gain_loaded, 16)
                sp.sem_inc(out_stored[0], 16)
                sp.sem_inc(out_stored[1], 16)

                def load(t, u):
                    sp.wait_ge(out_ready, t + 1)
                    sp.dma_start(x2[:, u], g.x2[ds(t * P, P)]).then_inc(x2_loaded[u], 16)

                def store(t, u, n):
                    sp.wait_ge(out_ready, t + 3)
                    sp.dma_start(g.y_out[ds(t * P, n)], out[0:n, u]).then_inc(out_stored[u], 16)

                load(0, 0)
                with sp.Fori(0, NT // 2) as i:
                    for u in range(2):
                        load(i * 2 + (u + 1), 1 - u)
                        store(i * 2 + u, u, P)
                store(NT - 1, 0, T - (NT - 1) * P)
                sp.wait_ge(out_stored[0], 16 + 16 * (NT // 2 + 1))
                sp.wait_ge(out_stored[1], 16 + 16 * (NT // 2))

            @block.gpsimd
            def _(pool):
                pool.memset(junk[:, 0:1], 0.0).then_inc(consts, 1)

                def tile(t, u, n):
                    pool.wait_ge(added, t + 1)
                    pool.sem_inc(passed, 1)
                    pool.tensor_copy(rows[:, u], g.dest_i[:, ds(t, 1), :].rearrange("p a s -> p (a s)")).then_inc(rows_ready, 1)
                    pool.wait_ge(rows_ready, t + 1)
                    pool.sem_inc(passed, 1)
                    for s, (e, done) in enumerate(((e0, gathered0), (e1, gathered1))):
                        pool.indirect_dma_start(e[:, u], None, g.yb, bass.IndirectOffsetOnAxis(ap=rows[:, u, s:s + 1], axis=0)).then_inc(done, 16)
                    pool.wait_ge(gathered0, t * 16 + 16)
                    pool.wait_ge(gathered1, t * 16 + 16)
                tiles(pool, tile)

            @block.scalar
            def _(act):
                def tile(t, u, n):
                    act.wait_ge(added, t + 3)
                    act.activation(junk[:, :], out[:, u], ACT.Square, accum_out=ss[:, :]).then_inc(squared, 1)
                    act.wait_ge(ms_ready, t + 1)
                    act.activation(lms[:, :], ms[:, :], ACT.Ln).then_inc(ln_ready, 1)
                    act.wait_ge(ln_ready, t + 1)
                    act.activation(rstd[:, :], lms[:, :], ACT.Exp, scale=-0.5).then_inc(rstd_ready, 1)
                act.wait_ge(consts, 1)
                tiles(act, tile)

            @block.vector
            def _(dve):
                dve.sem_inc(added, 2)
                dve.sem_inc(out_ready, 2)
                dve.wait_ge(gain_loaded, 16)

                def tile(t, u, n):
                    dve.wait_ge(x2_loaded[u], t * 8 + (16 - 8 * u))
                    dve.wait_ge(gathered0, t * 16 + 16)
                    dve.wait_ge(out_stored[u], t * 8 + (16 - 8 * u))
                    dve.scalar_tensor_tensor(out[:, u], e0[:, u], g.gate_of[:, ds(t, 1), 0], x2[:, u], ALU.mult, ALU.add).then_inc(first_added, 1)
                    dve.wait_ge(gathered1, t * 16 + 16)
                    dve.wait_ge(first_added, t + 1)
                    dve.scalar_tensor_tensor(out[:, u], e1[:, u], g.gate_of[:, ds(t, 1), 1], out[:, u], ALU.mult, ALU.add).then_inc(added, 1)
                    dve.wait_ge(squared, t + 1)
                    dve.tensor_scalar(ms[:, :], ss[:, :], 1.0 / D, NORM_EPS, ALU.mult, ALU.add).then_inc(ms_ready, 1)
                    dve.wait_ge(rstd_ready, t + 1)
                    dve.scalar_tensor_tensor(out[:, u], out[:, u], rstd[:, :], gain[:, :], ALU.mult, ALU.mult).then_inc(out_ready, 1)
                tiles(dve, tile)


PHASES = [norm_inputs, project_glu, project_rwkv, project_gates, prepare_recurrence, recurrence, finish_mixing,
          mix_branches, route, run_experts, combine]


def hybrid_step(nc, ins, outs):
    g = Tensors(ins, outs)

    def scratch(name, shape, dt=F32):
        return nc.dram_tensor(name, shape, dt, kind="Internal").ap()

    g.xm = scratch("xm", [RWB, P, T])
    g.gates = scratch("gates", [2 * KC, P, T])
    g.zc = scratch("zc", [NCH, P, 4, NPAIR, C])
    g.y = scratch("y", [NPAIR, P, T])
    g.go = scratch("go", [NPAIR, P, T])
    g.bonus = scratch("bonus", [NPAIR, P, T])
    g.m = scratch("m", [KC, P, NT * P])
    g.x2 = scratch("x2", [NT * P, D])
    g.h = scratch("h", [NT * P, D])
    g.row_token = scratch("row_token", [(NBLK + 1) * EB, 1], I32)
    g.yb = scratch("yb", [(NBLK + 1) * EB, D])
    with ExitStack() as late:
        def kept(ctx, name, shape, dt=F32):
            return ctx.enter_context(nc.sbuf_tensor(name, shape, dt))

        g.row_of = kept(late, "row_of", [P, NBLK], I32)
        g.block_expert, g.block_fresh, g.block_buffer = (kept(late, n, [P, NBLK], I32) for n in (
            "block_expert", "block_fresh", "block_buffer"))
        g.dest_i = kept(late, "dest_i", [P, NT, 2], I32)
        g.gate_of = kept(late, "gate_of", [P, NT, 2])
        with ExitStack() as ctx:
            g.conv = kept(ctx, "conv", [P, CB, T])
            with ExitStack() as early:
                g.glu_p = kept(early, "glu_p", [P, CB, HIST + NP])
                g.glu_s = kept(early, "glu_s", [P, CB, DB, HIST + DS])
                g.hist_s = kept(early, "hist_s", [P, CB, DB, HIST])
                g.u = kept(early, "u", [P, KC, TC])
                for phase in PHASES[:4]:
                    phase(nc, g)
            g.lam_p = kept(ctx, "lam_p", [P, NPAIR, NCH - 1])
            g.lam_s = kept(ctx, "lam_s", [P, NPAIR, DB])
            for phase in PHASES[4:6]:
                phase(nc, g)
            g.mixed = kept(ctx, "mixed", [P, NPAIR, T])
            for phase in PHASES[6:8]:
                phase(nc, g)
        for phase in PHASES[8:]:
            phase(nc, g)


def kernel(**inputs):
    import numpy as np
    import concourse.bacc as bacc
    from concourse.bass_utils import run_bass_kernel_spmd

    f = {k: np.asarray(v) for k, v in inputs.items()}
    f = {k: v[0] if k not in ("x_prompt", "x_sample", "final_norm_g") else v for k, v in f.items()}

    def by_channel(v):
        return np.ascontiguousarray(v.reshape(-1, P).T)

    x = np.concatenate([f["x_prompt"][0], f["x_sample"].reshape(NS, D)])
    arrays = {
        "xT": np.ascontiguousarray(np.concatenate([x, f["state_shift"]]).T).reshape(KC, P, TC),
        "norm1": by_channel(f["norm1_g"]),
        "w_in": np.ascontiguousarray(f["w_in"].reshape(KC, P, -1, P).transpose(2, 1, 0, 3)),
        "state_conv": np.ascontiguousarray(f["state_conv"].reshape(DB, HIST, CB, P).transpose(3, 2, 0, 1)),
        "conv_w": np.ascontiguousarray(f["conv_dw_w"].reshape(CK, CB, P).transpose(2, 1, 0)),
        "conv_b": by_channel(f["conv_dw_b"]),
        "mu": by_channel(f["rwkv_mu"]),
        "rwkv_par": np.ascontiguousarray(np.stack(
            [by_channel(f[n]) for n in ("rwkv_w0", "rwkv_a0", "rwkv_k_k", "rwkv_k_a", "rwkv_k_a", "rwkv_r_k")], axis=2)),
        "lora": np.ascontiguousarray(np.stack([
            np.concatenate([f["rwkv_w2"], np.zeros_like(f["rwkv_w2"])]),
            np.concatenate([np.zeros_like(f["rwkv_a2"]), f["rwkv_a2"]]), f["rwkv_g2"]])
            .reshape(3, P, NPAIR, P).transpose(2, 1, 0, 3)),
    }
    arrays |= {
        "norm_par": np.ascontiguousarray(np.stack(
            [by_channel(f["rwkv_gn_g"]), by_channel(f["rwkv_gn_b"]),
             *(np.pad(by_channel(f[n]), ((0, 0), (0, NPAIR - CB))) for n in ("conv_ln_g", "conv_ln_b"))], axis=1)),
        "w_branch": np.ascontiguousarray(np.concatenate([f["rwkv_out_w"], f["conv_out_w"]])
                                         .reshape(KC + CB, P, KC, P).transpose(2, 1, 0, 3)),
        "conv_out_b": by_channel(f["conv_out_b"]),
        "w_o": np.ascontiguousarray(f["w_o"].reshape(KC, P, D).transpose(1, 0, 2)),
        "router_w": np.ascontiguousarray(np.concatenate([f["router_group_w"], f["router_expert_w"]], axis=1)
                                         .reshape(KC, P, NG + NE).transpose(1, 0, 2)),
        "router_b": np.concatenate([f["router_group_b"], f["router_expert_b"]])[None],
        "norm2": f["norm2_g"][None], "norm_f": f["final_norm_g"][None],
        "x": np.concatenate([x, np.zeros((NT * P - T, D), x.dtype)]),
        "w_up": np.ascontiguousarray(np.concatenate([f["expert_w_gate"], f["expert_w_up"]], axis=2)
                                     .reshape(NE, KC, P, 2 * DE).transpose(0, 2, 1, 3)).reshape(NE, P, KC * 2 * DE),
        "w_down": np.ascontiguousarray(f["expert_w_down"].reshape(NE, 2, P, D).transpose(0, 2, 1, 3)).reshape(NE, P, 2 * D),
        "ident": np.eye(P, dtype=np.float32), "earlier": np.triu(np.ones((P, P), np.float32), 1),
    }
    j, t = np.arange(C)[:, None], np.arange(C)[None, :]
    same = j // DS == t // DS
    pair_step = (j % 2 == 0) & (t == j + 1)
    both = lambda m: np.concatenate([m, m]).astype(np.float32)
    arrays |= {
        "masks": np.stack([np.stack([both(-1.0 * (pair_step & s)), both(-1.0 * ((j <= t) & s)), both((j < t) & s),
                                     both((j <= t) & s), both(-1.0 * ((t < j) & s))], axis=1)
                           for s in (same | True, same)], axis=1),
        "doubling": np.stack([both((j // (2 * m) == t // (2 * m)) & (j % (2 * m) < m) & (t % (2 * m) >= m))
                              for m in (2, 4, 8, 16, 32)], axis=1).astype(np.int32),
        "eye": both(j == t),
        "seq": both(j // DS == np.arange(DB)[None, :]),
        "state_s": np.ascontiguousarray(f["state_wkv"].reshape(DB, NPAIR, 2, HD, HD).transpose(2, 4, 1, 0, 3)
                                        .reshape(P, NPAIR, DB, HD)),
    }
    shapes = {
        "y_out": (T, D),
        "wkv_p": (P, NPAIR, HD), "wkv_s": (P, NPAIR, DB, HD),
        "shift_p": (P, KC, 1), "shift_s": (P, KC, DB), "conv_p": (P, CB, HIST), "conv_s": (P, CB, DB, HIST),
    }
    nc = bacc.Bacc("TRN2", target_bir_lowering=False, num_devices=1)
    ins = {k: nc.dram_tensor(f"in_{k}", a.shape, mybir.dt.from_np(a.dtype), kind="ExternalInput").ap()
           for k, a in arrays.items()}
    outs = {k: nc.dram_tensor(f"out_{k}", s, F32, kind="ExternalOutput").ap() for k, s in shapes.items()}
    hybrid_step(nc, ins, outs)
    r = run_bass_kernel_spmd(nc, [{f"in_{k}": a for k, a in arrays.items()}], core_ids=[0])
    o = {k: np.asarray(r.results[0][f"out_{k}"]) for k in shapes}

    def channels_last(v):
        return np.ascontiguousarray(np.moveaxis(v, (1, 0), (-2, -1))).reshape(*v.shape[2:], -1)

    wkv_p = o["wkv_p"].reshape(2, HD, NPAIR, HD).transpose(2, 0, 3, 1).reshape(1, 1, 2 * NPAIR, HD, HD)
    wkv_s = o["wkv_s"].reshape(2, HD, NPAIR, DB, HD).transpose(3, 2, 0, 4, 1).reshape(1, DB, 2 * NPAIR, HD, HD)
    return (o["y_out"][None, :NP], o["y_out"][NP:].reshape(DB, DS, D),
            channels_last(o["conv_p"])[None, None], channels_last(o["shift_p"])[None], np.ascontiguousarray(wkv_p),
            channels_last(o["conv_s"])[None], channels_last(o["shift_s"])[None], np.ascontiguousarray(wkv_s))
```

```python
from contextlib import ExitStack
from math import exp

import concourse.bass as bass
from concourse import mybir

P = 128
D = 1024
KC = D // P
NP = 2048
DB, DS = 8, 8
NS = DB * DS
T = NP + NS
TC = T + DB
CW = D // 2
CB = CW // P
CK = 31
HIST = CK - 1
HD = 64
NPAIR = D // P
C = 64
NCH = T // C
RWB = 26
Q, QW = 5, TC // 5
SEG, SW = 6, T // 6
NG, NE, EPG = 4, 32, 8
DE = 256
EB = 128
NBLK = (2 * T + NE * (EB - 1)) // EB
NT = (T + P - 1) // P

ALU = mybir.AluOpType
ACT = mybir.ActivationFunctionType
AX = mybir.AxisListType
F32 = mybir.dt.float32
F32R = mybir.dt.float32r
I32 = mybir.dt.int32
U32 = mybir.dt.uint32
NORM_EPS, LN_EPS, GN_EPS = 1e-6, 1e-5, 64e-5
ds = bass.ds


class Tensors:

    def __init__(self, ins, outs):
        self.xT, self.norm1, self.w_in, self.state_conv, self.conv_w, self.conv_b = (ins[n] for n in ("xT", "norm1", "w_in", "state_conv", "conv_w", "conv_b"))
        self.mu, self.rwkv_par, self.lora, self.norm_par, self.w_branch, self.conv_out_b = (ins[n] for n in ("mu", "rwkv_par", "lora", "norm_par", "w_branch", "conv_out_b"))
        self.w_o, self.router_w, self.router_b, self.norm2, self.x, self.w_up = (ins[n] for n in ("w_o", "router_w", "router_b", "norm2", "x", "w_up"))
        self.w_down, self.ident, self.masks, self.doubling, self.eye, self.seq = (ins[n] for n in ("w_down", "ident", "masks", "doubling", "eye", "seq"))
        self.state_s, self.norm_f, self.earlier = (ins[n] for n in ("state_s", "norm_f", "earlier"))
        self.y_out, self.wkv_p, self.wkv_s, self.shift_p, self.shift_s, self.conv_p = (outs[n] for n in ("y_out", "wkv_p", "wkv_s", "shift_p", "shift_s", "conv_p"))
        self.conv_s = outs["conv_s"]


class Phase:

    def __init__(self, nc, name):
        self.nc, self.name, self.ctx, self.sems = nc, name, ExitStack(), []

    def __enter__(self):
        return self

    def __exit__(self, *a):
        for s in self.sems:
            self.nc.gpsimd.sem_clear(s)
        self.ctx.close()

    def sb(self, name, shape, dt=F32):
        return self.ctx.enter_context(self.nc.sbuf_tensor(f"{self.name}_{name}", shape, dt))

    def psum(self, name, shape, dt=F32):
        return self.ctx.enter_context(self.nc.psum_tensor(f"{self.name}_{name}", shape, dt))

    def sem(self, name):
        self.sems.append(self.ctx.enter_context(self.nc.semaphore(f"{self.name}_{name}")))
        return self.sems[-1]

    def pool_dma_sem(self, name):
        return self.nc.alloc_semaphore(f"{self.name}_{name}")

    def block(self):
        return self.nc.Block()


def norm_inputs(nc, g):
    with Phase(nc, "norm") as ph:
        ones = ph.sb("ones", [P, P])
        sq = ph.sb("sq", [P, 2, KC, SW])
        ms = ph.sb("ms", [P, 2, SW])
        lms = ph.sb("lms", [P, 2, SW])
        rstd = ph.sb("rstd", [P, 2, SW])
        gain = ph.sb("gain", [P, KC])
        total = ph.psum("total", [P, 2, 512])
        x_loaded = [ph.sem(f"x_loaded{s}") for s in range(SEG)]
        shift_loaded, gain_loaded, out_stored = ph.sem("shift_loaded"), ph.sem("gain_loaded"), ph.sem("out_stored")
        ones_set, squared, summed, ms_ready, lms_ready, rstd_ready, scaled = (
            ph.sem(n) for n in ("ones_set", "squared", "summed", "ms_ready", "lms_ready", "rstd_ready", "scaled"))
        with ph.block() as block:
            @block.sync
            def _(sp):
                for s in range(SEG):
                    cols = slice(s * SW, (s + 1) * SW)
                    sp.dma_start(g.u[:, :, cols], g.xT[:, :, cols].rearrange("k p t -> p k t")).then_inc(x_loaded[s], 16)
                sp.dma_start(g.u[:, :, T:TC], g.xT[:, :, T:TC].rearrange("k p t -> p k t")).then_inc(shift_loaded, 16)
                sp.dma_start(gain[:, :], g.norm1).then_inc(gain_loaded, 16)
                sp.wait_ge(scaled, SEG)
                with nc.allow_non_contiguous_dma(reason="one column per channel"):
                    sp.dma_start(g.shift_p, g.u[:, :, NP - 1:NP]).then_inc(out_stored, 16)
                    for kc in range(KC):
                        sp.dma_start(g.shift_s[:, kc], g.u[:, kc, NP + DS - 1:T:DS]).then_inc(out_stored, 16)
                sp.wait_ge(out_stored, 16 * (1 + KC))
                sp.wait_ge(shift_loaded, 16)

            @block.scalar
            def _(act):
                def square(s):
                    act.wait_ge(x_loaded[s], 16)
                    if s >= 2:
                        act.wait_ge(summed, s - 1)
                    act.activation(sq[:, s % 2], g.u[:, :, s * SW:(s + 1) * SW], ACT.Square).then_inc(squared, 1)

                square(0)
                for s in range(SEG):
                    if s + 1 < SEG:
                        square(s + 1)
                    act.wait_ge(ms_ready, s + 1)
                    act.activation(lms[:, s % 2], ms[:, s % 2], ACT.Ln).then_inc(lms_ready, 1)
                    act.wait_ge(lms_ready, s + 1)
                    act.activation(rstd[:, s % 2], lms[:, s % 2], ACT.Exp, scale=-0.5).then_inc(rstd_ready, 1)

            @block.tensor
            def _(pe):
                pe.wait_ge(ones_set, 1)
                for s in range(SEG):
                    pe.wait_ge(squared, s + 1)
                    if s >= 2:
                        pe.wait_ge(ms_ready, s - 1)
                    for kc in range(KC):
                        mm = pe.matmul(total[:, s % 2, 0:SW], ones[:, :], sq[:, s % 2, kc], start=kc == 0, stop=kc == KC - 1)
                    mm.then_inc(summed, 1)

            @block.vector
            def _(dve):
                dve.memset(ones[:, :], 1.0).then_inc(ones_set, 1)
                dve.wait_ge(gain_loaded, 16)

                def mean_square(s):
                    dve.wait_ge(summed, s + 1)
                    if s >= 2:
                        dve.wait_ge(rstd_ready, s - 1)
                    dve.tensor_scalar(ms[:, s % 2], total[:, s % 2, 0:SW], 1.0 / D, NORM_EPS, ALU.mult, ALU.add).then_inc(ms_ready, 1)

                mean_square(0)
                for s in range(SEG):
                    if s + 1 < SEG:
                        mean_square(s + 1)
                    dve.wait_ge(x_loaded[s], 16)
                    dve.wait_ge(rstd_ready, s + 1)
                    for kc in range(KC):
                        cols = g.u[:, kc, s * SW:(s + 1) * SW]
                        op = dve.scalar_tensor_tensor(cols, cols, gain[:, kc:kc + 1], rstd[:, s % 2], ALU.mult, ALU.mult)
                    op.then_inc(scaled, 1)


def project_block(pe, bank, w, u, waits, bank_ready):
    for q in range(Q):
        waits(q)
        for kc in range(KC):
            mm = pe.matmul(bank[:, q, 0:QW], w[:, kc, :], u[:, kc, q * QW:(q + 1) * QW],
                           start=kc == 0, stop=kc == KC - 1)
        mm.then_inc(bank_ready, 1)


def project_glu(nc, g):
    with Phase(nc, "glu") as ph:
        w = ph.sb("w", [P, 2, KC, P])
        sig = ph.sb("sig", [P, TC])
        bank = ph.psum("bank", [P, Q, 512])
        w_loaded = [ph.sem("gate_w_loaded"), ph.sem("value_w_loaded")]
        gate_ready, value_ready, sig_ready, glu_ready, zeroed, hist_loaded, stored = (
            ph.sem(n) for n in ("gate_ready", "value_ready", "sig_ready", "glu_ready", "zeroed",
                                "hist_loaded", "stored"))
        last = Q - 1
        tail = NP - last * QW
        with ph.block() as block:
            @block.sync
            def _(sp):
                sp.dma_start(g.hist_s[:, :, :, :], g.state_conv).then_inc(hist_loaded, 16)
                with sp.Fori(0, CB) as cb:
                    for u in range(2):
                        sp.wait_ge((gate_ready, value_ready)[u], cb * Q + 1)
                        sp.dma_start(w[:, u], g.w_in[ds(cb + CB * (1 - u), 1)].rearrange("a p k c -> p (a k) c")).then_inc(w_loaded[u], 16)
                sp.wait_ge(glu_ready, Q * CB + Q)
                sp.wait_ge(hist_loaded, 16)
                sp.wait_ge(zeroed, 2)
                with nc.allow_non_contiguous_dma(reason="the last 30 rows of each sequence"):
                    sp.dma_start(g.conv_p, g.glu_p[:, :, NP:NP + HIST]).then_inc(stored, 16)
                    for cb in range(CB):
                        sp.dma_start(g.conv_s[:, cb], g.glu_s[:, cb, :, DS:DS + HIST]).then_inc(stored, 16)
                sp.wait_ge(stored, 16 * (1 + CB))

            @block.tensor
            def _(pe):
                pe.sem_inc(gate_ready, 1)
                pe.sem_inc(value_ready, 1)
                with pe.Fori(0, CB) as cb:
                    pe.wait_ge(w_loaded[0], cb * 16 + 16)
                    project_block(pe, bank, w[:, 0], g.u, lambda q: pe.wait_ge(glu_ready, cb * Q + (q + 1)), gate_ready)
                    pe.wait_ge(w_loaded[1], cb * 16 + 16)
                    project_block(pe, bank, w[:, 1], g.u, lambda q: pe.wait_ge(sig_ready, cb * Q + (q + 1)), value_ready)

            @block.scalar
            def _(act):
                with act.Fori(0, CB) as cb:
                    for q in range(Q):
                        act.wait_ge(gate_ready, cb * Q + (q + 2))
                        act.wait_ge(glu_ready, cb * Q + (q + 1))
                        act.activation(sig[:, q * QW:(q + 1) * QW], bank[:, q, 0:QW], ACT.Sigmoid).then_inc(sig_ready, 1)

            @block.vector
            def _(dve):
                dve.sem_inc(glu_ready, Q)
                dve.memset(g.glu_p[:, :, 0:HIST], 0.0).then_inc(zeroed, 1)
                dve.wait_ge(hist_loaded, 16)
                dve.tensor_copy(g.glu_s[:, :, :, 0:HIST], g.hist_s[:, :, :, :]).then_inc(zeroed, 1)
                with dve.Fori(0, CB) as cb:
                    for q in range(Q):
                        dve.wait_ge(value_ready, cb * Q + (q + 2))
                        dve.wait_ge(sig_ready, cb * Q + (q + 1))
                        n = tail if q == last else QW
                        s0 = q * QW
                        op = dve.tensor_tensor(g.glu_p[:, ds(cb, 1), HIST + s0:HIST + s0 + n].rearrange("p a n -> p (a n)"),
                                               bank[:, q, 0:n], sig[:, s0:s0 + n], ALU.mult)
                        if q == last:
                            op = dve.tensor_tensor(
                                g.glu_s[:, ds(cb, 1), :, HIST:HIST + DS].rearrange("p a b n -> p (a b) n"),
                                bank[:, q, n:n + NS].rearrange("p (b n) -> p b n", n=DS),
                                sig[:, NP:T].rearrange("p (b n) -> p b n", n=DS), ALU.mult)
                        op.then_inc(glu_ready, 1)


def project_rwkv(nc, g):
    with Phase(nc, "mix") as ph:
        w = ph.sb("w", [P, 2, KC, P])
        row = ph.sb("row", [P, 2, 1 + TC])
        diff = ph.sb("diff", [P, 2, T])
        xm = ph.sb("xm", [P, 2, T])
        mu = ph.sb("mu", [P, RWB])
        bank = ph.psum("bank", [P, Q, 512])
        w_loaded = [ph.sem("w_loaded0"), ph.sem("w_loaded1")]
        xm_stored, xm_free = ph.pool_dma_sem("xm_stored"), ph.sem("xm_free")
        bank_ready = [ph.sem("bank_ready0"), ph.sem("bank_ready1")]
        row_ready, zeroed, mu_loaded, shifted, xm_ready, diff_ready, seq_ready = (
            ph.sem(n) for n in ("row_ready", "zeroed", "mu_loaded", "shifted",
                                "xm_ready", "diff_ready", "seq_ready"))
        with ph.block() as block:
            @block.sync
            def _(sp):
                sp.dma_start(mu[:, :], g.mu).then_inc(mu_loaded, 16)
                with sp.Fori(0, RWB // 2) as i:
                    for u in range(2):
                        sp.wait_ge(bank_ready[u], i * Q + 1)
                        sp.dma_start(w[:, u], g.w_in[ds(i * 2 + (u + 2 * CB), 1)].rearrange("a p k c -> p (a k) c")).then_inc(w_loaded[u], 16)

            @block.tensor
            def _(pe):
                pe.sem_inc(bank_ready[0], 1)
                pe.sem_inc(bank_ready[1], 1)
                with pe.Fori(0, RWB // 2) as i:
                    for u in range(2):
                        pe.wait_ge(w_loaded[u], i * 16 + 16)
                        project_block(pe, bank, w[:, u], g.u,
                                      lambda q: pe.wait_ge(row_ready, i * (2 * Q) + (u * Q + q + 1)), bank_ready[u])

            @block.scalar
            def _(act):
                act.sem_inc(row_ready, Q)
                act.wait_ge(zeroed, 1)
                with act.Fori(0, RWB // 2) as i:
                    for u in range(2):
                        act.wait_ge(xm_ready, i * 2 + (u + 1))
                        for q in range(Q):
                            act.wait_ge(bank_ready[u], i * Q + (q + 2))
                            act.copy(row[:, u, 1 + q * QW:1 + (q + 1) * QW], bank[:, q, 0:QW]).then_inc(row_ready, 1)

            @block.vector
            def _(dve):
                dve.sem_inc(xm_ready, 2)
                dve.memset(row[:, :, 0:1], 0.0).then_inc(zeroed, 1)
                dve.wait_ge(mu_loaded, 16)
                dve.wait_ge(zeroed, 1)
                with dve.Fori(0, RWB // 2) as i:
                    for u in range(2):
                        n = i * 2 + u
                        dve.wait_ge(row_ready, n * Q + 2 * Q)
                        now = row[:, u, 1:1 + T]
                        dve.tensor_tensor(diff[:, u], row[:, u, 0:T], now, ALU.subtract).then_inc(diff_ready, 1)
                        dve.wait_ge(diff_ready, n + 1)
                        dve.tensor_tensor(diff[:, u, NP:T:DS], row[:, u, 1 + T:1 + TC], row[:, u, 1 + NP:1 + T:DS],
                                          ALU.subtract).then_inc(seq_ready, 1)
                        dve.wait_ge(seq_ready, n + 1)
                        dve.wait_ge(xm_free, n + 1)
                        dve.scalar_tensor_tensor(xm[:, u], diff[:, u], mu[:, ds(n, 1)], now, ALU.mult, ALU.add).then_inc(xm_ready, 1)

            @block.gpsimd
            def _(pool):
                pool.sem_inc(xm_free, 2)
                with pool.Fori(0, RWB // 2) as i:
                    for u in range(2):
                        pool.wait_ge(xm_ready, i * 2 + (u + 3))
                        pool.dma_start(g.xm[ds(i * 2 + u, 1)].rearrange("a p t -> p (a t)"), xm[:, u]).then_inc(xm_stored, 16)
                        pool.wait_ge(xm_stored, i * 32 + (u + 1) * 16)
                        pool.sem_inc(xm_free, 1)


def project_gates(nc, g):
    with Phase(nc, "gate") as ph:
        w = ph.sb("w", [P, 2, KC, P])
        row = ph.sb("row", [P, 2, T])
        taps = ph.sb("taps", [P, CB, CK])
        bias = ph.sb("bias", [P, CB])
        bank = ph.psum("bank", [P, Q, 512])
        w_loaded = [ph.sem("w_loaded0"), ph.sem("w_loaded1")]
        row_stored, row_free = ph.pool_dma_sem("row_stored"), ph.sem("row_free")
        bank_ready = [ph.sem("bank_ready0"), ph.sem("bank_ready1")]
        row_ready, taps_loaded, tapped = (
            ph.sem(n) for n in ("row_ready", "taps_loaded", "tapped"))
        NB = 2 * KC
        with ph.block() as block:
            @block.sync
            def _(sp):
                sp.dma_start(taps[:, :, :], g.conv_w).then_inc(taps_loaded, 16)
                sp.dma_start(bias[:, :], g.conv_b).then_inc(taps_loaded, 16)
                with sp.Fori(0, NB // 2) as i:
                    for u in range(2):
                        sp.wait_ge(bank_ready[u], i * Q + 1)
                        sp.dma_start(w[:, u], g.w_in[ds(i * 2 + (u + 2 * CB + RWB), 1)].rearrange("a p k c -> p (a k) c")).then_inc(w_loaded[u], 16)

            @block.tensor
            def _(pe):
                pe.sem_inc(bank_ready[0], 1)
                pe.sem_inc(bank_ready[1], 1)
                with pe.Fori(0, NB // 2) as i:
                    for u in range(2):
                        pe.wait_ge(w_loaded[u], i * 16 + 16)
                        project_block(pe, bank, w[:, u], g.u,
                                      lambda q: pe.wait_ge(row_ready, i * (2 * Q) + (u * Q + q + 1)), bank_ready[u])

            @block.scalar
            def _(act):
                act.sem_inc(row_ready, Q)
                with act.Fori(0, NB // 2) as i:
                    for u in range(2):
                        act.wait_ge(row_free, i * 2 + (u + 1))
                        for q in range(Q):
                            n = min(QW, T - q * QW)
                            act.wait_ge(bank_ready[u], i * Q + (q + 2))
                            act.activation(row[:, u, q * QW:q * QW + n], bank[:, q, 0:n], ACT.Sigmoid).then_inc(row_ready, 1)

            @block.vector
            def _(dve):
                dve.wait_ge(taps_loaded, 32)
                with dve.Fori(0, CB) as cb:
                    def full(j, sample):
                        if sample:
                            return g.glu_s[:, ds(cb, 1), :, ds(j, DS)].rearrange("p a b n -> p (a b) n")
                        return g.glu_p[:, ds(cb, 1), ds(j, NP)].rearrange("p a n -> p (a n)")

                    acc_p = g.conv[:, ds(cb, 1), 0:NP].rearrange("p a n -> p (a n)")
                    acc_s = g.conv[:, ds(cb, 1), NP:T].rearrange("p a (b n) -> p (a b) n", n=DS)
                    for acc, sample in ((acc_p, 0), (acc_s, 1)):
                        dve.tensor_scalar(acc, full(0, sample), taps[:, ds(cb, 1), 0], bias[:, ds(cb, 1)],
                                          ALU.mult, ALU.add).then_inc(tapped, 1)
                    with dve.Fori(0, HIST) as j:
                        for acc, sample in ((acc_p, 0), (acc_s, 1)):
                            dve.wait_ge(tapped, cb * (2 * CK) + j * 2 + (sample + 1))
                            dve.scalar_tensor_tensor(acc, full(j + 1, sample), taps[:, ds(cb, 1), ds(j + 1, 1)].rearrange("p a j -> p (a j)"),
                                                     acc, ALU.mult, ALU.add).then_inc(tapped, 1)

            @block.gpsimd
            def _(pool):
                pool.sem_inc(row_free, 2)
                with pool.Fori(0, NB // 2) as i:
                    for u in range(2):
                        pool.wait_ge(row_ready, i * (2 * Q) + (u + 2) * Q)
                        pool.dma_start(g.gates[ds(i * 2 + u, 1)].rearrange("a p t -> p (a t)"), row[:, u]).then_inc(row_stored, 16)
                        pool.wait_ge(row_stored, i * 32 + (u + 1) * 16)
                        pool.sem_inc(row_free, 1)


def prepare_recurrence(nc, g):
    with Phase(nc, "prep") as ph:
        lora_in = ph.sb("lora_in", [P, T])
        gate_in = ph.sb("gate_in", [P, T])
        keep = ph.sb("keep", [P, T])
        rows = {n: ph.sb(n, [P, T]) for n in
                ("r", "k", "v", "W", "L", "X1", "X2", "X3", "A", "N", "KK", "G", "RK", "B")}
        r, k, v, W, L, X1, X2, X3, A, N, KK, G, RK, B = rows.values()
        heads = ph.sb("heads", [P, P])
        lora_w = ph.sb("lora_w", [P, 3, P])
        par = ph.sb("par", [P, NPAIR + 1, 6])
        first, second = ph.sb("first", [P, 3]), ph.sb("second", [P, 3])
        lora_bank = ph.psum("lora_bank", [P, 3, 2, 512])
        head_bank = ph.psum("head_bank", [P, 2, 512])
        r_loaded, k_loaded, v_loaded = ([ph.pool_dma_sem(f"{n}_loaded{u}") for u in range(2)] for n in "rkv")
        lora_loaded, par_loaded, in_loaded = (ph.pool_dma_sem(n) for n in ("lora_loaded", "par_loaded", "in_loaded"))
        consts_set, in_ready, keep_set, first_ready, second_ready = (ph.sem(n) for n in (
            "consts_set", "in_ready", "keep_set", "first_ready", "second_ready"))
        g_stored, alpha_stored, rho_stored, beta_stored, kappa_stored, bonus_stored = stores = [
            [ph.sem(f"{n}_stored{u}") for u in range(2)] for n in ("g", "alpha", "rho", "beta", "kappa", "bonus")]
        sq_ready, lw_ready, sum_ready, before_ready, kk0_ready, rn_ready, kk_ready, t1_ready, kp_ready, b_ready, \
            lam_ready, lam_before_ready, lam_inv_ready, alpha_ready, rho_ready, rk_ready, kappa_ready, beta_ready, \
            ends_ready, ln_ready = credit = [ph.sem(n) for n in (
                "sq_ready", "lw_ready", "sum_ready", "before_ready", "kk0_ready", "rn_ready", "kk_ready", "t1_ready",
                "kp_ready", "b_ready", "lam_ready", "lam_before_ready", "lam_inv_ready", "alpha_ready", "rho_ready",
                "rk_ready", "kappa_ready", "beta_ready", "ends_ready", "ln_ready")]
        lora_done, lora_read, head_done, head_read = (
            ph.sem(n) for n in ("lora_done", "lora_read", "head_done", "head_read"))
        CUT = (NCH // 2 + 1) * C
        part = [slice(0, CUT), slice(CUT, T)]
        NSEG = 3
        SQ, BONUS, SUMS = 0, 2 * NSEG, 4 * NSEG

        def head_sum(kind, u, s):
            return kind + u * NSEG + s

        seg = [[slice(0, 384), slice(384, 736), slice(736, CUT)], [slice(CUT, CUT + 352), slice(CUT + 352, CUT + 704), slice(CUT + 704, T)]]

        with ph.block() as block:
            @block.gpsimd
            def _(pool):
                pool.dma_start(par[:, 0:NPAIR, :], g.rwkv_par).then_inc(par_loaded, 16)
                pool.dma_start(lora_in[:, :], g.xm[RWB - 2]).then_inc(in_loaded, 16)
                pool.dma_start(gate_in[:, :], g.xm[RWB - 1]).then_inc(in_loaded, 16)
                with pool.Fori(0, NPAIR) as p:
                    pool.wait_ge(lora_done, p * (2 * NSEG) + 1)
                    pool.dma_start(lora_w[:, :, :], g.lora[ds(p, 1)].rearrange("a p k c -> p (a k) c")).then_inc(lora_loaded, 16)
                    for u in range(2):
                        i = p * 2 + u
                        for x, loaded, b0, uses in ((k, k_loaded, NPAIR, (rk_ready, kappa_ready, sq_ready)),
                                                    (r, r_loaded, 0, (rk_ready, rho_ready))):
                            for s in uses:
                                pool.wait_ge(s, i + 1)
                            pool.dma_start(x[:, part[u]], g.xm[ds(p + b0, 1), :, part[u]].rearrange("a p t -> p (a t)")).then_inc(loaded[u], 16)
                        pool.wait_ge(head_read, p * SUMS + head_sum(BONUS, u, NSEG))
                        pool.dma_start(v[:, part[u]], g.xm[ds(p + 2 * NPAIR, 1), :, part[u]].rearrange("a p t -> p (a t)")).then_inc(v_loaded[u], 16)

            @block.sync
            def _(sp):
                for stored in stores:
                    for s in stored:
                        sp.sem_inc(s, 16)
                with sp.Fori(0, NPAIR) as p:
                    for u in range(2):
                        i = p * 2 + u
                        chunks = slice(part[u].start // C, part[u].stop // C)
                        sp.wait_ge(lora_read, i * NSEG + (NSEG + 2))
                        sp.dma_start(g.go[ds(p, 1), :, part[u]].rearrange("a p t -> p (a t)"), G[:, part[u]]).then_inc(g_stored[u], 16)
                    for u in range(2):
                        i = p * 2 + u
                        chunks = slice(part[u].start // C, part[u].stop // C)
                        for ready, n, x, stored in ((alpha_ready, 0, X1, alpha_stored), (rho_ready, 1, X2, rho_stored),
                                                    (beta_ready, 2, A, beta_stored), (kappa_ready, 3, X3, kappa_stored)):
                            sp.wait_ge(ready, i + 3)
                            sp.dma_start(g.zc[chunks, :, n, ds(p, 1), :].rearrange("c p a t -> p c (a t)"),
                                         x[:, part[u]].rearrange("p (c t) -> p c t", t=C)).then_inc(stored[u], 16)
                        sp.wait_ge(head_read, p * SUMS + (SUMS + head_sum(BONUS, u, NSEG)))
                        sp.dma_start(g.bonus[ds(p, 1), :, part[u]].rearrange("a p t -> p (a t)"), B[:, part[u]]).then_inc(bonus_stored[u], 16)
                for stored in stores:
                    for s in stored:
                        sp.wait_ge(s, 16 + 16 * NPAIR)

            @block.tensor
            def _(pe):
                pe.sem_inc(lora_done, 1)
                pe.sem_inc(head_done, SUMS)
                pe.wait_ge(consts_set, 3)
                pe.wait_ge(in_ready, 2)

                def lora(p, u):
                    if u == 0:
                        pe.wait_ge(lora_loaded, p * 16 + 16)
                    for s in range(NSEG):
                        cols, n = seg[u][s], seg[u][s].stop - seg[u][s].start
                        pe.wait_ge(lora_read, p * (2 * NSEG) + (u * NSEG + s + 1))
                        for j, x in enumerate((lora_in, lora_in, gate_in)):
                            mm = pe.matmul(lora_bank[:, j, (u + s) % 2, 0:n], lora_w[:, j, :], x[:, cols], start=True, stop=True)
                        mm.then_inc(lora_done, 1)

                def sums(p, u, kind, ready):
                    pe.wait_ge(ready, p * 2 + (u + 3))
                    for s in range(NSEG):
                        k = head_sum(kind, u, s)
                        cols, n = seg[u][s], seg[u][s].stop - seg[u][s].start
                        pe.wait_ge(head_read, p * SUMS + (SUMS + k - 1))
                        pe.matmul(head_bank[:, k % 2, 0:n], heads[:, :], RK[:, cols], start=True, stop=True).then_inc(head_done, 1)

                def pair(p, more=True):
                    sums(p, 0, BONUS, rk_ready)
                    if more:
                        lora(p + 1, 0)
                    sums(p, 1, BONUS, rk_ready)
                    if more:
                        sums(p + 1, 0, SQ, sq_ready)
                        lora(p + 1, 1)
                        sums(p + 1, 1, SQ, sq_ready)

                for u in range(2):
                    lora(0, u)
                    sums(0, u, SQ, sq_ready)
                with pe.Fori(0, NPAIR - 1) as p:
                    pair(p)
                pair(NPAIR - 1, more=False)

            @block.scalar
            def _(act):
                for s in (sq_ready, lam_ready, lam_before_ready, lam_inv_ready, rn_ready, ln_ready):
                    act.sem_inc(s, 2)
                act.sem_inc(lora_read, 2)
                act.wait_ge(in_loaded, 32)
                act.activation(lora_in[0:C, :], lora_in[0:C, :], ACT.Tanh).then_inc(in_ready, 1)
                act.activation(gate_in[:, :], gate_in[:, :], ACT.Sigmoid).then_inc(in_ready, 1)
                with act.Fori(0, NPAIR) as p:
                    act.wait_ge(first_ready, p + 1)
                    for u in range(2):
                        i = p * 2 + u
                        act.wait_ge(kp_ready, i + 1)
                        act.wait_ge(beta_stored[u], p * 16 + 16)
                        act.wait_ge(g_stored[u], p * 16 + 16)
                        for s in range(NSEG):
                            cols, n, at = seg[u][s], seg[u][s].stop - seg[u][s].start, (u + s) % 2
                            act.wait_ge(lora_done, i * NSEG + (s + 2))
                            act.activation(W[:, cols], lora_bank[:, 0, at, 0:n], ACT.Sigmoid, bias=first[:, 0:1])
                            act.activation(A[:, cols], lora_bank[:, 1, at, 0:n], ACT.Sigmoid, bias=first[:, 1:2])
                            act.copy(G[:, cols], lora_bank[:, 2, at, 0:n]).then_inc(lora_read, 1)
                        act.wait_ge(k_loaded[u], p * 16 + 16)
                        act.wait_ge(head_done, p * SUMS + head_sum(BONUS, u, NSEG))
                        act.activation(RK[:, part[u]], k[:, part[u]], ACT.Square, scale=first[:, 2:3]).then_inc(sq_ready, 1)
                    for u in range(2):
                        i = p * 2 + u
                        act.wait_ge(head_read, p * SUMS + (SUMS + head_sum(SQ, u, NSEG)))
                        act.activation(N[:, part[u]], N[:, part[u]], ACT.Ln, scale=2.0 ** 30).then_inc(ln_ready, 1)
                        act.wait_ge(ln_ready, i + 3)
                        act.activation(N[:, part[u]], N[:, part[u]], ACT.Exp, scale=-0.5).then_inc(rn_ready, 1)
                        act.wait_ge(before_ready, i + 3)
                        act.activation(X1[:, part[u]], X1[:, part[u]], ACT.Exp).then_inc(lam_before_ready, 1)
                        act.wait_ge(rho_stored[u], p * 16 + 16)
                        act.activation(X2[:, part[u]], L[:, part[u]], ACT.Exp).then_inc(lam_ready, 1)
                        act.wait_ge(kappa_stored[u], p * 16 + 16)
                        act.activation(X3[:, part[u]], L[:, part[u]], ACT.Exp, scale=-1.0).then_inc(lam_inv_ready, 1)

            @block.vector
            def _(dve):
                for s in credit:
                    if s not in (sq_ready, lam_ready, lam_before_ready, lam_inv_ready, rn_ready, ln_ready):
                        dve.sem_inc(s, 2)
                dve.sem_inc(head_read, SUMS)
                dve.memset(par[:, NPAIR, :], 0.0).then_inc(keep_set, 1)
                dve.memset(heads[:, :], 0.0).then_inc(consts_set, 1)
                dve.wait_ge(consts_set, 1)
                for h in range(2):
                    o = dve.memset(heads[h * HD:(h + 1) * HD, h * HD:(h + 1) * HD], 1.0).then_inc(consts_set, 1)
                dve.memset(keep[:, :], 1.0).then_inc(keep_set, 1)
                dve.wait_ge(keep_set, 2)
                dve.memset(keep[:, 0:NP:C], 0.0)
                dve.memset(keep[:, NP:T:DS], 0.0).then_inc(keep_set, 1)
                dve.wait_ge(par_loaded, 16)
                dve.tensor_scalar(par[:, 0:NPAIR, 4], par[:, 0:NPAIR, 3], -1.0, 1.0, ALU.mult, ALU.add).then_inc(keep_set, 1)
                dve.wait_ge(keep_set, 4)
                dve.tensor_copy(first[:, :], par[:, 0, 0:3]).then_inc(first_ready, 1)
                with dve.Fori(0, NPAIR) as p:
                    pd = ds(p, 1)
                    for u in range(2):
                        i, h = p * 2 + u, part[u]
                        dve.wait_ge(lora_read, i * NSEG + (NSEG + 2))
                        dve.tensor_scalar(W[:, h], W[:, h], -exp(-0.5), None, ALU.mult).then_inc(lw_ready, 1)
                        dve.wait_ge(lw_ready, i + 3)
                        dve.tensor_tensor_scan(L[:, h], keep[:, h], W[:, h], 0.0, ALU.mult, ALU.add).then_inc(sum_ready, 1)
                        dve.wait_ge(sum_ready, i + 3)
                        dve.wait_ge(alpha_stored[u], p * 16 + 16)
                        dve.tensor_tensor(X1[:, h], L[:, h], W[:, h], ALU.subtract).then_inc(before_ready, 1)
                        dve.wait_ge(k_loaded[u], p * 16 + 16)
                        dve.wait_ge(first_ready, p + 1)
                        dve.tensor_scalar(KK[:, h], k[:, h], first[:, 2:3], 2.0 ** 15, ALU.mult, ALU.mult).then_inc(kk0_ready, 1)
                        for s in range(NSEG):
                            cols, n = seg[u][s], seg[u][s].stop - seg[u][s].start
                            at = head_sum(SQ, u, s)
                            dve.wait_ge(head_done, p * SUMS + (SUMS + at + 1))
                            dve.tensor_scalar(N[:, cols], head_bank[:, at % 2, 0:n], 1e-24, None, ALU.max).then_inc(head_read, 1)
                    dve.tensor_copy(second[:, :], par[:, pd, 3:6].rearrange("p a n -> p (a n)")).then_inc(second_ready, 1)
                    dve.tensor_copy(first[:, :], par[:, ds(p + 1, 1), 0:3].rearrange("p a n -> p (a n)")).then_inc(first_ready, 1)
                    dve.wait_ge(second_ready, p + 1)
                    for u in range(2):
                        i, h = p * 2 + u, part[u]

                        def this(s):
                            dve.wait_ge(s, i + 3)
                        this(before_ready)
                        dve.tensor_scalar(W[:, h], A[:, h], second[:, 0:1], second[:, 1:2], ALU.mult, ALU.add).then_inc(t1_ready, 1)
                        this(t1_ready)
                        dve.tensor_tensor(k[:, h], k[:, h], W[:, h], ALU.mult).then_inc(kp_ready, 1)
                        this(rn_ready)
                        this(kk0_ready)
                        dve.tensor_tensor(KK[:, h], KK[:, h], N[:, h], ALU.mult).then_inc(kk_ready, 1)
                        this(kk_ready)
                        dve.tensor_tensor(A[:, h], A[:, h], KK[:, h], ALU.mult).then_inc(b_ready, 1)
                        this(kp_ready)
                        dve.wait_ge(r_loaded[u], p * 16 + 16)
                        dve.scalar_tensor_tensor(RK[:, h], r[:, h], second[:, 2:3], k[:, h], ALU.mult, ALU.mult).then_inc(rk_ready, 1)
                        this(lam_before_ready)
                        dve.tensor_tensor(X1[:, h], X1[:, h], KK[:, h], ALU.mult).then_inc(alpha_ready, 1)
                        this(lam_ready)
                        if u == 0:
                            dve.tensor_copy(g.lam_p[:, pd, 0:CUT // C].rearrange("p a c -> p (a c)"), X2[:, C - 1:CUT:C]).then_inc(ends_ready, 1)
                        else:
                            dve.tensor_copy(g.lam_p[:, pd, CUT // C:].rearrange("p a c -> p (a c)"), X2[:, CUT + C - 1:NP:C])
                            dve.tensor_copy(g.lam_s[:, pd, :].rearrange("p a c -> p (a c)"), X2[:, NP + DS - 1:T:DS]).then_inc(ends_ready, 1)
                        this(ends_ready)
                        dve.tensor_tensor(X2[:, h], X2[:, h], r[:, h], ALU.mult).then_inc(rho_ready, 1)
                        this(lam_inv_ready)
                        this(b_ready)
                        dve.tensor_tensor(A[:, h], A[:, h], X3[:, h], ALU.mult).then_inc(beta_ready, 1)
                        this(beta_ready)
                        dve.tensor_tensor(X3[:, h], X3[:, h], k[:, h], ALU.mult).then_inc(kappa_ready, 1)
                        dve.wait_ge(v_loaded[u], p * 16 + 16)
                        dve.wait_ge(bonus_stored[u], p * 16 + 16)
                        for s in range(NSEG):
                            cols, n = seg[u][s], seg[u][s].stop - seg[u][s].start
                            at = head_sum(BONUS, u, s)
                            dve.wait_ge(head_done, p * SUMS + (SUMS + at + 1))
                            dve.tensor_tensor(B[:, cols], head_bank[:, at % 2, 0:n], v[:, cols], ALU.mult).then_inc(head_read, 1)


def recurrence(nc, g):
    LEVELS = 5
    with Phase(nc, "wkv") as ph:
        z = ph.sb("z", [P, 2, 4, NPAIR, C])
        rho = ph.sb("rho", [P, 2, NPAIR, C])
        v = ph.sb("v", [P, 2, NPAIR, C])
        masks = ph.sb("masks", [P, 2, 5, C])
        doubling = ph.sb("doubling", [P, LEVELS, C], I32)
        eye = ph.sb("eye", [P, C])
        ident = ph.sb("ident", [P, P])
        seq = ph.sb("seq", [P, DB])
        state = ph.sb("state", [P, NPAIR, HD])
        grown = ph.sb("grown", [P, NPAIR, HD])
        tt = ph.sb("tt", [P, NPAIR, C])
        zt = ph.sb("zt", [P, NPAIR, C])
        ws = ph.sb("ws", [P, NPAIR, HD])
        us = ph.sb("us", [P, NPAIR, HD])
        qt, rt, vt = (ph.sb(n, [P, 2, NPAIR, C]) for n in ("qt", "rt", "vt"))
        ys = ph.sb("ys", [P, 2, NPAIR, C])
        BD = [P, NPAIR, 2, C]
        beta_bd, kappa_bd, v_bd, a_bd, t_bd, u_bd, state_bd = single = [
            ph.sb(n, BD) for n in ("beta_bd", "kappa_bd", "v_bd", "a_bd", "t_bd", "u_bd", "state_bd")]
        alpha_bd, bt_bd, tt_bd, vt_bd, betat_bd, kappat_bd = double = [
            ph.sb(n, [P, 2] + BD[1:]) for n in ("alpha_bd", "bt_bd", "tt_bd", "vt_bd", "betat_bd", "kappat_bd")]
        bank = ph.psum("bank", [P, 8, NPAIR, C])
        states_s = ph.sb("states_s", [P, NPAIR, DB, HD])
        picked = ph.sb("picked", [P, DB, HD])
        read_s = ph.sb("read_s", [P, NPAIR, HD])
        T_BANK, Z_BANK, X_BANK, TURN_BANK, W_BANK, YS_BANK = 0, 2, 3, 4, 6, 7

        z_loaded, v_loaded = ([ph.sem(f"{n}_loaded{u}") for u in range(2)] for n in ("z", "v"))
        y_stored = [ph.sem("y_stored0"), ph.sem("y_stored1")]
        rho_loaded = [ph.sem("rho_loaded0"), ph.sem("rho_loaded1")]
        tt_bd_ready = [ph.sem("tt_bd_ready0"), ph.sem("tt_bd_ready1")]
        consts_loaded, state_stored, cleared, expanded, aq_done, br_done, a_done, vt_done, betat_done, kappat_done, \
            t_done, z_done, x_done, tt_ready, q_ready, br_ready, a_ready, vt_ready, betat_ready, kappat_ready, \
            t_ready, z_ready, vt_bd_ready, w_done, w_ready, u_done, u_ready, u_bd_ready, y_done, y_ready, \
            s_done, grown_ready, state_ready, state_bd_ready, cross_done, masked, cross_read, cross_picked, masked_tt, bv_ready = (
                ph.sem(n) for n in (
                    "consts_loaded", "state_stored", "cleared", "expanded", "aq_done", "br_done", "a_done", "vt_done",
                    "betat_done", "kappat_done", "t_done", "z_done", "x_done", "tt_ready", "q_ready", "br_ready",
                    "a_ready", "vt_ready", "betat_ready", "kappat_ready", "t_ready", "z_ready",
                    "vt_bd_ready", "w_done", "w_ready", "u_done", "u_ready", "u_bd_ready", "y_done", "y_ready",
                    "s_done", "grown_ready", "state_ready", "state_bd_ready", "cross_done", "masked", "cross_read",
                    "cross_picked", "masked_tt", "bv_ready"))
        half = [slice(0, HD), slice(HD, P)]
        NPC = NCH - 1

        def spread(copy, dst, src):
            copy(dst[half[0], :, 0, :], src[half[0]])
            return copy(dst[half[1], :, 1, :], src[half[1]])

        def over_pairs(m, n=NPAIR):
            return m.unsqueeze(1).to_broadcast([m.shape[0], n, m.shape[1]])
        passed, dve_passed = ph.sem("passed"), ph.sem("dve_passed")

        with ph.block() as block:
            @block.sync
            def _(sp):
                for dst, src in ((masks, g.masks), (doubling, g.doubling), (eye, g.eye), (seq, g.seq), (states_s, g.state_s), (ident, g.ident)):
                    sp.dma_start(dst[:], src).then_inc(consts_loaded, 16)
                sp.sem_inc(y_stored[0], 16)
                sp.sem_inc(y_stored[1], 16)

                def load(c, u):
                    sp.wait_ge(expanded, c + 1)
                    sp.wait_ge(a_done, c + 1)
                    sp.dma_start(z[:, u].rearrange("p i a t -> p (i a t)"),
                                 g.zc[ds(c, 1)].rearrange("c p i a t -> p (c i a t)")).then_inc(z_loaded[u], 16)
                    sp.dma_start(v[:, u], g.xm[2 * NPAIR:3 * NPAIR, :, ds(c * C, C)].rearrange("a p t -> p a t")).then_inc(v_loaded[u], 16)

                def load_rho(c, u):
                    sp.wait_ge(y_done, c + 1)
                    sp.dma_start(rho[:, u], g.zc[ds(c, 1), :, 1].rearrange("c p a t -> p (c a) t")).then_inc(rho_loaded[u], 16)

                def store(c, u):
                    sp.wait_ge(consts_loaded, 96)
                    sp.wait_ge(y_ready, c + 2)
                    sp.dma_start(g.y[:, :, ds(c * C, C)].rearrange("a p t -> p a t"), ys[:, u]).then_inc(y_stored[u], 16)

                load(0, 0)
                load_rho(0, 0)
                load(1, 1)
                load_rho(1, 1)
                with sp.Fori(0, NPC // 2 - 1) as i:
                    for u in range(2):
                        load(i * 2 + (u + 2), u)
                        store(i * 2 + u, u)
                        load_rho(i * 2 + (u + 2), u)
                load(NPC, 0)
                store(NPC - 2, 0)
                load_rho(NPC, 0)
                store(NPC - 1, 1)
                sp.wait_ge(state_ready, NPC + 1)
                sp.dma_start(g.wkv_p, state[:, :, :]).then_inc(state_stored, 16)
                store(NPC, 0)
                sp.wait_ge(bv_ready, NPAIR + 1)
                sp.dma_start(g.wkv_s, states_s[:, :, :, :]).then_inc(state_stored, 16)
                sp.wait_ge(state_stored, 32)
                sp.wait_ge(y_stored[0], 16 * (NPC // 2) + 32)
                sp.wait_ge(y_stored[1], 16 * (NPC // 2) + 16)

            @block.gpsimd
            def _(pool):
                pool.sem_inc(expanded, 2)
                for t in (*single, state):
                    op = pool.memset(t[:], 0.0)
                op.then_inc(cleared, 1)
                pool.wait_ge(cleared, 2)
                pool.sem_inc(state_bd_ready, 1)

                def prepare(c, u):
                    pool.wait_ge(z_loaded[u], c * 8 + (16 - 8 * u))
                    pool.wait_ge(v_loaded[u], c * 8 + (16 - 8 * u))
                    pool.wait_ge(kappat_done, c + 1)
                    pool.wait_ge(w_done, c + 1)
                    pool.sem_inc(passed, 1)
                    for dst, src in ((beta_bd, z[:, u, 2]), (kappa_bd, z[:, u, 3]), (alpha_bd[:, u], z[:, u, 0]), (v_bd, v[:, u])):
                        op = spread(pool.tensor_copy, dst, src)
                    op.then_inc(expanded, 1)

                def spread_vt(c, u):
                    pool.wait_ge(vt_ready, c + 1)
                    pool.wait_ge(y_done, c + 1)
                    pool.sem_inc(passed, 1)
                    spread(pool.tensor_copy, vt_bd[:, u], vt[:, u]).then_inc(vt_bd_ready, 1)

                def advance_u(c):
                    pool.wait_ge(u_ready, c + 2)
                    pool.wait_ge(y_done, c + 2)
                    pool.sem_inc(passed, 1)
                    spread(pool.tensor_copy, u_bd, us).then_inc(u_bd_ready, 1)

                def advance_state(c):
                    pool.wait_ge(state_ready, c + 2)
                    pool.wait_ge(y_done, c + 3)
                    pool.sem_inc(passed, 1)
                    spread(pool.tensor_copy, state_bd, state).then_inc(state_bd_ready, 1)

                def ahead(c, u, advance=None, more=True):
                    spread_vt(c, u)
                    if advance is not None:
                        advance_u(advance)
                    if more:
                        prepare(c + 1, 1 - u)
                    if advance is not None:
                        advance_state(advance)

                prepare(0, 0)
                ahead(0, 0)
                with pool.Fori(0, NPC // 2 - 1) as i:
                    ahead(i * 2 + 1, 1, i * 2)
                    ahead(i * 2 + 2, 0, i * 2 + 1)
                ahead(NPC - 1, 1, NPC - 2)
                ahead(NPC, 0, NPC - 1, more=False)
                pool.wait_ge(cleared, 2)
                pool.wait_ge(kappat_done, NPC + 2)
                pool.sem_inc(passed, 1)
                spread(pool.tensor_copy, beta_bd, z[:, 0, 1]).then_inc(expanded, 1)
                advance_u(NPC)
                pool.wait_ge(cleared, 2)
                pool.wait_ge(cross_picked, 2 * NPAIR + 1)
                pool.wait_ge(expanded, NPC + 4)
                pool.sem_inc(passed, 1)
                spread(pool.tensor_copy, state_bd, read_s).then_inc(state_bd_ready, 1)

            @block.tensor
            def _(pe):
                for s, n in ((kappat_done, 1), (w_done, 2), (u_done, 2), (y_done, 2), (s_done, 2), (a_done, 2)):
                    pe.sem_inc(s, n)
                pe.wait_ge(cleared, 2)
                pe.wait_ge(consts_loaded, 96)

                def pairs(b, *terms, rows=range(NPAIR), padded=True):
                    for a in rows:
                        n = 2 if padded and a < NPAIR - 1 else 1
                        for k, (lhs, rhs) in enumerate(terms):
                            mm = pe.matmul(bank[:, b, a:a + n].rearrange("p a t -> p (a t)"), lhs[:, a].rearrange("p h t -> p (h t)"),
                                           rhs[:, a:a + n].rearrange("p a t -> p (a t)"),
                                           start=k == 0, stop=k == len(terms) - 1)
                    return mm

                def double(b, lhs, rhs):
                    for a in range(NPAIR):
                        mm = pe.matmul(bank[:, b + a // 4, 2 * (a % 4):2 * (a % 4) + 2, :], lhs[:, a].rearrange("p h t -> p (h t)"),
                                       rhs[:, :, a, :], start=True, stop=True)
                    return mm

                def turn(b, x):
                    for a in range(NPAIR):
                        mm = pe.transpose(bank[:, b + a // 4, 2 * (a % 4):2 * (a % 4) + 2, :].rearrange("p h t -> p (h t)"),
                                          x[:, a].rearrange("p h t -> p (h t)"), ident[:, :])
                    return mm

                def products(c, u):
                    pe.wait_ge(expanded, c + 3)
                    double(T_BANK, beta_bd, z[:, u, 0:2]).then_inc(aq_done, 1)
                    pe.wait_ge(tt_ready, c * (LEVELS + 1) + (LEVELS + 1))
                    double(Z_BANK, kappa_bd, z[:, u, 0:2]).then_inc(br_done, 1)
                    pe.wait_ge(kappat_ready, c + 1)
                    pairs(TURN_BANK, (alpha_bd[:, u], z[:, u, 2])).then_inc(a_done, 1)

                def turn_v(c):
                    pe.wait_ge(a_ready, c + 1)
                    turn(TURN_BANK, v_bd).then_inc(vt_done, 1)

                def turn_beta(c):
                    pe.wait_ge(vt_ready, c + 1)
                    turn(TURN_BANK, beta_bd).then_inc(betat_done, 1)

                def turn_kappa(c):
                    pe.wait_ge(betat_ready, c + 2)
                    turn(TURN_BANK, kappa_bd).then_inc(kappat_done, 1)

                def level_z(c, l):
                    pe.wait_ge(tt_ready, c * (LEVELS + 1) + (LEVELS + 2 + l))
                    pe.wait_ge(a_ready, c + 1)
                    pairs(Z_BANK, (a_bd, tt)).then_inc(z_done, 1)

                def level_t(c, u, l):
                    for h in range(2):
                        pe.wait_ge(tt_bd_ready[h], c * (LEVELS + 1) + (l + 2))
                    turn(T_BANK, tt_bd[:, u]).then_inc(t_done, 1)

                def level_x(c, l):
                    pe.wait_ge(t_ready, c * LEVELS + (l + 1))
                    pe.wait_ge(z_ready, c * LEVELS + (l + 1))
                    pairs(X_BANK, (t_bd, zt)).then_inc(x_done, 1)

                def w_products(c, u):
                    pe.wait_ge(vt_ready, c + 1)
                    pe.wait_ge(state_ready, c + 1)
                    pe.wait_ge(u_ready, c + 1)
                    pairs(W_BANK, (bt_bd[:, u], vt[:, u]), (alpha_bd[:, u], state)).then_inc(w_done, 1)

                def u_products(c, u):
                    for h in range(2):
                        pe.wait_ge(tt_bd_ready[h], c * (LEVELS + 1) + (LEVELS + 2))
                    pe.wait_ge(w_ready, c + 1)
                    pairs(W_BANK, (tt_bd[:, u], ws)).then_inc(u_done, 1)

                def y_products(c, u, rows):
                    if rows[0] == 0:
                        pe.wait_ge(vt_bd_ready, c + 1)
                        pe.wait_ge(state_bd_ready, c + 1)
                        pe.wait_ge(u_bd_ready, c + 1)
                        pe.wait_ge(q_ready, c + 1)
                        pe.wait_ge(rho_loaded[u], c * 8 + (16 - 8 * u))
                        pe.wait_ge(grown_ready, c + 1)
                    mm = pairs(YS_BANK, (vt_bd[:, u], rt[:, u]), (state_bd, rho[:, u]), (u_bd, qt[:, u]), rows=rows)
                    if rows[-1] == NPAIR - 1:
                        mm.then_inc(y_done, 1)

                def state_products(c, u):
                    pe.wait_ge(u_ready, c + 2)
                    pe.wait_ge(kappat_ready, c + 2)
                    pe.wait_ge(betat_ready, c + 2)
                    pe.wait_ge(y_ready, c + 2)
                    pairs(YS_BANK, (kappat_bd[:, u], vt[:, u]), (betat_bd[:, u], us)).then_inc(s_done, 1)

                def ahead(c, u, advance=None):
                    def back(step, *a):
                        if advance is not None:
                            step(advance, 1 - u, *a)
                    products(c, u)
                    back(w_products)
                    level_z(c, 0)
                    level_t(c, u, 0)
                    turn_v(c)
                    level_x(c, 0)
                    turn_beta(c)
                    level_z(c, 1)
                    level_t(c, u, 1)
                    back(u_products)
                    level_x(c, 1)
                    turn_kappa(c)
                    level_z(c, 2)
                    level_t(c, u, 2)
                    back(y_products, range(0, 2))
                    level_x(c, 2)
                    back(y_products, range(2, 4))
                    level_z(c, 3)
                    level_t(c, u, 3)
                    back(y_products, range(4, 6))
                    level_x(c, 3)
                    back(y_products, range(6, 8))
                    level_z(c, 4)
                    level_t(c, u, 4)
                    back(state_products)
                    level_x(c, 4)

                ahead(0, 0)
                with pe.Fori(0, NPC // 2 - 1) as i:
                    ahead(i * 2 + 1, 1, i * 2)
                    ahead(i * 2 + 2, 0, i * 2 + 1)
                ahead(NPC - 1, 1, NPC - 2)
                ahead(NPC, 0, NPC - 1)

                c = NPC
                pe.wait_ge(expanded, c + 4)
                pe.wait_ge(u_ready, c + 1)
                for n, lhs in enumerate((alpha_bd[:, 0], beta_bd)):
                    for a in range(NPAIR):
                        pe.wait_ge(masked, n * NPAIR + a + 1)
                        pe.matmul(bank[:, W_BANK].rearrange("p a t -> p (a t)"), lhs[:, a].rearrange("p h t -> p (h t)"),
                                  states_s[:, a].rearrange("p b v -> p (b v)"), start=True, stop=True).then_inc(cross_done, 1)
                pe.wait_ge(masked, 2 * NPAIR + 1)
                pairs(W_BANK, (bt_bd[:, 0], vt[:, 0])).then_inc(w_done, 1)
                u_products(c, 0)
                pe.wait_ge(state_bd_ready, c + 2)
                pe.wait_ge(vt_bd_ready, c + 1)
                pe.wait_ge(u_bd_ready, c + 1)
                pe.wait_ge(q_ready, c + 1)
                pe.wait_ge(grown_ready, c + 1)
                pairs(YS_BANK, (vt_bd[:, 0], rt[:, 0]), (state_bd, eye[:, :].unsqueeze(1).to_broadcast([P, NPAIR, C])),
                      (u_bd, qt[:, 0]), padded=False).then_inc(y_done, 1)
                pe.wait_ge(y_ready, c + 2)
                pe.wait_ge(kappat_ready, c + 2)
                pe.wait_ge(betat_ready, c + 2)
                for a in range(NPAIR):
                    pe.wait_ge(grown_ready, NPC + a + 1)
                    pe.wait_ge(cross_read, 2 * a + 2)
                    pe.matmul(bank[:, YS_BANK].rearrange("p a t -> p (a t)"), kappat_bd[:, 0, a].rearrange("p h t -> p (h t)"),
                              z[:, 0].rearrange("p i a t -> p (i a t)")[:, 0:DB * HD], start=True, stop=False)
                    pe.matmul(bank[:, YS_BANK].rearrange("p a t -> p (a t)"), betat_bd[:, 0, a].rearrange("p h t -> p (h t)"),
                              z[:, 0].rearrange("p i a t -> p (i a t)")[:, DB * HD:2 * DB * HD], start=False, stop=True).then_inc(s_done, 1)

            @block.scalar
            def _(act):
                act.sem_inc(betat_ready, 1)
                act.sem_inc(kappat_ready, 1)
                act.sem_inc(y_ready, 1)
                act.sem_inc(tt_bd_ready[0], 1)
                act.wait_ge(cleared, 2)
                turned = bank[:, TURN_BANK:TURN_BANK + 2].rearrange("p b (a h) t -> p (b a) h t", h=2)
                turned_t = bank[:, T_BANK:T_BANK + 2].rearrange("p b (a h) t -> p (b a) h t", h=2)

                def gather(copy, dst, src, last):
                    for h in range(2):
                        op = copy(dst(h), src[half[h], :, h, :])
                    op.then_inc(last, 1)

                def turn_v(c, u):
                    act.wait_ge(vt_done, c + 1)
                    act.wait_ge(s_done, c + 1)
                    gather(act.copy, lambda h: vt[half[h], u], turned, vt_ready)

                def turn_beta(c, u):
                    act.wait_ge(betat_done, c + 1)
                    gather(lambda o, x: act.mul(o, x, -1.0), lambda h: betat_bd[half[h], u, :, h, :], turned, betat_ready)

                def turn_kappa(c, u):
                    act.wait_ge(kappat_done, c + 2)
                    gather(act.copy, lambda h: kappat_bd[half[h], u, :, h, :], turned, kappat_ready)

                def level_t(c, l):
                    act.wait_ge(t_done, c * LEVELS + (l + 1))
                    gather(act.copy, lambda h: t_bd[half[h], :, h, :], turned_t, t_ready)

                def spread_tt(c, u, l):
                    act.wait_ge(tt_ready, c * (LEVELS + 1) + (LEVELS + 2 + l))
                    if l == 0:
                        act.wait_ge(u_done, c + 1)
                    act.copy(tt_bd[half[0], u, :, 0, :], tt[half[0]]).then_inc(tt_bd_ready[0], 1)

                def advance_y(c, u):
                    act.wait_ge(y_done, c + 3)
                    act.wait_ge(y_stored[u], c * 8 + (16 - 8 * u))
                    act.copy(ys[:, u], bank[:, YS_BANK]).then_inc(y_ready, 1)

                def ahead(c, u, advance=None):
                    spread_tt(c, u, 0)
                    level_t(c, 0)
                    turn_v(c, u)
                    spread_tt(c, u, 1)
                    turn_beta(c, u)
                    level_t(c, 1)
                    spread_tt(c, u, 2)
                    turn_kappa(c, u)
                    level_t(c, 2)
                    spread_tt(c, u, 3)
                    level_t(c, 3)
                    spread_tt(c, u, 4)
                    if advance is not None:
                        advance_y(advance, 1 - u)
                    level_t(c, 4)
                    spread_tt(c, u, 5)

                ahead(0, 0)
                with act.Fori(0, NPC // 2 - 1) as i:
                    ahead(i * 2 + 1, 1, i * 2)
                    ahead(i * 2 + 2, 0, i * 2 + 1)
                ahead(NPC - 1, 1, NPC - 2)
                ahead(NPC, 0, NPC - 1)
                advance_y(NPC, 0)

            @block.vector
            def _(dve):
                for t in double:
                    op = dve.memset(t[:], 0.0)
                op.then_inc(cleared, 1)
                dve.sem_inc(tt_ready, LEVELS + 1)
                dve.sem_inc(grown_ready, 1)
                dve.sem_inc(tt_bd_ready[1], 1)
                dve.sem_inc(u_ready, 1)
                dve.sem_inc(state_ready, 1)
                dve.wait_ge(cleared, 2)
                dve.wait_ge(consts_loaded, 96)
                wide_aq = bank[:, T_BANK:T_BANK + 2].rearrange("p b (a w) t -> p (b a) w t", w=2)
                wide_br = bank[:, Z_BANK:Z_BANK + 2].rearrange("p b (a w) t -> p (b a) w t", w=2)

                def spread_tt(c, u, l):
                    dve.wait_ge(tt_ready, c * (LEVELS + 1) + (LEVELS + 2 + l))
                    if l == 0:
                        dve.wait_ge(u_done, c + 1)
                    dve.tensor_copy(tt_bd[half[1], u, :, 1, :], tt[half[1]]).then_inc(tt_bd_ready[1], 1)

                def products(c, u, m):
                    dve.wait_ge(aq_done, c + 1)
                    for h in range(2):
                        dve.wait_ge(tt_bd_ready[h], c * (LEVELS + 1) + 1)
                    dve.tensor_tensor(tt[:, :, :], wide_aq[:, :, 0, :], over_pairs(masks[:, m, 0]), ALU.mult).then_inc(masked_tt, 1)
                    dve.wait_ge(y_done, c + 1)
                    dve.tensor_tensor(qt[:, u], wide_aq[:, :, 1, :], over_pairs(masks[:, m, 1]), ALU.mult).then_inc(q_ready, 1)
                    dve.wait_ge(masked_tt, c + 1)
                    dve.tensor_tensor(tt[:, :, :], tt[:, :, :], over_pairs(eye[:, :]), ALU.add).then_inc(tt_ready, 1)
                    spread_tt(c, u, 0)
                    dve.wait_ge(br_done, c + 1)
                    for h in range(2):
                        dve.tensor_tensor(bt_bd[half[h], u, :, h, :], wide_br[half[h], :, 0, :], over_pairs(masks[half[h], m, 2]), ALU.mult)
                    dve.tensor_tensor(rt[:, u], wide_br[:, :, 1, :], over_pairs(masks[:, m, 3]), ALU.mult).then_inc(br_ready, 1)
                    dve.wait_ge(a_done, c + 3)
                    for h in range(2):
                        op = dve.tensor_tensor(a_bd[half[h], :, h, :], bank[half[h], TURN_BANK], over_pairs(masks[half[h], m, 4]), ALU.mult)
                    op.then_inc(a_ready, 1)

                def level_z(c, l):
                    dve.wait_ge(z_done, c * LEVELS + (l + 1))
                    dve.tensor_copy(zt[:, :, :], bank[:, Z_BANK]).then_inc(z_ready, 1)

                def level_x(c, u, l):
                    dve.wait_ge(x_done, c * LEVELS + (l + 1))
                    dve.wait_ge(tt_bd_ready[1], c * (LEVELS + 1) + (l + 2))
                    dve.sem_inc(dve_passed, 1)
                    dve.copy_predicated(tt[:, :, :], over_pairs(doubling[:, l]), bank[:, X_BANK]).then_inc(tt_ready, 1)
                    spread_tt(c, u, l + 1)

                def advance_w(c):
                    dve.wait_ge(w_done, c + 3)
                    dve.tensor_copy(ws[:, :, :], bank[:, W_BANK]).then_inc(w_ready, 1)

                def advance_u(c):
                    dve.wait_ge(u_done, c + 3)
                    dve.tensor_copy(us[:, :, :], bank[:, W_BANK]).then_inc(u_ready, 1)

                def advance_state(c):
                    dve.wait_ge(s_done, c + 3)
                    dve.tensor_tensor(grown[:, :, :], bank[:, YS_BANK], state[:, :, :], ALU.add).then_inc(grown_ready, 1)
                    dve.wait_ge(grown_ready, c + 2)
                    dve.wait_ge(state_bd_ready, c + 1)
                    dve.tensor_tensor(state[:, :, :], grown[:, :, :], g.lam_p[:, :, ds(c, 1)].to_broadcast([P, NPAIR, HD]),
                                      ALU.mult).then_inc(state_ready, 1)

                def ahead(c, u, m=0, advance=None):
                    def back(step):
                        if advance is not None:
                            step(advance)
                    products(c, u, m)
                    back(advance_w)
                    level_z(c, 0)
                    level_x(c, u, 0)
                    level_z(c, 1)
                    back(advance_u)
                    level_x(c, u, 1)
                    for l in (2, 3):
                        level_z(c, l)
                        level_x(c, u, l)
                    level_z(c, 4)
                    back(advance_state)
                    level_x(c, u, 4)

                ahead(0, 0)
                with dve.Fori(0, NPC // 2 - 1) as i:
                    ahead(i * 2 + 1, 1, 0, i * 2)
                    ahead(i * 2 + 2, 0, 0, i * 2 + 1)
                ahead(NPC - 1, 1, 0, NPC - 2)
                ahead(NPC, 0, 1, NPC - 1)

                c = NPC
                by_seq = seq[:, :].unsqueeze(2).to_broadcast([P, DB, HD])
                dve.sem_inc(masked, 1)
                dve.sem_inc(cross_picked, 1)
                for n, out in enumerate((ws, read_s)):
                    for a in range(NPAIR):
                        k = n * NPAIR + a
                        dve.wait_ge(cross_done, k + 1)
                        dve.wait_ge(cross_picked, k + 1)
                        dve.tensor_tensor(picked[:, :, :], bank[:, W_BANK], by_seq, ALU.mult).then_inc(masked, 1)
                        dve.wait_ge(masked, k + 2)
                        dve.tensor_reduce(out[:, a, :], picked[:, :, :].rearrange("p b v -> p v b"), AX.X, ALU.add).then_inc(cross_picked, 1)
                dve.wait_ge(cross_picked, 2 * NPAIR + 1)
                dve.wait_ge(w_done, c + 3)
                dve.tensor_tensor(ws[:, :, :], bank[:, W_BANK], ws[:, :, :], ALU.add).then_inc(w_ready, 1)
                advance_u(c)
                dve.sem_inc(bv_ready, 1)
                dve.wait_ge(u_ready, c + 2)
                dve.wait_ge(y_done, c + 3)
                zf = z[:, 0].rearrange("p i a t -> p (i a t)")
                for a in range(NPAIR):
                    if a:
                        dve.wait_ge(s_done, NPC + 2 + a)
                    for j, x in enumerate((vt[:, 0, a, :], us[:, a, :])):
                        dve.tensor_tensor(zf[:, j * DB * HD:(j + 1) * DB * HD].rearrange("p (b v) -> p b v", b=DB),
                                          x.unsqueeze(1).to_broadcast([P, DB, HD]), by_seq, ALU.mult).then_inc(cross_read, 1)
                    dve.wait_ge(s_done, NPC + 3 + a)
                    dve.tensor_tensor(picked[:, :, :], bank[:, YS_BANK], states_s[:, a], ALU.add).then_inc(grown_ready, 1)
                    dve.wait_ge(grown_ready, NPC + a + 2)
                    dve.tensor_tensor(states_s[:, a], picked[:, :, :],
                                      g.lam_s[:, a, :].unsqueeze(2).to_broadcast([P, DB, HD]), ALU.mult).then_inc(bv_ready, 1)


def finish_mixing(nc, g):
    with Phase(nc, "finish") as ph:
        buf = {n: ph.sb(n, [P, 2, T]) for n in ("y", "bonus", "gate")}
        sq = ph.sb("sq", [P, T])
        rstd = ph.sb("rstd", [P, T])
        heads = ph.sb("heads", [P, P])
        means = ph.sb("means", [P, P])
        par = ph.sb("par", [P, 4, NPAIR])
        pp = ph.sb("pp", [P, 2])
        eps = ph.sb("eps", [P, 2])
        bank = ph.psum("bank", [P, SEG, 512])
        loaded = [ph.sem("loaded0"), ph.sem("loaded1")]
        par_loaded, consts_set, pp_ready, mean_done, centred, squared, var_done, ln_ready, rstd_ready, scaled, biased, \
            mixed_ready, conv_mean, conv_centred, conv_squared, conv_var, conv_ln, conv_rstd, conv_scaled, conv_sig, \
            conv_ready = (
                ph.sem(n) for n in (
                    "par_loaded", "consts_set", "pp_ready", "mean_done", "centred", "squared", "var_done", "ln_ready",
                    "rstd_ready", "scaled", "biased", "mixed_ready", "conv_mean", "conv_centred", "conv_squared",
                    "conv_var", "conv_ln", "conv_rstd", "conv_scaled", "conv_sig", "conv_ready"))
        seg = [slice(s * SW, (s + 1) * SW) for s in range(SEG)]
        y, bonus, gate = buf["y"], buf["bonus"], buf["gate"]
        part = [slice(0, T // 2), slice(T // 2, T)]

        def cut(x):
            return x.rearrange("p (s n) -> p s n", n=SW)

        with ph.block() as block:
            @block.sync
            def _(sp):
                sp.dma_start(par[:, :, :], g.norm_par).then_inc(par_loaded, 16)
                with sp.Fori(0, NPAIR // 2) as i:
                    for u in range(2):
                        sp.wait_ge(mixed_ready, i * 2 + (u + 1))
                        for x, src in ((y, g.y), (bonus, g.bonus), (gate, g.go)):
                            sp.dma_start(x[:, u], src[ds(i * 2 + u, 1)].rearrange("a p t -> p (a t)")).then_inc(loaded[u], 16)

            @block.tensor
            def _(pe):
                pe.sem_inc(var_done, 2)
                pe.wait_ge(consts_set, 5)
                with pe.Fori(0, NPAIR // 2) as j:
                    for u in range(2):
                        pe.wait_ge(loaded[u], j * 48 + 48)
                        for h in range(2):
                            i = j * 4 + (u * 2 + h)
                            pe.wait_ge(ln_ready, i + 1)
                            for s in range(3 * h, 3 * h + 3):
                                mm = pe.matmul(bank[:, s, 0:SW], heads[:, :], y[:, u, seg[s]], start=True, stop=True)
                            mm.then_inc(mean_done, 1)
                        for h in range(2):
                            i = j * 4 + (u * 2 + h)
                            pe.wait_ge(squared, i + 1)
                            for s in range(3 * h, 3 * h + 3):
                                mm = pe.matmul(bank[:, s, 0:SW], heads[:, :], sq[:, seg[s]], start=True, stop=True)
                            mm.then_inc(var_done, 1)
                pe.wait_ge(ln_ready, 2 * NPAIR + 2)
                for s in range(SEG):
                    for b in range(CB):
                        mm = pe.matmul(bank[:, s, 0:SW], means[:, :], g.conv[:, b, seg[s]], start=b == 0, stop=b == CB - 1)
                mm.then_inc(conv_mean, 1)
                for s in range(SEG):
                    for b in range(CB):
                        pe.wait_ge(conv_squared, s * CB + b + 1)
                        pe.matmul(bank[:, s, 0:SW], means[:, :], sq[:, (b % 2) * SW:(b % 2 + 1) * SW],
                                  start=b == 0, stop=b == CB - 1).then_inc(conv_var, 1)

            @block.scalar
            def _(act):
                act.sem_inc(ln_ready, 2)
                act.wait_ge(consts_set, 5)
                with act.Fori(0, NPAIR // 2) as j:
                    for u in range(2):
                        for h in range(2):
                            i = j * 4 + (u * 2 + h)
                            act.wait_ge(centred, i + 1)
                            act.wait_ge(var_done, i + 1)
                            act.activation(sq[:, part[h]], y[:, u, part[h]], ACT.Square).then_inc(squared, 1)
                        for h in range(2):
                            i = j * 4 + (u * 2 + h)
                            act.wait_ge(var_done, i + 3)
                            act.wait_ge(scaled, i + 1)
                            act.activation(cut(rstd[:, part[h]]), bank[:, 3 * h:3 * h + 3, 0:SW], ACT.Ln, bias=eps[:, 0:1]).then_inc(ln_ready, 1)
                            act.wait_ge(ln_ready, i + 3)
                            act.activation(rstd[:, part[h]], rstd[:, part[h]], ACT.Exp, scale=-0.5).then_inc(rstd_ready, 1)
                act.wait_ge(conv_centred, 1)
                for s in range(SEG):
                    for b in range(CB):
                        if s * CB + b >= 2:
                            act.wait_ge(conv_var, s * CB + b - 1)
                        act.activation(sq[:, (b % 2) * SW:(b % 2 + 1) * SW], g.conv[:, b, seg[s]], ACT.Square).then_inc(conv_squared, 1)
                act.wait_ge(conv_var, SEG * CB)
                act.wait_ge(scaled, 2 * NPAIR + 2)
                act.activation(rstd[:, :].rearrange("p (s n) -> p s n", s=SEG), bank[:, :, 0:SW], ACT.Ln,
                               bias=eps[:, 1:2]).then_inc(conv_ln, 1)
                act.wait_ge(conv_ln, 1)
                act.activation(rstd[:, :], rstd[:, :], ACT.Exp, scale=-0.5).then_inc(conv_rstd, 1)
                for b in range(CB):
                    act.wait_ge(conv_scaled, b + 1)
                    if b > 1:
                        act.wait_ge(conv_ready, b - 1)
                    act.activation(buf["y"][:, b % 2], g.conv[:, b, :], ACT.Sigmoid, bias=par[:, 3, b:b + 1]).then_inc(conv_sig, 1)

            @block.vector
            def _(dve):
                dve.memset(means[:, :], 1.0 / CW).then_inc(consts_set, 1)
                dve.memset(heads[:, :], 0.0).then_inc(consts_set, 1)
                dve.memset(eps[:, 0:1], GN_EPS)
                dve.memset(eps[:, 1:2], LN_EPS).then_inc(consts_set, 1)
                dve.wait_ge(consts_set, 3)
                for h in range(2):
                    dve.memset(heads[h * HD:(h + 1) * HD, h * HD:(h + 1) * HD], 1.0 / HD).then_inc(consts_set, 1)
                dve.sem_inc(mixed_ready, 2)
                dve.sem_inc(scaled, 2)
                dve.wait_ge(par_loaded, 16)
                with dve.Fori(0, NPAIR // 2) as j:
                    for u in range(2):
                        p = j * 2 + u
                        dve.tensor_copy(pp[:, :], par[:, 0:2, ds(p, 1)].rearrange("p n a -> p (n a)")).then_inc(pp_ready, 1)
                        dve.wait_ge(loaded[u], j * 48 + 48)
                        for h in range(2):
                            i, yu = j * 4 + (u * 2 + h), y[:, u, part[h]]
                            dve.wait_ge(mean_done, i + 1)
                            dve.tensor_tensor(cut(yu), cut(yu), bank[:, 3 * h:3 * h + 3, 0:SW], ALU.subtract).then_inc(centred, 1)
                        dve.wait_ge(pp_ready, p + 1)
                        for h in range(2):
                            i, yu = j * 4 + (u * 2 + h), y[:, u, part[h]]
                            dve.wait_ge(rstd_ready, i + 1)
                            dve.scalar_tensor_tensor(yu, yu, pp[:, 0:1], rstd[:, part[h]], ALU.mult, ALU.mult).then_inc(scaled, 1)
                            dve.wait_ge(scaled, i + 3)
                            dve.scalar_tensor_tensor(yu, yu, pp[:, 1:2], bonus[:, u, part[h]], ALU.add, ALU.add).then_inc(biased, 1)
                            dve.wait_ge(biased, i + 1)
                            op = dve.tensor_tensor(g.mixed[:, ds(p, 1), part[h]].rearrange("p a t -> p (a t)"), yu, gate[:, u, part[h]], ALU.mult)
                        op.then_inc(mixed_ready, 1)
                dve.wait_ge(conv_mean, 1)
                for b in range(CB):
                    x = g.conv[:, b, :].rearrange("p (s n) -> p s n", s=SEG)
                    op = dve.tensor_tensor(x, x, bank[:, :, 0:SW], ALU.subtract)
                op.then_inc(conv_centred, 1)
                dve.wait_ge(conv_rstd, 1)
                for b in range(CB):
                    dve.scalar_tensor_tensor(g.conv[:, b, :], g.conv[:, b, :], par[:, 2, b:b + 1], rstd[:, :],
                                             ALU.mult, ALU.mult).then_inc(conv_scaled, 1)
                for b in range(CB):
                    dve.wait_ge(conv_sig, b + 1)
                    dve.scalar_tensor_tensor(g.conv[:, b, :], g.conv[:, b, :], par[:, 3, b:b + 1], buf["y"][:, b % 2],
                                             ALU.add, ALU.mult).then_inc(conv_ready, 1)


def mix_branches(nc, g):
    with Phase(nc, "branch") as ph:
        w = ph.sb("w", [P, 2, KC + CB, P])
        gate = ph.sb("gate", [P, 2, 2, T])
        m = ph.sb("m", [P, 2, NT * P])
        part = ph.sb("part", [P, 2, QW])
        bias = ph.sb("bias", [P, KC])
        bb = ph.sb("bb", [P, 2])
        bank = ph.psum("bank", [P, 2, 2, 512])
        w_loaded = [ph.sem("w_loaded0"), ph.sem("w_loaded1")]
        gate_loaded = [ph.sem("gate_loaded0"), ph.sem("gate_loaded1")]
        bias_loaded, bank_ready, bank_free, bb_ready, gated_ready, m_ready, m_free = (
            ph.sem(n) for n in ("bias_loaded", "bank_ready", "bank_free", "bb_ready", "gated_ready",
                                "m_ready", "m_free"))
        m_stored = ph.pool_dma_sem("m_stored")

        with ph.block() as block:
            @block.sync
            def _(sp):
                sp.dma_start(bias[:, :], g.conv_out_b).then_inc(bias_loaded, 16)
                with sp.Fori(0, KC // 2) as i:
                    for u in range(2):
                        cb = i * 2 + u
                        sp.wait_ge(m_ready, cb + 1)
                        sp.dma_start(w[:, u], g.w_branch[ds(cb, 1)].rearrange("a p k c -> p (a k) c")).then_inc(w_loaded[u], 16)
                        for n in range(2):
                            sp.dma_start(gate[:, u, n], g.gates[ds(cb + n * KC, 1)].rearrange("a p t -> p (a t)")).then_inc(gate_loaded[u], 16)

            @block.gpsimd
            def _(pool):
                with pool.Fori(0, KC // 2) as i:
                    for u in range(2):
                        cb = i * 2 + u
                        pool.wait_ge(m_ready, cb + 3)
                        pool.dma_start(g.m[ds(cb, 1)].rearrange("a p t -> p (a t)"), m[:, u]).then_inc(m_stored, 16)
                        pool.wait_ge(m_stored, cb * 16 + 16)
                        pool.sem_inc(m_free, 1)

            @block.tensor
            def _(pe):
                with pe.Fori(0, KC // 2) as i:
                    for u in range(2):
                        cb = i * 2 + u
                        pe.wait_ge(w_loaded[u], i * 16 + 16)
                        for q in range(Q):
                            n = min(QW, T - q * QW)
                            k = cb * Q + q
                            pe.wait_ge(bank_free, k + 1)
                            for src, b, k0, kn in ((g.mixed, 0, 0, KC), (g.conv, 1, KC, CB)):
                                for kc in range(kn):
                                    mm = pe.matmul(bank[:, b, (q + u) % 2, 0:n], w[:, u, k0 + kc, :], src[:, kc, q * QW:q * QW + n],
                                                   start=kc == 0, stop=kc == kn - 1)
                            mm.then_inc(bank_ready, 1)

            @block.vector
            def _(dve):
                dve.sem_inc(bank_free, 2)
                dve.sem_inc(m_ready, 2)
                dve.sem_inc(m_free, 2)
                dve.memset(m[:, :, T:NT * P], 0.0)
                dve.wait_ge(bias_loaded, 16)
                with dve.Fori(0, KC // 2) as i:
                    for u in range(2):
                        cb = i * 2 + u
                        dve.tensor_copy(bb[:, u:u + 1], bias[:, ds(cb, 1)]).then_inc(bb_ready, 1)
                        dve.wait_ge(bb_ready, cb + 1)
                        dve.wait_ge(gate_loaded[u], i * 32 + 32)
                        dve.wait_ge(m_free, cb + 1)
                        for q in range(Q):
                            n = min(QW, T - q * QW)
                            k = cb * Q + q
                            cols = slice(q * QW, q * QW + n)
                            dve.wait_ge(bank_ready, k + 1)
                            dve.scalar_tensor_tensor(part[:, 0, 0:n], bank[:, 1, (q + u) % 2, 0:n], bb[:, u:u + 1],
                                                     gate[:, u, 0, cols], ALU.add, ALU.mult)
                            dve.tensor_tensor(part[:, 1, 0:n], bank[:, 0, (q + u) % 2, 0:n], gate[:, u, 1, cols], ALU.mult).then_inc(bank_free, 1)
                            dve.wait_ge(bank_free, k + 3)
                            dve.tensor_tensor(m[:, u, cols], part[:, 0, 0:n], part[:, 1, 0:n], ALU.add).then_inc(gated_ready, 1)
                            dve.wait_ge(gated_ready, k + 1)
                        dve.sem_inc(m_ready, 1)


def route(nc, g):
    with Phase(nc, "route") as ph:
        w_o = ph.sb("w_o", [P, KC, D])
        rw = ph.sb("rw", [P, KC, NG + NE])
        rb = ph.sb("rb", [P, NG + NE])
        gain = ph.sb("gain", [P, D])
        ident = ph.sb("ident", [P, P])
        earlier = ph.sb("earlier", [P, P])
        ones = ph.sb("ones", [P, P])
        w_hi, w_lo = (ph.sb(n, [P, KC, D], F32R) for n in ("w_hi", "w_lo"))
        m = ph.sb("m", [P, 2, KC, P])
        m_hi, m_lo = (ph.sb(n, [P, 2, KC, P], F32R) for n in ("m_hi", "m_lo"))
        x = ph.sb("x", [P, 2, D])
        x2 = ph.sb("x2", [P, 2, D])
        h = ph.sb("h", [P, 2, D])
        hT = ph.sb("hT", [P, KC, P])
        junk = ph.sb("junk", [P, D])
        ss, ms, lms, rstd, nmax, esum, g_one = (ph.sb(n, [P, 1]) for n in (
            "ss", "ms", "lms", "rstd", "nmax", "esum", "g_one"))
        logits = ph.sb("logits", [P, NG + NE])
        glog = ph.sb("glog", [P, 8])
        top, etop, e_exp = (ph.sb(n, [P, 8]) for n in ("top", "etop", "e_exp"))
        gexp = ph.sb("gexp", [P, NG])
        gidx, eidx = (ph.sb(n, [P, 8], U32) for n in ("gidx", "eidx"))
        gid = ph.sb("gid", [P, 1])
        ghot = ph.sb("ghot", [P, NG])
        chosen = ph.sb("chosen", [P, EPG])
        ids = ph.sb("ids", [P, NE])
        hot = ph.sb("hot", [P, 2, NE])
        both = ph.sb("both", [P, NE])
        base = ph.sb("base", [P, NE])
        rank = ph.sb("rank", [P, NE])
        at = ph.sb("at", [P, 2, NE])
        valid = ph.sb("valid", [P, 1])
        expert = ph.sb("expert", [P, NT, 2])
        ranks = ph.sb("ranks", [P, NT, 2])
        dest = ph.sb("dest", [P, NT, 2])
        allhot = ph.sb("allhot", [P, NT * 2, NE])
        count_i = ph.sb("count_i", [P, NE], I32)
        padded, ends, starts, each_one = (ph.sb(n, [P, NE]) for n in ("padded", "ends", "starts", "each_one"))
        blocks = ph.sb("blocks", [P, NBLK])
        filled = ph.sb("filled", [P, NBLK, NE])
        block_of, fresh, block_ones = (ph.sb(n, [P, NBLK]) for n in ("block_of", "fresh", "block_ones"))
        token = ph.sb("token", [P, NT], I32)
        nothing = ph.sb("nothing", [P, NBLK + 1], I32)
        spare = ph.sb("spare", [P, 2])
        bank = ph.psum("bank", [P, 8, 512])
        m_loaded, x_loaded, x2_stored, h_stored = ([ph.sem(f"{n}{u}") for u in range(2)] for n in
                                                   ("m_loaded", "x_loaded", "x2_stored", "h_stored"))
        consts_loaded, consts_set, out_done, x2_ready, h_ready, squared, ln_ready, rstd_ready, turned, hT_ready, \
            logits_done, counts_done, gexp_ready, eexp_ready, routed, tile_done, dest_ready, nothing_set, \
            ms_ready, nmax_ready, e_diff_ready, hot_ready, valid_set = (
                ph.sem(n) for n in (
                    "consts_loaded", "consts_set", "out_done", "x2_ready", "h_ready", "squared",
                    "ln_ready", "rstd_ready", "turned", "hT_ready", "logits_done", "counts_done", "gexp_ready",
                    "eexp_ready", "routed", "tile_done", "dest_ready", "nothing_set",
                    "ms_ready", "nmax_ready", "e_diff_ready", "hot_ready", "valid_set"))
        LINKS, CHOICE = 22, 19
        NCONST = 5
        WQ = 4
        w_loaded = [ph.sem(f"w_loaded{q}") for q in range(WQ)]
        table_cleared, scattered, ids_stored = (ph.pool_dma_sem(n) for n in ("table_cleared", "scattered", "ids_stored"))
        w_hi_ready, w_lo_ready, m_hi_ready, m_lo_ready, ranked = (ph.sem(n) for n in (
            "w_hi_ready", "w_lo_ready", "m_hi_ready", "m_lo_ready", "ranked"))
        OUT, TURNED, LOGITS, COUNTS = (0, 2), 4, 6, 7
        passed = ph.sem("passed")

        def chunks(q):
            return slice(q * KC // WQ, (q + 1) * KC // WQ)

        with ph.block() as block:
            @block.sync
            def _(sp):
                for s in (*x2_stored, *h_stored):
                    sp.sem_inc(s, 16)

                def load(t, u):
                    sp.wait_ge(m_lo_ready, t + 1)
                    sp.dma_start(m[:, u], g.m[:, :, ds(t * P, P)].rearrange("k p t -> p k t")).then_inc(m_loaded[u], 16)
                    sp.wait_ge(x2_ready, t + 1)
                    sp.dma_start(x[:, u], g.x[ds(t * P, P)]).then_inc(x_loaded[u], 16)

                def store(t, u):
                    sp.wait_ge(h_ready, t + 1)
                    sp.dma_start(g.x2[ds(t * P, P)], x2[:, u]).then_inc(x2_stored[u], 16)
                    sp.dma_start(g.h[ds(t * P, P)], h[:, u]).then_inc(h_stored[u], 16)

                for q in range(WQ):
                    sp.dma_start(w_o[:, chunks(q)], g.w_o[:, chunks(q)]).then_inc(w_loaded[q], 16)
                    if q < 2:
                        load(q, q)
                for dst, src in ((rw, g.router_w), (ident, g.ident), (earlier, g.earlier)):
                    sp.dma_start(dst[:], src).then_inc(consts_loaded, 16)
                sp.dma_start(rb[:, :], g.router_b.to_broadcast([P, NG + NE])).then_inc(consts_loaded, 16)
                sp.dma_start(gain[:, :], g.norm2.to_broadcast([P, D])).then_inc(consts_loaded, 16)
                with sp.Fori(0, NT // 2 - 1) as i:
                    for u in range(2):
                        load(i * 2 + (u + 2), u)
                        store(i * 2 + u, u)
                load(NT - 1, 0)
                for t in range(NT - 3, NT):
                    store(t, t % 2)
                for s, n in ((x2_stored, 0), (h_stored, 0)):
                    sp.wait_ge(s[0], 16 + 16 * (NT // 2 + 1))
                    sp.wait_ge(s[1], 16 + 16 * (NT // 2))

            @block.tensor
            def _(pe):
                def product(t, u, n, arriving=False):
                    if n == 0:
                        pe.wait_ge(m_lo_ready, t + 3)
                        pe.wait_ge(x2_ready, t + 1)
                    cols = slice(n * 512, (n + 1) * 512)
                    for kc in range(KC):
                        if arriving and kc % (KC // WQ) == 0:
                            pe.wait_ge(w_lo_ready, kc // (KC // WQ) + 1)
                        for k, (a, w) in enumerate(((m_hi, w_hi), (m_hi, w_lo), (m_lo, w_hi))):
                            mm = pe.matmul(bank[:, OUT[u] + n], a[:, u, kc, :], w[:, kc, cols],
                                           start=kc == 0 and k == 0, stop=kc == KC - 1 and k == 2)
                    if n == 1:
                        mm.then_inc(out_done, 1)

                def turn(t, u):
                    pe.wait_ge(h_ready, t + 1)
                    pe.wait_ge(hT_ready, t + 1)
                    for kc in range(KC):
                        mm = pe.transpose(bank[:, TURNED + kc // 4, (kc % 4) * P:(kc % 4 + 1) * P], h[:, u, kc * P:(kc + 1) * P], ident[:, :])
                    mm.then_inc(turned, 1)

                def count(t):
                    pe.wait_ge(tile_done, t + 1)
                    pe.matmul(bank[:, COUNTS, 0:NE], earlier[:, :], both[:, :], start=True, stop=True)
                    pe.matmul(bank[:, COUNTS, NE:2 * NE], ones[:, :], both[:, :], start=True, stop=True).then_inc(counts_done, 1)

                def score(t):
                    pe.wait_ge(hT_ready, t + 2)
                    pe.wait_ge(ranked, t + 1)
                    for kc in range(KC):
                        mm = pe.matmul(bank[:, LOGITS, 0:NG + NE], hT[:, kc, :], rw[:, kc, :], start=kc == 0, stop=kc == KC - 1)
                    mm.then_inc(logits_done, 1)

                def first():
                    pe.sem_inc(ranked, 1)
                    product(0, 0, 0, arriving=True)
                    product(0, 0, 1)
                    pe.wait_ge(consts_loaded, 16 * NCONST)
                    pe.wait_ge(consts_set, 1)

                def step(t, u, ranks=True, split=True):
                    product(t + 1, 1 - u, 0)
                    if ranks:
                        count(t - 1)
                    turn(t, u)
                    product(t + 1, 1 - u, 1)
                    score(t)

                def last(t, u):
                    count(t - 1)
                    turn(t, u)
                    score(t)
                    count(t)

                first()
                step(0, 0, ranks=False)
                with pe.Fori(0, (NT - 3) // 2) as i:
                    step(i * 2 + 1, 1)
                    step(i * 2 + 2, 0)
                step(NT - 2, 1, split=False)
                last(NT - 1, 0)

            @block.scalar
            def _(act):
                act.sem_inc(hT_ready, 1)

                def split(t, u):
                    act.wait_ge(m_loaded[u], t * 8 + (16 - 8 * u))
                    act.wait_ge(out_done, t + 1)
                    act.copy(m_hi[:, u], m[:, u]).then_inc(m_hi_ready, 1)

                def rms(t, u):
                    act.wait_ge(x2_ready, t + 3)
                    act.activation(junk[:, :], x2[:, u], ACT.Square, accum_out=ss[:, :]).then_inc(squared, 1)
                    act.wait_ge(ms_ready, t + 1)
                    act.activation(lms[:, :], ms[:, :], ACT.Ln).then_inc(ln_ready, 1)
                    act.wait_ge(ln_ready, t + 1)
                    act.activation(rstd[:, :], lms[:, :], ACT.Exp, scale=-0.5).then_inc(rstd_ready, 1)

                def turn(t):
                    act.wait_ge(turned, t + 1)
                    act.copy(hT[:, :, :].rearrange("p k t -> p (k t)"), bank[:, TURNED:TURNED + 2].rearrange("p b t -> p (b t)")).then_inc(hT_ready, 1)

                def gates(t):
                    act.wait_ge(nmax_ready, t + 1)
                    act.activation(gexp[:, :], logits[:, 0:NG], ACT.Exp, bias=nmax[:, :], accum_out=esum[:, :]).then_inc(gexp_ready, 1)
                    act.wait_ge(e_diff_ready, t + 1)
                    act.activation(e_exp[:, 0:1], etop[:, 2:3], ACT.Exp).then_inc(eexp_ready, 1)

                def first():
                    act.sem_inc(out_done, 2)
                    for q in range(WQ):
                        act.wait_ge(w_loaded[q], 16)
                        act.copy(w_hi[:, chunks(q)], w_o[:, chunks(q)]).then_inc(w_hi_ready, 1)
                        if q < 2:
                            split(q, q)
                    rms(0, 0)

                def step(t, u, ranks=True, split_on=True):
                    turn(t)
                    if split_on:
                        split(t + 2, u)
                    rms(t + 1, 1 - u)
                    gates(t)

                def last(t, u):
                    turn(t)
                    gates(t)

                first()
                step(0, 0, ranks=False)
                with act.Fori(0, (NT - 3) // 2) as i:
                    step(i * 2 + 1, 1)
                    step(i * 2 + 2, 0)
                step(NT - 2, 1, split_on=False)
                last(NT - 1, 0)

            @block.gpsimd
            def _(pool):
                pool.iota(ids[:, :], [[1, NE]], base=0, channel_multiplier=0, allow_small_or_imprecise_dtypes=True)
                pool.iota(blocks[:, :], [[EB, NBLK]], base=0, channel_multiplier=0, allow_small_or_imprecise_dtypes=True)
                pool.iota(spare[:, :], [[-(T % P), 2]], base=NBLK * EB, channel_multiplier=1, allow_small_or_imprecise_dtypes=True)
                pool.iota(token[:, :], [[P, NT]], base=0, channel_multiplier=1)
                pool.memset(nothing[:, :], 0).then_inc(nothing_set, 1)
                for u in range(2):
                    pool.sem_inc(m_lo_ready, 1)

                def split(t, u):
                    pool.wait_ge(m_hi_ready, t + 1)
                    pool.wait_ge(out_done, t + 1)
                    pool.tensor_tensor(m_lo[:, u], m[:, u], m_hi[:, u].bitcast(F32), ALU.subtract).then_inc(m_lo_ready, 1)

                split(0, 0)
                split(1, 1)
                with pool.Fori(0, NT // 2 - 1) as i:
                    for u in range(2):
                        split(i * 2 + (u + 2), u)
                split(NT - 1, 0)
                pool.wait_ge(nothing_set, 1)
                pool.dma_start(g.row_token.rearrange("(p n) a -> p (n a)", p=P), nothing[:, :]).then_inc(table_cleared, 16)
                pool.wait_ge(table_cleared, 16)
                pool.wait_ge(dest_ready, 1)
                for t in range(NT):
                    for s in range(2):
                        pool.indirect_dma_start(g.row_token, bass.IndirectOffsetOnAxis(ap=g.dest_i[:, t, s:s + 1], axis=0),
                                                token[:, t:t + 1], None).then_inc(scattered, 16)
                pool.wait_ge(scattered, 16 * 2 * NT)
                with nc.allow_non_contiguous_dma(reason="a block's rows go over the partitions"):
                    pool.dma_start(g.row_of[:, :], g.row_token[0:NBLK * EB].rearrange("(n p) a -> p (n a)", p=P)).then_inc(ids_stored, 16)
                pool.wait_ge(ids_stored, 16)

            @block.vector
            def _(dve):
                dve.sem_inc(x2_ready, 2)
                dve.sem_inc(routed, 1)
                dve.memset(each_one[:, :], 1.0)
                dve.memset(block_ones[:, :], 1.0)
                dve.memset(base[:, :], 0.0)
                dve.memset(glog[:, :], -3.0e38)
                dve.memset(valid[:, :], 0.0)
                dve.memset(ones[:, :], 1.0).then_inc(consts_set, 1)
                dve.wait_ge(consts_set, 1)
                dve.memset(valid[0:T % P, :], 1.0).then_inc(valid_set, 1)
                dve.wait_ge(nothing_set, 1)
                dve.wait_ge(valid_set, 1)
                for q in range(WQ):
                    dve.wait_ge(w_loaded[q], 16)
                    dve.wait_ge(w_hi_ready, q + 1)
                    dve.tensor_tensor(w_lo[:, chunks(q)], w_o[:, chunks(q)], w_hi[:, chunks(q)].bitcast(F32), ALU.subtract).then_inc(w_lo_ready, 1)
                dve.wait_ge(consts_loaded, 16 * NCONST)
                n = [0]

                def links(t):
                    def link(op, before_max=False):
                        op.then_inc(routed, 1)
                        n[0] += 1
                        dve.wait_ge(routed, t * LINKS + (n[0] + 1))
                        if before_max:
                            dve.sem_inc(passed, 1)

                    return link

                def residual(t, u):
                    dve.wait_ge(out_done, t + 3)
                    dve.wait_ge(x_loaded[u], t * 8 + (16 - 8 * u))
                    dve.wait_ge(x2_stored[u], t * 8 + (16 - 8 * u))
                    dve.tensor_tensor(x2[:, u], bank[:, OUT[u]:OUT[u] + 2].rearrange("p b t -> p (b t)"), x[:, u], ALU.add).then_inc(x2_ready, 1)

                def mean_square(t):
                    dve.wait_ge(squared, t + 1)
                    dve.tensor_scalar(ms[:, :], ss[:, :], 1.0 / D, NORM_EPS, ALU.mult, ALU.add).then_inc(ms_ready, 1)

                def normalise(t, u):
                    dve.wait_ge(rstd_ready, t + 1)
                    dve.wait_ge(h_stored[u], t * 8 + (16 - 8 * u))
                    dve.scalar_tensor_tensor(h[:, u], x2[:, u], rstd[:, :], gain[:, :], ALU.mult, ALU.mult).then_inc(h_ready, 1)

                def choose(t, partial=False):
                    n[0] = 0
                    link = links(t)
                    dve.wait_ge(logits_done, t + 1)
                    link(dve.tensor_tensor(logits[:, :], bank[:, LOGITS, 0:NG + NE], rb[:, :], ALU.add))
                    link(dve.tensor_copy(glog[:, 0:NG], logits[:, 0:NG]), before_max=True)
                    link(dve.max(top[:, :], glog[:, :]), before_max=True)
                    link(dve.max_index(gidx[:, :], top[:, :], glog[:, :]))
                    dve.tensor_scalar(nmax[:, :], top[:, 0:1], -1.0, None, ALU.mult).then_inc(nmax_ready, 1)
                    link(dve.tensor_copy(gid[:, :], gidx[:, 0:1]))
                    link(dve.tensor_scalar(ghot[:, :], ids[:, 0:NG], gid[:, :], None, ALU.is_equal))
                    le = logits[:, NG:].rearrange("p (n e) -> p n e", n=NG)
                    link(dve.tensor_scalar(chosen[:, :], le[:, 0], ghot[:, 0:1], None, ALU.mult))
                    for k in range(1, NG):
                        link(dve.scalar_tensor_tensor(chosen[:, :], le[:, k], ghot[:, k:k + 1], chosen[:, :], ALU.mult, ALU.add), before_max=k == NG - 1)
                    link(dve.max(etop[:, :], chosen[:, :]), before_max=True)
                    link(dve.max_index(eidx[:, :], etop[:, :], chosen[:, :]))
                    link(dve.tensor_tensor(etop[:, 2:3], etop[:, 1:2], etop[:, 0:1], ALU.subtract))
                    dve.tensor_scalar(gid[:, :], gid[:, :], float(EPG), None, ALU.mult).then_inc(e_diff_ready, 1)
                    dve.wait_ge(e_diff_ready, t + 1)
                    ex = expert[:, ds(t, 1), :].rearrange("p a s -> p (a s)")
                    link(dve.tensor_copy(ex, eidx[:, 0:2]))
                    link(dve.tensor_scalar(ex, ex, gid[:, :], None, ALU.add))
                    for s in range(2):
                        dve.tensor_scalar(hot[:, s], ids[:, :], expert[:, ds(t, 1), s], None, ALU.is_equal).then_inc(hot_ready, 1)
                    dve.wait_ge(hot_ready, t * 2 + 2)
                    link(dve.tensor_tensor(both[:, :], hot[:, 0], hot[:, 1], ALU.add))
                    if partial:
                        dve.tensor_scalar(both[:, :], both[:, :], valid[:, :], None, ALU.mult).then_inc(tile_done, 1)
                    else:
                        dve.sem_inc(tile_done, 1)
                    dve.wait_ge(gexp_ready, t + 1)
                    dve.wait_ge(eexp_ready, t + 1)
                    link(dve.tensor_scalar(g_one[:, :], e_exp[:, 0:1], 1.0, None, ALU.add))
                    link(dve.tensor_tensor(esum[:, :], esum[:, :], g_one[:, :], ALU.mult))
                    gt = g.gate_of[:, ds(t, 1), :].rearrange("p a s -> p (a s)")
                    link(dve.reciprocal(gt[:, 0:1], esum[:, :]))
                    dve.tensor_tensor(gt[:, 1:2], gt[:, 0:1], e_exp[:, 0:1], ALU.mult)
                    assert n[0] == CHOICE, n[0]

                def rank_rows(t):
                    n[0] = CHOICE
                    link = links(t)
                    dve.wait_ge(counts_done, t + 1)
                    link(dve.tensor_tensor(rank[:, :], bank[:, COUNTS, 0:NE], base[:, :], ALU.add))
                    link(dve.tensor_tensor(at[:, :, :], hot[:, :, :], rank[:, :].unsqueeze(1).to_broadcast([P, 2, NE]), ALU.mult))
                    dve.tensor_reduce(ranks[:, ds(t, 1), :].rearrange("p a s -> p (a s)"), at[:, :, :], AX.X, ALU.add)
                    link(dve.tensor_tensor(base[:, :], bank[:, COUNTS, NE:2 * NE], base[:, :], ALU.add))
                    assert n[0] == LINKS, n[0]
                    dve.sem_inc(ranked, 1)

                def first():
                    residual(0, 0)
                    mean_square(0)
                    normalise(0, 0)

                def step(t, u, ranks=True, split=True):
                    residual(t + 1, 1 - u)
                    if ranks:
                        rank_rows(t - 1)
                    mean_square(t + 1)
                    choose(t)
                    normalise(t + 1, 1 - u)

                def last(t, u):
                    rank_rows(t - 1)
                    choose(t, partial=True)
                    rank_rows(t)

                first()
                step(0, 0, ranks=False)
                with dve.Fori(0, (NT - 3) // 2) as i:
                    step(i * 2 + 1, 1)
                    step(i * 2 + 2, 0)
                step(NT - 2, 1, split=False)
                last(NT - 1, 0)

                n[0] = NT * LINKS + 1

                def link(op):
                    op.then_inc(routed, 1)
                    n[0] += 1
                    dve.wait_ge(routed, n[0])

                link(dve.tensor_scalar(count_i[:, :], base[:, :], float(EB - 1), None, ALU.add))
                link(dve.tensor_scalar(count_i[:, :], count_i[:, :], 7, 7, ALU.logical_shift_right, ALU.logical_shift_left))
                link(dve.tensor_copy(padded[:, :], count_i[:, :]))
                link(dve.tensor_tensor_scan(ends[:, :], each_one[:, :], padded[:, :], 0.0, ALU.mult, ALU.add))
                link(dve.tensor_tensor(starts[:, :], ends[:, :], padded[:, :], ALU.subtract))
                ex = expert[:, :, :].rearrange("p t s -> p (t s)")
                link(dve.tensor_tensor(allhot[:, :, :], ids[:, :].unsqueeze(1).to_broadcast([P, 2 * NT, NE]),
                                       ex.unsqueeze(2).to_broadcast([P, 2 * NT, NE]), ALU.is_equal))
                link(dve.tensor_tensor(allhot[:, :, :], allhot[:, :, :], starts[:, :].unsqueeze(1).to_broadcast([P, 2 * NT, NE]), ALU.mult))
                link(dve.tensor_reduce(dest[:, :, :].rearrange("p t s -> p (t s)"), allhot[:, :, :], AX.X, ALU.add))
                link(dve.tensor_tensor(dest[:, :, :], dest[:, :, :], ranks[:, :, :], ALU.add))
                last = dest[:, NT - 1, :]
                link(dve.tensor_tensor(last, last, spare[:, :], ALU.subtract))
                link(dve.tensor_scalar(last, last, valid[:, :], None, ALU.mult))
                link(dve.tensor_tensor(last, last, spare[:, :], ALU.add))
                link(dve.tensor_copy(g.dest_i[:, :, :], dest[:, :, :]))
                dve.sem_inc(dest_ready, 1)
                link(dve.tensor_tensor(filled[:, :, :], blocks[:, :].unsqueeze(2).to_broadcast([P, NBLK, NE]),
                                       ends[:, :].unsqueeze(1).to_broadcast([P, NBLK, NE]), ALU.is_ge))
                link(dve.tensor_reduce(block_of[:, :], filled[:, :, :], AX.X, ALU.add))
                link(dve.tensor_scalar(block_of[:, :], block_of[:, :], float(NE - 1), None, ALU.min))
                link(dve.tensor_copy(g.block_expert[:, :], block_of[:, :]))
                link(dve.memset(fresh[:, 0:1], 1.0))
                link(dve.tensor_tensor(fresh[:, 1:], block_of[:, 1:], block_of[:, 0:NBLK - 1], ALU.not_equal))
                link(dve.tensor_copy(g.block_fresh[:, :], fresh[:, :]))
                link(dve.tensor_tensor_scan(block_of[:, :], block_ones[:, :], fresh[:, :], 0.0, ALU.mult, ALU.add))
                link(dve.tensor_copy(g.block_buffer[:, :], block_of[:, :]))
                link(dve.tensor_scalar(g.block_buffer[:, :], g.block_buffer[:, :], 1, None, ALU.bitwise_and))


def run_experts(nc, g):
    DEPTH = 2
    HW = 2 * DE
    with Phase(nc, "expert") as ph:
        w = ph.sb("w", [P, DEPTH, KC * HW])
        wd = ph.sb("wd", [P, DEPTH, 2 * D])
        ident = ph.sb("ident", [P, P])
        rows = ph.sb("rows", [P, DEPTH], I32)
        x = ph.sb("x", [P, DEPTH, D])
        xT = ph.sb("xT", [P, KC, P])
        sig = ph.sb("sig", [P, DE])
        act_h = ph.sb("act_h", [P, DE])
        hT = ph.sb("hT", [P, 2, P])
        out = ph.sb("out", [P, DEPTH, D])
        zero = ph.sb("zero", [P, D])
        bank = ph.psum("bank", [P, 8, 512])
        w_loaded, wd_loaded, out_stored = ([ph.sem(f"{n}{u}") for u in range(DEPTH)] for n in ("w_loaded", "wd_loaded", "out_stored"))
        ident_loaded, rows_ready, turned, xT_ready, up_done, sig_ready, gated, h_ready, h_turned, hT_ready, \
            down_done, out_ready, zero_set, half_out = (
                ph.sem(n) for n in ("ident_loaded", "rows_ready", "turned", "xT_ready", "up_done",
                                    "sig_ready", "gated", "h_ready", "h_turned", "hT_ready", "down_done", "out_ready",
                                    "zero_set", "half_out"))
        zero_stored, gathered = (ph.pool_dma_sem(n) for n in ("zero_stored", "gathered"))
        passed, sp_passed = ph.sem("passed"), ph.sem("sp_passed")

        with ph.block() as block:
            @block.sync
            def _(sp):
                sp.dma_start(ident[:, :], g.ident).then_inc(ident_loaded, 16)

                def load(b, u, dst, src, used, loaded):
                    e = sp.value_load(g.block_expert[0:1, ds(b, 1)], min_val=0, max_val=NE - 1)
                    buf = sp.value_load(g.block_buffer[0:1, ds(b, 1)], min_val=0, max_val=1)
                    fresh = sp.value_load(g.block_fresh[0:1, ds(b, 1)], min_val=0, max_val=1)
                    sp.wait_ge(used, b + 1)
                    sp.sem_inc(sp_passed, 1)
                    with sp.If(fresh == 1):
                        sp.dma_start(dst[:, ds(buf, 1)].rearrange("p a n -> p (a n)"), src[ds(e, 1)].rearrange("a p n -> p (a n)")).then_inc(loaded[u], 16)
                    with sp.Else():
                        sp.sem_inc(loaded[u], 16)

                load(0, 0, w, g.w_up, up_done, w_loaded)
                with sp.Fori(0, NBLK // 2 - 1) as i:
                    for u in range(2):
                        load(i * 2 + (u + 1), 1 - u, w, g.w_up, up_done, w_loaded)
                        load(i * 2 + u, u, wd, g.w_down, down_done, wd_loaded)
                load(NBLK - 1, 1, w, g.w_up, up_done, w_loaded)
                load(NBLK - 2, 0, wd, g.w_down, down_done, wd_loaded)
                load(NBLK - 1, 1, wd, g.w_down, down_done, wd_loaded)

            @block.gpsimd
            def _(pool):
                pool.memset(zero[:, :], 0.0).then_inc(zero_set, 1)
                pool.wait_ge(zero_set, 1)
                pool.dma_start(g.yb[NBLK * EB:], zero[:, :]).then_inc(zero_stored, 16)
                pool.wait_ge(zero_stored, 16)
                with pool.Fori(0, NBLK // 2) as i:
                    for u in range(2):
                        b = i * 2 + u
                        pool.wait_ge(turned, b + 1)
                        pool.sem_inc(passed, 1)
                        pool.tensor_copy(rows[:, u:u + 1], g.row_of[:, ds(b, 1)]).then_inc(rows_ready, 1)
                        pool.wait_ge(rows_ready, b + 1)
                        pool.sem_inc(passed, 1)
                        pool.indirect_dma_start(x[:, u], None, g.h, bass.IndirectOffsetOnAxis(ap=rows[:, u:u + 1], axis=0)).then_inc(gathered, 16)
                        pool.wait_ge(gathered, b * 16 + 16)

            @block.tensor
            def _(pe):
                for s in (turned, up_done, down_done):
                    pe.sem_inc(s, 2)
                pe.wait_ge(ident_loaded, 16)

                def turn(b, u):
                    pe.wait_ge(gathered, b * 16 + 16)
                    pe.wait_ge(xT_ready, b + 1)
                    for kc in range(KC):
                        mm = pe.transpose(bank[:, kc // 4, (kc % 4) * P:(kc % 4 + 1) * P], x[:, u, kc * P:(kc + 1) * P], ident[:, :])
                    mm.then_inc(turned, 1)

                def up(b, u):
                    buf = pe.value_load(g.block_buffer[0:1, ds(b, 1)], min_val=0, max_val=1)
                    pe.wait_ge(xT_ready, b + 2)
                    pe.wait_ge(w_loaded[u], b * 8 + (16 - 8 * u))
                    pe.wait_ge(h_ready, b + 1)
                    for kc in range(KC):
                        mm = pe.matmul(bank[:, 2], xT[:, kc, :], w[:, ds(buf, 1), kc * HW:(kc + 1) * HW].rearrange("p a n -> p (a n)"),
                                       start=kc == 0, stop=kc == KC - 1)
                    mm.then_inc(up_done, 1)

                def turn_h(b):
                    pe.wait_ge(h_ready, b + 2)
                    pe.wait_ge(hT_ready, b + 1)
                    for f in range(2):
                        mm = pe.transpose(bank[:, 3, f * P:(f + 1) * P], act_h[:, f * P:(f + 1) * P], ident[:, :])
                    mm.then_inc(h_turned, 1)

                def down(b, u):
                    buf = pe.value_load(g.block_buffer[0:1, ds(b, 1)], min_val=0, max_val=1)
                    pe.wait_ge(hT_ready, b + 2)
                    pe.wait_ge(wd_loaded[u], b * 8 + (16 - 8 * u))
                    pe.wait_ge(out_ready, b + 1)
                    for n in range(2):
                        for f in range(2):
                            mm = pe.matmul(bank[:, 4 + n], hT[:, f, :], wd[:, ds(buf, 1), f * D + n * 512:f * D + (n + 1) * 512].rearrange("p a n -> p (a n)"),
                                           start=f == 0, stop=f == 1)
                    mm.then_inc(down_done, 1)

                def step(b, u):
                    up(b, u)
                    turn(b + 1, 1 - u)
                    down(b - 1, 1 - u)
                    turn_h(b)

                turn(0, 0)
                up(0, 0)
                turn(1, 1)
                turn_h(0)
                with pe.Fori(0, NBLK // 2 - 1) as i:
                    step(i * 2 + 1, 1)
                    step(i * 2 + 2, 0)
                up(NBLK - 1, 1)
                down(NBLK - 2, 0)
                turn_h(NBLK - 1)
                down(NBLK - 1, 1)

            @block.scalar
            def _(act):
                act.sem_inc(out_ready, 1)
                for u in range(2):
                    act.sem_inc(out_stored[u], 16)

                def gate(b):
                    act.wait_ge(up_done, b + 3)
                    act.activation(sig[:, :], bank[:, 2, 0:DE], ACT.Sigmoid).then_inc(sig_ready, 1)

                def store(b, u):
                    act.wait_ge(down_done, b + 3)
                    act.wait_ge(out_stored[u], b * 8 + (16 - 8 * u))
                    act.copy(out[:, u], bank[:, 4:6].rearrange("p b n -> p (b n)")).then_inc(out_ready, 1)
                    act.wait_ge(out_ready, b + 2)
                    act.dma_start(g.yb[ds(b * EB, EB)], out[:, u]).then_inc(out_stored[u], 16)

                act.wait_ge(up_done, 3)
                act.activation(sig[:, :], bank[:, 2, 0:DE], ACT.Sigmoid).then_inc(sig_ready, 1)
                with act.Fori(0, NBLK // 2 - 1) as i:
                    gate(i * 2 + 1)
                    store(i * 2, 0)
                    gate(i * 2 + 2)
                    store(i * 2 + 1, 1)
                gate(NBLK - 1)
                store(NBLK - 2, 0)
                store(NBLK - 1, 1)
                for u in range(2):
                    act.wait_ge(out_stored[u], 16 + 16 * (NBLK // 2))

            @block.vector
            def _(dve):
                dve.sem_inc(xT_ready, 1)
                dve.sem_inc(h_ready, 1)
                dve.sem_inc(hT_ready, 1)

                def move_x(b):
                    dve.wait_ge(turned, b + 3)
                    dve.wait_ge(up_done, b + 2)
                    dve.tensor_copy(xT[:, :, :].rearrange("p k t -> p (k t)"), bank[:, 0:2].rearrange("p b t -> p (b t)")).then_inc(xT_ready, 1)

                def gate(b):
                    dve.wait_ge(sig_ready, b + 1)
                    dve.tensor_tensor(sig[:, :], bank[:, 2, 0:DE], sig[:, :], ALU.mult).then_inc(gated, 1)
                    dve.wait_ge(gated, b + 1)
                    dve.tensor_tensor(act_h[:, :], bank[:, 2, DE:HW], sig[:, :], ALU.mult).then_inc(h_ready, 1)

                def move_h(b):
                    dve.wait_ge(h_turned, b + 1)
                    dve.wait_ge(down_done, b + 2)
                    dve.tensor_copy(hT[:, :, :].rearrange("p k t -> p (k t)"), bank[:, 3, 0:2 * P]).then_inc(hT_ready, 1)

                move_x(0)
                with dve.Fori(0, NBLK // 2 - 1) as i:
                    for u in range(2):
                        gate(i * 2 + u)
                        move_x(i * 2 + (u + 1))
                        move_h(i * 2 + u)
                gate(NBLK - 2)
                move_x(NBLK - 1)
                move_h(NBLK - 2)
                gate(NBLK - 1)
                move_h(NBLK - 1)


def combine(nc, g):
    with Phase(nc, "combine") as ph:
        gain = ph.sb("gain", [P, D])
        x2 = ph.sb("x2", [P, 2, D])
        rows = ph.sb("rows", [P, 2, 2], I32)
        e0, e1 = (ph.sb(n, [P, 2, D]) for n in ("e0", "e1"))
        out = ph.sb("out", [P, 2, D])
        junk = ph.sb("junk", [P, D])
        ss, ms, inv, rstd = (ph.sb(n, [P, 1]) for n in ("ss", "ms", "inv", "rstd"))
        x2_loaded, out_stored = ([ph.sem(f"{n}{u}") for u in range(2)] for n in ("x2_loaded", "out_stored"))
        gain_loaded, rows_ready, first_added, added, squared, ms_ready, inv_ready, rstd_ready, out_ready, consts = (
            ph.sem(n) for n in ("gain_loaded", "rows_ready", "first_added", "added", "squared",
                                "ms_ready", "inv_ready", "rstd_ready", "out_ready", "consts"))
        gathered = [[ph.pool_dma_sem(f"gathered{n}{u}") for u in range(2)] for n in range(2)]
        passed = ph.sem("passed")

        with ph.block() as block:
            def tiles(eng, tile):
                with eng.Fori(0, NT // 2) as i:
                    for u in range(2):
                        tile(i * 2 + u, u, P)
                tile(NT - 1, 0, T - (NT - 1) * P)

            @block.sync
            def _(sp):
                sp.dma_start(gain[:, :], g.norm_f.to_broadcast([P, D])).then_inc(gain_loaded, 16)
                sp.sem_inc(out_stored[0], 16)
                sp.sem_inc(out_stored[1], 16)

                def load(t, u):
                    sp.wait_ge(out_ready, t + 1)
                    sp.dma_start(x2[:, u], g.x2[ds(t * P, P)]).then_inc(x2_loaded[u], 16)

                def store(t, u, n):
                    sp.wait_ge(out_ready, t + 3)
                    sp.dma_start(g.y_out[ds(t * P, n)], out[0:n, u]).then_inc(out_stored[u], 16)

                load(0, 0)
                with sp.Fori(0, NT // 2) as i:
                    for u in range(2):
                        load(i * 2 + (u + 1), 1 - u)
                        store(i * 2 + u, u, P)
                store(NT - 1, 0, T - (NT - 1) * P)
                sp.wait_ge(out_stored[0], 16 + 16 * (NT // 2 + 1))
                sp.wait_ge(out_stored[1], 16 + 16 * (NT // 2))

            @block.gpsimd
            def _(pool):
                pool.memset(junk[:, 0:1], 0.0).then_inc(consts, 1)

                def tile(t, u, n):
                    pool.wait_ge(added, t + 1)
                    pool.sem_inc(passed, 1)
                    pool.tensor_copy(rows[:, u], g.dest_i[:, ds(t, 1), :].rearrange("p a s -> p (a s)")).then_inc(rows_ready, 1)
                    pool.wait_ge(rows_ready, t + 1)
                    pool.sem_inc(passed, 1)
                    for s, e in enumerate((e0, e1)):
                        pool.indirect_dma_start(e[:, u], None, g.yb, bass.IndirectOffsetOnAxis(ap=rows[:, u, s:s + 1], axis=0)).then_inc(gathered[s][u], 16)
                tiles(pool, tile)

            @block.scalar
            def _(act):
                def tile(t, u, n):
                    act.wait_ge(added, t + 3)
                    act.activation(junk[:, :], out[:, u], ACT.Square, accum_out=ss[:, :]).then_inc(squared, 1)
                    act.wait_ge(inv_ready, t + 1)
                    act.activation(rstd[:, :], inv[:, :], ACT.Sqrt).then_inc(rstd_ready, 1)
                act.wait_ge(consts, 1)
                tiles(act, tile)

            @block.vector
            def _(dve):
                dve.sem_inc(added, 2)
                dve.sem_inc(out_ready, 2)
                dve.wait_ge(gain_loaded, 16)

                def tile(t, u, n):
                    dve.wait_ge(x2_loaded[u], t * 8 + (16 - 8 * u))
                    dve.wait_ge(gathered[0][u], t * 8 + (16 - 8 * u))
                    dve.wait_ge(out_stored[u], t * 8 + (16 - 8 * u))
                    dve.scalar_tensor_tensor(out[:, u], e0[:, u], g.gate_of[:, ds(t, 1), 0], x2[:, u], ALU.mult, ALU.add).then_inc(first_added, 1)
                    dve.wait_ge(gathered[1][u], t * 8 + (16 - 8 * u))
                    dve.wait_ge(first_added, t + 1)
                    dve.scalar_tensor_tensor(out[:, u], e1[:, u], g.gate_of[:, ds(t, 1), 1], out[:, u], ALU.mult, ALU.add).then_inc(added, 1)
                    dve.wait_ge(squared, t + 1)
                    dve.tensor_scalar(ms[:, :], ss[:, :], 1.0 / D, NORM_EPS, ALU.mult, ALU.add).then_inc(ms_ready, 1)
                    dve.wait_ge(ms_ready, t + 1)
                    dve.reciprocal(inv[:, :], ms[:, :]).then_inc(inv_ready, 1)
                    dve.wait_ge(rstd_ready, t + 1)
                    dve.scalar_tensor_tensor(out[:, u], out[:, u], rstd[:, :], gain[:, :], ALU.mult, ALU.mult).then_inc(out_ready, 1)
                tiles(dve, tile)


PHASES = [norm_inputs, project_glu, project_rwkv, project_gates, prepare_recurrence, recurrence, finish_mixing,
          mix_branches, route, run_experts, combine]


def hybrid_step(nc, ins, outs):
    g = Tensors(ins, outs)

    def scratch(name, shape, dt=F32):
        return nc.dram_tensor(name, shape, dt, kind="Internal").ap()

    g.xm = scratch("xm", [RWB, P, T])
    g.gates = scratch("gates", [2 * KC, P, T])
    g.zc = scratch("zc", [NCH, P, 4, NPAIR, C])
    g.y = scratch("y", [NPAIR, P, T])
    g.go = scratch("go", [NPAIR, P, T])
    g.bonus = scratch("bonus", [NPAIR, P, T])
    g.m = scratch("m", [KC, P, NT * P])
    g.x2 = scratch("x2", [NT * P, D])
    g.h = scratch("h", [NT * P, D])
    g.row_token = scratch("row_token", [(NBLK + 1) * EB, 1], I32)
    g.yb = scratch("yb", [(NBLK + 1) * EB, D])
    with ExitStack() as late:
        def kept(ctx, name, shape, dt=F32):
            return ctx.enter_context(nc.sbuf_tensor(name, shape, dt))

        g.row_of = kept(late, "row_of", [P, NBLK], I32)
        g.block_expert, g.block_fresh, g.block_buffer = (kept(late, n, [P, NBLK], I32) for n in (
            "block_expert", "block_fresh", "block_buffer"))
        g.dest_i = kept(late, "dest_i", [P, NT, 2], I32)
        g.gate_of = kept(late, "gate_of", [P, NT, 2])
        with ExitStack() as ctx:
            g.conv = kept(ctx, "conv", [P, CB, T])
            with ExitStack() as early:
                g.glu_p = kept(early, "glu_p", [P, CB, HIST + NP])
                g.glu_s = kept(early, "glu_s", [P, CB, DB, HIST + DS])
                g.hist_s = kept(early, "hist_s", [P, CB, DB, HIST])
                g.u = kept(early, "u", [P, KC, TC])
                for phase in PHASES[:4]:
                    phase(nc, g)
            g.lam_p = kept(ctx, "lam_p", [P, NPAIR, NCH - 1])
            g.lam_s = kept(ctx, "lam_s", [P, NPAIR, DB])
            for phase in PHASES[4:6]:
                phase(nc, g)
            g.mixed = kept(ctx, "mixed", [P, NPAIR, T])
            for phase in PHASES[6:8]:
                phase(nc, g)
        for phase in PHASES[8:]:
            phase(nc, g)


def kernel(**inputs):
    import numpy as np
    import concourse.bacc as bacc
    from concourse.bass_utils import run_bass_kernel_spmd

    f = {k: np.asarray(v) for k, v in inputs.items()}
    f = {k: v[0] if k not in ("x_prompt", "x_sample", "final_norm_g") else v for k, v in f.items()}

    def by_channel(v):
        return np.ascontiguousarray(v.reshape(-1, P).T)

    x = np.concatenate([f["x_prompt"][0], f["x_sample"].reshape(NS, D)])
    arrays = {
        "xT": np.ascontiguousarray(np.concatenate([x, f["state_shift"]]).T).reshape(KC, P, TC),
        "norm1": by_channel(f["norm1_g"]),
        "w_in": np.ascontiguousarray(f["w_in"].reshape(KC, P, -1, P).transpose(2, 1, 0, 3)),
        "state_conv": np.ascontiguousarray(f["state_conv"].reshape(DB, HIST, CB, P).transpose(3, 2, 0, 1)),
        "conv_w": np.ascontiguousarray(f["conv_dw_w"].reshape(CK, CB, P).transpose(2, 1, 0)),
        "conv_b": by_channel(f["conv_dw_b"]),
        "mu": by_channel(f["rwkv_mu"]),
        "rwkv_par": np.ascontiguousarray(np.stack(
            [by_channel(f[n]) for n in ("rwkv_w0", "rwkv_a0", "rwkv_k_k", "rwkv_k_a", "rwkv_k_a", "rwkv_r_k")], axis=2)),
        "lora": np.ascontiguousarray(np.stack([
            np.concatenate([f["rwkv_w2"], np.zeros_like(f["rwkv_w2"])]),
            np.concatenate([np.zeros_like(f["rwkv_a2"]), f["rwkv_a2"]]), f["rwkv_g2"]])
            .reshape(3, P, NPAIR, P).transpose(2, 1, 0, 3)),
    }
    arrays |= {
        "norm_par": np.ascontiguousarray(np.stack(
            [by_channel(f["rwkv_gn_g"]), by_channel(f["rwkv_gn_b"]),
             *(np.pad(by_channel(f[n]), ((0, 0), (0, NPAIR - CB))) for n in ("conv_ln_g", "conv_ln_b"))], axis=1)),
        "w_branch": np.ascontiguousarray(np.concatenate([f["rwkv_out_w"], f["conv_out_w"]])
                                         .reshape(KC + CB, P, KC, P).transpose(2, 1, 0, 3)),
        "conv_out_b": by_channel(f["conv_out_b"]),
        "w_o": np.ascontiguousarray(f["w_o"].reshape(KC, P, D).transpose(1, 0, 2)),
        "router_w": np.ascontiguousarray(np.concatenate([f["router_group_w"], f["router_expert_w"]], axis=1)
                                         .reshape(KC, P, NG + NE).transpose(1, 0, 2)),
        "router_b": np.concatenate([f["router_group_b"], f["router_expert_b"]])[None],
        "norm2": f["norm2_g"][None], "norm_f": f["final_norm_g"][None],
        "x": np.concatenate([x, np.zeros((NT * P - T, D), x.dtype)]),
        "w_up": np.ascontiguousarray(np.concatenate([f["expert_w_gate"], f["expert_w_up"]], axis=2)
                                     .reshape(NE, KC, P, 2 * DE).transpose(0, 2, 1, 3)).reshape(NE, P, KC * 2 * DE),
        "w_down": np.ascontiguousarray(f["expert_w_down"].reshape(NE, 2, P, D).transpose(0, 2, 1, 3)).reshape(NE, P, 2 * D),
        "ident": np.eye(P, dtype=np.float32), "earlier": np.triu(np.ones((P, P), np.float32), 1),
    }
    j, t = np.arange(C)[:, None], np.arange(C)[None, :]
    same = j // DS == t // DS
    pair_step = (j % 2 == 0) & (t == j + 1)
    both = lambda m: np.concatenate([m, m]).astype(np.float32)
    arrays |= {
        "masks": np.stack([np.stack([both(-1.0 * (pair_step & s)), both(-1.0 * ((j <= t) & s)), both((j < t) & s),
                                     both((j <= t) & s), both(-1.0 * ((t < j) & s))], axis=1)
                           for s in (same | True, same)], axis=1),
        "doubling": np.stack([both((j // (2 * m) == t // (2 * m)) & (j % (2 * m) < m) & (t % (2 * m) >= m))
                              for m in (2, 4, 8, 16, 32)], axis=1).astype(np.int32),
        "eye": both(j == t),
        "seq": both(j // DS == np.arange(DB)[None, :]),
        "state_s": np.ascontiguousarray(f["state_wkv"].reshape(DB, NPAIR, 2, HD, HD).transpose(2, 4, 1, 0, 3)
                                        .reshape(P, NPAIR, DB, HD)),
    }
    shapes = {
        "y_out": (T, D),
        "wkv_p": (P, NPAIR, HD), "wkv_s": (P, NPAIR, DB, HD),
        "shift_p": (P, KC, 1), "shift_s": (P, KC, DB), "conv_p": (P, CB, HIST), "conv_s": (P, CB, DB, HIST),
    }
    nc = bacc.Bacc("TRN2", target_bir_lowering=False, num_devices=1)
    ins = {k: nc.dram_tensor(f"in_{k}", a.shape, mybir.dt.from_np(a.dtype), kind="ExternalInput").ap()
           for k, a in arrays.items()}
    outs = {k: nc.dram_tensor(f"out_{k}", s, F32, kind="ExternalOutput").ap() for k, s in shapes.items()}
    hybrid_step(nc, ins, outs)
    r = run_bass_kernel_spmd(nc, [{f"in_{k}": a for k, a in arrays.items()}], core_ids=[0])
    o = {k: np.asarray(r.results[0][f"out_{k}"]) for k in shapes}

    def channels_last(v):
        return np.ascontiguousarray(np.moveaxis(v, (1, 0), (-2, -1))).reshape(*v.shape[2:], -1)

    wkv_p = o["wkv_p"].reshape(2, HD, NPAIR, HD).transpose(2, 0, 3, 1).reshape(1, 1, 2 * NPAIR, HD, HD)
    wkv_s = o["wkv_s"].reshape(2, HD, NPAIR, DB, HD).transpose(3, 2, 0, 4, 1).reshape(1, DB, 2 * NPAIR, HD, HD)
    return (o["y_out"][None, :NP], o["y_out"][NP:].reshape(DB, DS, D),
            channels_last(o["conv_p"])[None, None], channels_last(o["shift_p"])[None], np.ascontiguousarray(wkv_p),
            channels_last(o["conv_s"])[None], channels_last(o["shift_s"])[None], np.ascontiguousarray(wkv_s))
```
